# Optimizing a Trainium2 kernel written in Bass

```python
import jax, jax.numpy as jnp
from jax import lax
import numpy as np

D_MODEL = 1024
BATCH = 1
SEQ = 1024
DEPTH = 1

CHUNK = 64
N_META = 16
D_CONV = D_MODEL
CONV_W = 3
N_FOX_HEADS = 16
FOX_HEAD_DIM = 64
D_ATT = N_FOX_HEADS * FOX_HEAD_DIM
N_GROUPS = 4
EXPERTS_PER_GROUP = 8
N_EXPERTS = N_GROUPS * EXPERTS_PER_GROUP
TOP_K_IN_GROUP = 2
D_EXPERT = 512
Q_BLOCK = 128
MOE_BLOCK = 128
EPS = 1e-6
SPLIT_SIZES = (D_CONV, D_CONV, D_CONV, D_ATT, D_ATT, D_ATT, N_FOX_HEADS, D_MODEL, D_MODEL)
IN_COLS = sum(SPLIT_SIZES)

kernel_name = "hybrid_conv_fox_hiermoe_block"

def rms_norm(x, g):
    xf = x.astype(jnp.float32)
    y = xf * lax.rsqrt(jnp.mean(xf * xf, axis=-1, keepdims=True) + EPS)
    return (y * g.astype(jnp.float32)).astype(x.dtype)

def short_gated_conv(b_gate, c_gate, u, conv_w):
    z = c_gate * u
    L = z.shape[1]
    zp = jnp.pad(z, ((0, 0), (CONV_W - 1, 0), (0, 0)))
    y = zp[:, 0:L] * conv_w[0]
    for i in range(1, CONV_W):
        y = y + zp[:, i:i + L] * conv_w[i]
    return b_gate * y

def forgetting_attention(q, k, v, f_logit, q_g, k_g):
    Bn, L, H, hd = q.shape
    q = rms_norm(q, q_g)
    k = rms_norm(k, k_g)
    c = jnp.cumsum(jax.nn.log_sigmoid(f_logit.astype(jnp.float32)), axis=1)
    n_blk = -(-L // Q_BLOCK)
    Lp = n_blk * Q_BLOCK
    pad = Lp - L
    q = jnp.pad(q, ((0, 0), (0, pad), (0, 0), (0, 0)))
    k = jnp.pad(k, ((0, 0), (0, pad), (0, 0), (0, 0)))
    v = jnp.pad(v, ((0, 0), (0, pad), (0, 0), (0, 0)))
    c = jnp.pad(c, ((0, 0), (0, pad), (0, 0)), mode="edge")
    c_k = c.transpose(0, 2, 1)
    q_blocks = q.reshape(Bn, n_blk, Q_BLOCK, H, hd).transpose(1, 0, 2, 3, 4)
    c_blocks = c.reshape(Bn, n_blk, Q_BLOCK, H).transpose(1, 0, 3, 2)
    k_pos = jnp.arange(Lp)
    scale = FOX_HEAD_DIM ** -0.5

    def one_block(args):
        i, q_i, c_i = args
        s = jnp.einsum('bqhd,bkhd->bhqk', q_i, k).astype(jnp.float32) * scale
        s = s + (c_i[..., :, None] - c_k[..., None, :])
        q_pos = i * Q_BLOCK + jnp.arange(Q_BLOCK)
        s = jnp.where(k_pos[None, :] <= q_pos[:, None], s, -jnp.inf)
        p = jax.nn.softmax(s, axis=-1).astype(v.dtype)
        return jnp.einsum('bhqk,bkhd->bqhd', p, v)

    o = lax.map(one_block, (jnp.arange(n_blk), q_blocks, c_blocks))
    return o.transpose(1, 0, 2, 3, 4).reshape(Bn, Lp, H * hd)[:, :L]

def hierarchical_moe(x, w_rg, b_rg, w_re, b_re, w_gate, w_up, w_down):
    Bn, L, D = x.shape
    xf = x.reshape(-1, D)
    N = xf.shape[0]
    g_logits = (xf @ w_rg + b_rg).astype(jnp.float32)
    g_prob = jax.nn.softmax(g_logits, axis=-1)
    g_idx = jnp.argmax(g_logits, axis=-1)
    g_w = jnp.take_along_axis(g_prob, g_idx[:, None], axis=-1)
    e_logits = (xf @ w_re + b_re).astype(jnp.float32).reshape(N, N_GROUPS, EXPERTS_PER_GROUP)
    e_logits = jnp.take_along_axis(e_logits, g_idx[:, None, None], axis=1)[:, 0]
    top_p, top_j = lax.top_k(jax.nn.softmax(e_logits, axis=-1), TOP_K_IN_GROUP)
    weights = g_w * top_p / jnp.sum(top_p, axis=-1, keepdims=True)
    expert = g_idx[:, None] * EXPERTS_PER_GROUP + top_j

    A = N * TOP_K_IN_GROUP
    eid = expert.reshape(-1).astype(jnp.int32)
    tok = jnp.repeat(jnp.arange(N, dtype=jnp.int32), TOP_K_IN_GROUP)
    wt = weights.reshape(-1)
    order = jnp.argsort(eid)
    s_eid = eid[order]
    counts = jnp.zeros((N_EXPERTS,), jnp.int32).at[eid].add(1)
    pcounts = (counts + MOE_BLOCK - 1) // MOE_BLOCK * MOE_BLOCK
    start = jnp.cumsum(counts) - counts
    pend = jnp.cumsum(pcounts)
    pstart = pend - pcounts
    dest = pstart[s_eid] + jnp.arange(A, dtype=jnp.int32) - start[s_eid]
    n_blocks = -(-(A + N_EXPERTS * (MOE_BLOCK - 1)) // MOE_BLOCK)
    P = n_blocks * MOE_BLOCK
    slot_tok = jnp.full((P,), N, jnp.int32).at[dest].set(tok[order])
    slot_w = jnp.zeros((P,), wt.dtype).at[dest].set(wt[order])
    blk_eid = jnp.minimum(jnp.searchsorted(pend, jnp.arange(n_blocks, dtype=jnp.int32) * MOE_BLOCK, side='right'), N_EXPERTS - 1)
    x_pad = jnp.concatenate([xf, jnp.zeros((1, D), xf.dtype)], axis=0)
    xs = x_pad[slot_tok].reshape(n_blocks, MOE_BLOCK, D)

    def expert_block(args):
        e, xb = args
        h = jax.nn.silu(xb @ w_gate[e]) * (xb @ w_up[e])
        return h @ w_down[e]

    ys = lax.map(expert_block, (blk_eid, xs)).reshape(P, D)
    ys = ys * slot_w[:, None]
    out = jnp.zeros((N + 1, D), ys.dtype).at[slot_tok].add(ys)[:N]
    return out.reshape(Bn, L, D).astype(x.dtype)

def setup_inputs(seed: int = 0) -> dict:
    key = jax.random.key(seed)
    ks = jax.random.split(key, 24)
    nrm = lambda k, shape, s: jax.random.normal(k, shape, jnp.float32) * s
    Dm = D_MODEL
    return {
        "x": nrm(ks[0], (BATCH, SEQ, Dm), 1.0),
        "meta_tokens": nrm(ks[1], (N_META, Dm), 1.0),
        "norm1_g": 1.0 + nrm(ks[2], (DEPTH, Dm), 0.02),
        "w_in": nrm(ks[3], (DEPTH, Dm, IN_COLS), Dm ** -0.5),
        "b_forget": jax.random.uniform(ks[4], (DEPTH, N_FOX_HEADS), jnp.float32, 1.0, 4.0),
        "conv_w": nrm(ks[5], (DEPTH, CONV_W, D_CONV), CONV_W ** -0.5),
        "w_conv_out": nrm(ks[6], (DEPTH, D_CONV, Dm), D_CONV ** -0.5),
        "q_norm_g": 1.0 + nrm(ks[7], (DEPTH, FOX_HEAD_DIM), 0.02),
        "k_norm_g": 1.0 + nrm(ks[8], (DEPTH, FOX_HEAD_DIM), 0.02),
        "w_att_out": nrm(ks[9], (DEPTH, D_ATT, Dm), D_ATT ** -0.5),
        "w_merge_out": nrm(ks[10], (DEPTH, Dm, Dm), Dm ** -0.5),
        "norm2_g": 1.0 + nrm(ks[11], (DEPTH, Dm), 0.02),
        "w_router_group": nrm(ks[12], (DEPTH, Dm, N_GROUPS), Dm ** -0.5),
        "b_router_group": nrm(ks[13], (DEPTH, N_GROUPS), 0.01),
        "w_router_expert": nrm(ks[14], (DEPTH, Dm, N_EXPERTS), Dm ** -0.5),
        "b_router_expert": nrm(ks[15], (DEPTH, N_EXPERTS), 0.01),
        "w_exp_gate": nrm(ks[16], (DEPTH, N_EXPERTS, Dm, D_EXPERT), Dm ** -0.5),
        "w_exp_up": nrm(ks[17], (DEPTH, N_EXPERTS, Dm, D_EXPERT), Dm ** -0.5),
        "w_exp_down": nrm(ks[18], (DEPTH, N_EXPERTS, D_EXPERT, Dm), D_EXPERT ** -0.5),
    }

def reference(x, meta_tokens, norm1_g, w_in, b_forget, conv_w, w_conv_out, q_norm_g, k_norm_g,
              w_att_out, w_merge_out, norm2_g, w_router_group, b_router_group, w_router_expert,
              b_router_expert, w_exp_gate, w_exp_up, w_exp_down):
    Bn, S, Dm = x.shape
    meta = jnp.broadcast_to(meta_tokens[None].astype(x.dtype), (Bn, N_META, Dm))
    h = jnp.concatenate([meta, x], axis=1)
    L = h.shape[1]
    split_at = list(np.cumsum(SPLIT_SIZES)[:-1])
    for l in range(DEPTH):
        hn = rms_norm(h, norm1_g[l])
        proj = hn @ w_in[l]
        b_g, c_g, u, q, k, v, f_logit, ga, gb = jnp.split(proj, split_at, axis=-1)
        y_a = short_gated_conv(b_g, c_g, u, conv_w[l]) @ w_conv_out[l]
        q = q.reshape(Bn, L, N_FOX_HEADS, FOX_HEAD_DIM)
        k = k.reshape(Bn, L, N_FOX_HEADS, FOX_HEAD_DIM)
        v = v.reshape(Bn, L, N_FOX_HEADS, FOX_HEAD_DIM)
        attn = forgetting_attention(q, k, v, f_logit + b_forget[l], q_norm_g[l], k_norm_g[l])
        y_b = attn @ w_att_out[l]
        y = (jax.nn.sigmoid(ga) * y_a + jax.nn.sigmoid(gb) * y_b) @ w_merge_out[l]
        h = h + y
        h = h + hierarchical_moe(rms_norm(h, norm2_g[l]), w_router_group[l], b_router_group[l],
                                 w_router_expert[l], b_router_expert[l], w_exp_gate[l],
                                 w_exp_up[l], w_exp_down[l])
    return h[:, N_META:]


_drawn_inputs = setup_inputs


def setup_inputs(seed=0):
    import zlib

    import numpy as np

    out = dict(_drawn_inputs(seed))
    spreads = {}
    factors = {'q_norm_g': 5.332, 'k_norm_g': 6.167, 'b_router_group': 5.889, 'b_router_expert': 4.175}
    for name, (base, spread) in spreads.items():
        noise = np.random.default_rng([zlib.crc32(name.encode()), seed]).standard_normal(out[name].shape)
        drawn = base * np.exp(spread * noise) if base else spread * noise
        out[name] = __import__('jax').numpy.asarray(drawn.astype(out[name].dtype))
    for name, factor in factors.items():
        out[name] = (out[name] * factor).astype(out[name].dtype)
    return out
```

```python
from contextlib import ExitStack

import concourse.bass as bass
from concourse import mybir

F32 = mybir.dt.float32
F32R = mybir.dt.float32r
BF16 = mybir.dt.bfloat16
I32 = mybir.dt.int32
ALU = mybir.AluOpType
ACT = mybir.ActivationFunctionType
AX = mybir.AxisListType

P = 128
BANK = 512
D = 1024
KT = D // P
SEQ = 1024
NB = SEQ // P
META = 16
L = SEQ + META
H, HD = 16, 64
NG, EPG = 4, 8
NE = NG * EPG
DE = 512
KE = DE // P
EPS = 1e-6
SLOTS = 2 * SEQ
XROWS = SLOTS + P
MAXBLK = SLOTS // P + NE - 1
NEG = -float(2 ** 100)
COL = dict(B=0, C=D, U=2 * D, Q=3 * D, K=4 * D, V=5 * D, F=6 * D, GA=6 * D + H, GB=7 * D + H)


class Memory:

    def __init__(self, nc):
        self.nc = nc
        self.base = (nc.sbuf_base + 63) // 64 * 64
        self.size = nc.sbuf_top - self.base

    def at(self, name, offset, shape, dtype=F32):
        n = 4
        for s in shape[1:]:
            n *= s
        if dtype == BF16:
            n //= 2
        assert offset + n <= self.size, (name, offset + n, self.size)
        return self.nc.alloc_sbuf_tensor_at(name, shape, dtype, offset=self.base + offset)


def f32(ap):
    return ap.bitcast(F32)


def gate(eng, sem, value, passed):
    eng.wait_ge(sem, value)
    eng.sem_inc(passed, 1)


def split3(eng, out, w_hi, w_lo, x_hi, x_lo, start, stop):
    eng.matmul(out, w_lo, x_hi, start=start, stop=False)
    eng.matmul(out, w_hi, x_lo, start=False, stop=False)
    return eng.matmul(out, w_hi, x_hi, start=False, stop=stop)


def norm1(nc, mem, sem, ctx, io, hT):
    h_hi, h_lo = hT
    base = 66560
    x_sb = [mem.at(f"n1_x{i}", base + 4096 * i, [P, D]) for i in range(2)]
    xn = [mem.at(f"n1_xn{i}", base + 8192 + 4096 * i, [P, D]) for i in range(2)]
    g_b = mem.at("n1_g", base + 16384, [P, D])
    sq = mem.at("n1_sq", base + 20480, [P, D])
    stat = mem.at("n1_stat", base + 24576, [P, 8])
    epsc = io["eps"]
    ident = io["ident"]
    pT = [ctx.enter_context(nc.psum_tensor(f"n1_T{i}", [P, KT, P], F32)) for i in range(2)]
    x_in = [sem(f"n1_x_in{i}") for i in range(2)]
    g_in, consts = sem("n1_g_in"), sem("n1_consts")
    squared, rms, recip, xn_done, turned, hi_done, lo_done = (
        sem("n1_" + s) for s in ("squared", "rms", "recip", "xn_done", "turned", "hi", "lo"))
    x_blocks = io["x"].rearrange("b (t p) d -> (b t) p d", p=P)

    def rows(n):
        return META if isinstance(n, int) and n == NB else P

    def hcols(n, r):
        return slice(SEQ, L) if r == META else bass.ds(n * P, P)

    with nc.Block() as block:
        @block.sync
        def _(sp):
            sp.dma_start(g_b[:], io["norm1_g"].partition_broadcast(P)).then_inc(g_in, 16)

            def load(n, s):
                r = rows(n)
                sp.wait_ge(xn_done, n + 1)
                src = io["meta_tokens"] if r == META else x_blocks[bass.ds(n, 1)].rearrange("a p d -> p (a d)")
                sp.dma_start(x_sb[s][0:r, :], src).then_inc(x_in[s], 16)

            load(0, 0)
            with sp.Fori(0, 3) as i:
                load(2 * i + 1, 1)
                load(2 * i + 2, 0)
            load(7, 1)
            load(8, 0)

        @block.gpsimd
        def _(pool):
            pool.memset(ident[:], 0.0).then_inc(consts, 1)
            pool.memset(io["onesp"][:], 1.0)
            pool.memset(io["one"][:], 1.0)
            pool.memset(epsc[:], EPS).then_inc(consts, 1)
            pool.wait_ge(consts, 2)
            pool.affine_select(out=ident[:], in_=ident[:], compare_op=ALU.not_equal, fill=1.0,
                               base=0, pattern=[[-1, P]], channel_multiplier=1).then_inc(consts, 1)

        @block.scalar
        def _(act):
            def front(n, s):
                r = rows(n)
                act.wait_ge(x_in[s], 16 * ((n + 2 - s) // 2) if isinstance(n, int) else 8 * (n - s) + 16)
                act.activation(sq[0:r, :], x_sb[s][0:r, :], ACT.Square,
                               accum_out=stat[0:r, s:s + 1]).then_inc(squared, 1)
                act.wait_ge(squared, n + 1)
                act.wait_ge(recip, n + 1)
                act.activation(stat[0:r, 2 + s:3 + s], stat[0:r, s:s + 1], ACT.Sqrt,
                               scale=1.0 / D, bias=epsc[0:r, :]).then_inc(rms, 1)

            def back(n, s):
                r = rows(n)
                act.wait_ge(turned, n + 3)
                act.activation(h_hi[:, :, hcols(n, r)], pT[s][:, :, 0:r], ACT.Copy).then_inc(hi_done, 1)

            act.wait_ge(consts, 2)
            front(0, 0)
            with act.Fori(0, 3) as i:
                front(2 * i + 1, 1)
                back(2 * i, 0)
                front(2 * i + 2, 0)
                back(2 * i + 1, 1)
            front(7, 1)
            back(6, 0)
            front(8, 0)
            back(7, 1)
            back(8, 0)

        @block.vector
        def _(dve):
            dve.sem_inc(xn_done, 2)
            dve.sem_inc(recip, 2)
            dve.sem_inc(lo_done, 2)

            def front(n, s):
                r = rows(n)
                dve.wait_ge(rms, n + 1)
                dve.reciprocal(stat[0:r, 4 + s:5 + s], stat[0:r, 2 + s:3 + s]).then_inc(recip, 1)
                dve.wait_ge(recip, n + 3)
                dve.wait_ge(turned, n + 1)
                dve.scalar_tensor_tensor(out=xn[s][0:r, :], in0=x_sb[s][0:r, :],
                                         scalar=stat[0:r, 4 + s:5 + s], in1=g_b[0:r, :],
                                         op0=ALU.mult, op1=ALU.mult).then_inc(xn_done, 1)

            def back(n, s):
                r = rows(n)
                dve.wait_ge(hi_done, n + 1)
                dve.tensor_tensor(h_lo[:, :, hcols(n, r)], pT[s][:, :, 0:r],
                                  f32(h_hi[:, :, hcols(n, r)]), ALU.subtract).then_inc(lo_done, 1)

            dve.wait_ge(g_in, 16)
            front(0, 0)
            with dve.Fori(0, 3) as i:
                front(2 * i + 1, 1)
                back(2 * i, 0)
                front(2 * i + 2, 0)
                back(2 * i + 1, 1)
            front(7, 1)
            back(6, 0)
            front(8, 0)
            back(7, 1)
            back(8, 0)

        @block.tensor
        def _(pe):
            pe.sem_inc(turned, 2)
            pe.wait_ge(consts, 3)

            def turn(n, s):
                r = rows(n)
                pe.wait_ge(xn_done, n + 3)
                pe.wait_ge(lo_done, n + 1)
                for k in range(KT):
                    last = pe.transpose(pT[s][:, k, 0:r], xn[s][0:r, k * P:(k + 1) * P], ident[0:r, 0:r])
                last.then_inc(turned, 1)

            turn(0, 0)
            with pe.Fori(0, 3) as i:
                turn(2 * i + 1, 1)
                turn(2 * i + 2, 0)
            turn(7, 1)
            turn(8, 0)


class WeightUnits:

    def __init__(self, mem, sem, name, base, slots):
        self.slots = slots
        self.raw = [mem.at(f"{name}_raw{i}", base + 4096 * i, [P, KT, P]) for i in range(slots)]
        base += 4096 * slots
        self.hi = [mem.at(f"{name}_whi{i}", base + 4096 * i, [P, KT, P], F32R) for i in range(slots)]
        base += 4096 * slots
        self.lo = [mem.at(f"{name}_wlo{i}", base + 4096 * i, [P, KT, P], F32R) for i in range(slots)]
        self.raw_in = [sem(f"{name}_raw_in{i}") for i in range(slots)]
        self.hi_done, self.lo_done, self.used, self.passed = (
            sem(f"{name}_{s}") for s in ("whi", "wlo", "wused", "passed"))

    def load(self, sp, source, n, s):
        gate(sp, self.lo_done, n + 1, self.passed)
        sp.dma_start(self.raw[s][:], source.rearrange("(k p) c -> p k c", p=P)).then_inc(self.raw_in[s], 16)

    def split_hi(self, act, n, s, use):
        act.wait_ge(self.raw_in[s], 16 * use + 16)
        act.wait_ge(self.used, n + 1)
        act.activation(self.hi[s][:], self.raw[s][:], ACT.Copy).then_inc(self.hi_done, 1)

    def split_lo(self, dve, n, s):
        dve.wait_ge(self.hi_done, n + 1)
        dve.tensor_tensor(self.lo[s][:], self.raw[s][:], f32(self.hi[s][:]),
                          ALU.subtract).then_inc(self.lo_done, 1)

    def product(self, pe, n, s, x, outs, cols):
        pe.wait_ge(self.lo_done, n + 1 + self.slots)
        last = None
        for k in range(KT):
            for step, (w, y) in enumerate(((self.lo, x[0]), (self.hi, x[1]), (self.hi, x[0]))):
                for out, c in zip(outs, cols):
                    last = pe.matmul(out, w[s][:, k, :], y[:, k, c], start=(k == 0 and step == 0),
                                     stop=(k == KT - 1 and step == 2))
        last.then_inc(self.used, 1)


def conv_merge(nc, mem, sem, ctx, io, hT, cT):
    h_hi, h_lo = hT
    c_hi, c_lo = cT
    base = 132096
    ring = WeightUnits(mem, sem, "cm", base, 3)
    base += 3 * 12288
    forget = WeightUnits(mem, sem, "cf", base, 1)
    c_sb = mem.at("cm_c", base, [P, SEQ + 2])
    z = mem.at("cm_z", base + 4160, [P, SEQ + 2])
    y0 = mem.at("cm_y0", base + 8320, [P, SEQ])
    y1 = mem.at("cm_y1", base + 12416, [P, SEQ])
    cv = mem.at("cm_cv", base + 16512, [P, SEQ])
    sga, part, sgb = c_sb, y0, y1
    fx = mem.at("cm_fx", base + 20608, [H, L])
    fa = mem.at("cm_fa", base + 24768, [H, L])
    cw = mem.at("cm_cw", base + 28928, [P, KT, 3])
    bf = mem.at("cm_bf", base + 29024, [H, 1])
    ones = io["onesp"]
    out = [ctx.enter_context(nc.psum_tensor(f"cm_o{i}", [P, SEQ], F32)) for i in range(3)]
    mt = [ctx.enter_context(nc.psum_tensor(f"cm_m{i}", [P, BANK], F32)) for i in range(2)]
    halves = [slice(0, BANK), slice(BANK, SEQ)]
    out_of = [[o[:, c] for c in halves] for o in out]
    consts_in = sem("cm_consts")
    evac = [sem(f"cm_evac{i}") for i in range(3)]
    y0_done, y1_done, conv_hi, conv_lo, fchain, f_out, stored = (
        sem("cm_" + s) for s in ("y0", "y1", "conv_hi", "conv_lo", "fchain", "f_out", "stored"))
    sgb_done, part_done, part_stored, sgb_stored, passed, part_free, sgb_free = (
        sem("cm_" + s) for s in ("sgb", "part", "part_stored", "sgb_stored", "pool_passed", "part_free", "sgb_free"))
    w_in, w_conv = io["w_in"][0], io["w_conv_out"][0]

    with nc.Block() as block:
        @block.sync
        def _(sp):
            with nc.allow_non_contiguous_dma(reason="small tables, one element each"):
                sp.dma_start(bf[:], io["b_forget"].rearrange("o h -> h o")).then_inc(consts_in, 16)
                for i in range(3):
                    sp.dma_start(cw[:, :, i], io["conv_w"][0, i].rearrange("(m p) -> p m", p=P)).then_inc(consts_in, 16)
            forget.load(sp, w_in[:, COL["F"]:COL["F"] + P], 0, 0)
            with sp.Fori(0, KT) as m:
                for s, first in enumerate((COL["C"], COL["U"], COL["B"])):
                    ring.load(sp, w_in[:, bass.ds(m * P + first, P)], 3 * m + s, s)
            with sp.Fori(0, KT) as m:
                ring.load(sp, w_in[:, bass.ds(m * P + COL["GA"], P)], 3 * m + 24, 0)
                ring.load(sp, w_conv[:, bass.ds(m * P, P)], 3 * m + 25, 1)
                ring.load(sp, w_in[:, bass.ds(m * P + COL["GB"], P)], 3 * m + 26, 2)

        @block.gpsimd
        def _(pool):
            pool.wait_ge(fchain, 6)
            pool.dma_start(io["qT"][:, HD, :], fa[:, 0:SEQ]).then_inc(stored, 16)
            pool.dma_start(io["qT"][:, HD + 1, :], ones[0:H, 0:SEQ]).then_inc(stored, 16)
            pool.dma_start(io["kT"][:, HD, :], ones[0:H, :]).then_inc(stored, 16)
            pool.dma_start(io["kT"][:, HD + 1, :], fx[:]).then_inc(stored, 16)
            with pool.Fori(0, KT) as m:
                gate(pool, part_done, m + 2, passed)
                pool.dma_start(io["part"][bass.ds(m, 1)].rearrange("a p t -> p (a t)"), part[:]).then_inc(part_stored, 16)
                gate(pool, sgb_done, m + 2, passed)
                pool.dma_start(io["sgb"][bass.ds(m, 1)].rearrange("a p t -> p (a t)"), sgb[:]).then_inc(sgb_stored, 16)
                pool.wait_ge(part_stored, 16 * m + 16)
                pool.sem_inc(part_free, 1)
                pool.wait_ge(sgb_stored, 16 * m + 16)
                pool.sem_inc(sgb_free, 1)
            pool.wait_ge(stored, 64)

        @block.scalar
        def _(act):
            act.wait_ge(forget.raw_in[0], 16)
            forget.split_hi(act, 0, 0, 0)
            ring.split_hi(act, 0, 0, 0)
            ring.split_hi(act, 1, 1, 0)
            act.wait_ge(fchain, 1)
            act.activation(fa[:], fa[:], ACT.Exp, scale=-1.0).then_inc(fchain, 1)
            act.wait_ge(fchain, 2)
            act.activation(fa[:], fa[:], ACT.Ln, bias=io["one"][0:H, :]).then_inc(fchain, 1)
            act.sem_inc(sgb_free, 1)
            act.sem_inc(sgb_done, 1)
            act.wait_ge(consts_in, 64)

            with act.Fori(0, KT) as m:
                ring.split_hi(act, 3 * m + 2, 2, m)
                act.wait_ge(ring.used, 3 * m + 4)
                act.wait_ge(evac[1], m + 1)
                act.activation(c_sb[:, 0:2], mt[0][:, 0:2], ACT.Copy)
                act.activation(c_sb[:, 2:], out[0][:], ACT.Copy).then_inc(evac[0], 1)
                ring.split_hi(act, 3 * m + 3, 0, m + 1)
                act.wait_ge(evac[1], m + 2)
                act.activation(y0[:], z[:, 0:SEQ], ACT.Copy,
                               scale=cw[:, bass.ds(m, 1), 0]).then_inc(y0_done, 1)
                ring.split_hi(act, 3 * m + 4, 1, m + 1)
                act.wait_ge(evac[2], m + 2)
                act.activation(c_hi[:, bass.ds(m, 1), :], cv[:], ACT.Copy).then_inc(conv_hi, 1)

            def gates(m, more):
                ring.split_hi(act, 3 * m + 26, 2, m + 8)
                act.wait_ge(ring.used, 3 * m + 28)
                act.wait_ge(evac[1], m + 9)
                act.activation(sga[:, 0:SEQ], out[0][:], ACT.Sigmoid).then_inc(evac[0], 1)
                if more:
                    ring.split_hi(act, 3 * m + 27, 0, m + 9)
                    ring.split_hi(act, 3 * m + 28, 1, m + 9)
                act.wait_ge(ring.used, 3 * m + 30)
                act.wait_ge(sgb_free, m + 1)
                act.activation(sgb[:], out[2][:], ACT.Sigmoid).then_inc(sgb_done, 1)

            with act.Fori(0, KT - 1) as m:
                gates(m, True)
            gates(KT - 1, False)

        @block.vector
        def _(dve):
            dve.sem_inc(forget.lo_done, 1)
            dve.sem_inc(ring.lo_done, 3)
            dve.sem_inc(evac[0], 1)
            dve.sem_inc(evac[1], 1)
            dve.sem_inc(part_free, 1)
            dve.sem_inc(part_done, 1)
            forget.split_lo(dve, 0, 0)
            ring.split_lo(dve, 0, 0)
            ring.split_lo(dve, 1, 1)
            dve.wait_ge(forget.used, 2)
            dve.wait_ge(consts_in, 64)
            dve.tensor_scalar(fx[:, SEQ:L], mt[1][0:H, 0:META], bf[:], None, ALU.add)
            dve.tensor_scalar(fx[:, 0:SEQ], out[2][0:H, :], bf[:], None, ALU.add).then_inc(evac[2], 1)
            dve.wait_ge(evac[2], 1)
            dve.scalar_tensor_tensor(out=fa[:], in0=fx[:], scalar=-1.0, in1=fx[:],
                                     op0=ALU.mult, op1=ALU.max).then_inc(fchain, 1)
            dve.wait_ge(fchain, 3)
            dve.scalar_tensor_tensor(out=fx[:], in0=fx[:], scalar=0.0, in1=fa[:],
                                     op0=ALU.min, op1=ALU.subtract).then_inc(fchain, 1)
            dve.wait_ge(fchain, 4)
            dve.tensor_tensor_scan(fa[:, SEQ:L], ones[0:H, 0:META], fx[:, SEQ:L], 0.0,
                                   ALU.mult, ALU.add).then_inc(f_out, 1)
            dve.wait_ge(f_out, 1)
            dve.tensor_tensor_scan(fa[:, 0:SEQ], ones[0:H, 0:SEQ], fx[:, 0:SEQ], fa[:, L - 1:L],
                                   ALU.mult, ALU.add).then_inc(fchain, 1)
            dve.wait_ge(fchain, 5)
            dve.tensor_scalar(fx[:], fa[:], -1.0, None, ALU.mult).then_inc(fchain, 1)

            with dve.Fori(0, KT) as m:
                ring.split_lo(dve, 3 * m + 2, 2)
                ring.split_lo(dve, 3 * m + 3, 0)
                dve.wait_ge(ring.used, 3 * m + 5)
                dve.wait_ge(evac[0], m + 2)
                dve.tensor_tensor(z[:, 0:2], mt[1][:, 0:2], c_sb[:, 0:2], ALU.mult)
                dve.tensor_tensor(z[:, 2:], out[1][:], c_sb[:, 2:], ALU.mult).then_inc(evac[1], 1)
                dve.wait_ge(evac[1], m + 2)
                dve.wait_ge(y0_done, m + 1)
                dve.scalar_tensor_tensor(out=y1[:], in0=z[:, 1:SEQ + 1], scalar=cw[:, bass.ds(m, 1), 1],
                                         in1=y0[:], op0=ALU.mult, op1=ALU.add).then_inc(y1_done, 1)
                dve.wait_ge(y1_done, 2 * m + 1)
                dve.scalar_tensor_tensor(out=y1[:], in0=z[:, 2:SEQ + 2], scalar=cw[:, bass.ds(m, 1), 2],
                                         in1=y1[:], op0=ALU.mult, op1=ALU.add).then_inc(y1_done, 1)
                ring.split_lo(dve, 3 * m + 4, 1)
                dve.wait_ge(y1_done, 2 * m + 2)
                dve.wait_ge(ring.used, 3 * m + 6)
                dve.tensor_tensor(cv[:], out[2][:], y1[:], ALU.mult).then_inc(evac[2], 1)
                dve.wait_ge(conv_hi, m + 1)
                dve.tensor_tensor(c_lo[:, bass.ds(m, 1), :], cv[:], f32(c_hi[:, bass.ds(m, 1), :]),
                                  ALU.subtract).then_inc(conv_lo, 1)

            def gated(m, more):
                ring.split_lo(dve, 3 * m + 26, 2)
                if more:
                    ring.split_lo(dve, 3 * m + 27, 0)
                dve.wait_ge(ring.used, 3 * m + 29)
                dve.wait_ge(evac[0], m + 10)
                dve.wait_ge(part_free, m + 1)
                dve.tensor_tensor(part[:], out[1][:], sga[:, 0:SEQ], ALU.mult).then_inc(part_done, 1)
                dve.wait_ge(part_done, m + 2)
                dve.sem_inc(evac[1], 1)
                if more:
                    ring.split_lo(dve, 3 * m + 28, 1)

            with dve.Fori(0, KT - 1) as m:
                gated(m, True)
            gated(KT - 1, False)

        @block.tensor
        def _(pe):
            pe.sem_inc(forget.used, 1)
            pe.sem_inc(ring.used, 3)
            meta2 = slice(L - 2, L)
            forget.product(pe, 0, 0, hT, [out[2][:, c] for c in halves] + [mt[1][:, 0:META]],
                           halves + [slice(SEQ, L)])
            with pe.Fori(0, KT) as m:
                pe.wait_ge(evac[0], m + 1)
                ring.product(pe, 3 * m, 0, hT, out_of[0] + [mt[0][:, 0:2]], halves + [meta2])
                pe.wait_ge(evac[1], m + 1)
                pe.wait_ge(evac[2], m + 1)
                ring.product(pe, 3 * m + 1, 1, hT, out_of[1] + [mt[1][:, 0:2]], halves + [meta2])
                ring.product(pe, 3 * m + 2, 2, hT, out_of[2], halves)
            pe.wait_ge(conv_lo, KT)
            with pe.Fori(0, KT) as m:
                pe.wait_ge(evac[0], m + 9)
                ring.product(pe, 3 * m + 24, 0, hT, out_of[0], halves)
                pe.wait_ge(evac[1], m + 9)
                ring.product(pe, 3 * m + 25, 1, cT, out_of[1], halves)
                pe.wait_ge(evac[2], 9)
                pe.wait_ge(sgb_done, m + 1)
                ring.product(pe, 3 * m + 26, 2, hT, out_of[2], halves)


def qkv(nc, mem, sem, ctx, io, hT):
    h_hi, h_lo = hT
    HPC = BANK // HD
    CT = BANK // P
    base = 66560
    raw = [mem.at(f"qk_raw{i}", base + 8192 * i, [P, KT // 2, BANK]) for i in range(2)]
    w_hi = mem.at("qk_whi", base + 16384, [P, KT, BANK], F32R)
    w_lo = mem.at("qk_wlo", base + 32768, [P, KT, BANK], F32R)
    base += 49152
    turned_sb = mem.at("qk_turned", base, [P, 2, CT, L])
    base += 33280
    qn = [mem.at(f"qk_qn{i}", base + 2048 * i, [P, BANK]) for i in range(3)]
    v_sb = [mem.at(f"qk_v{i}", base + 6144 + 2048 * i, [P, BANK]) for i in range(3)]
    sq = mem.at("qk_sq", base + 12288, [P, BANK])
    ss = mem.at("qk_ss", base + 14336, [P, HPC])
    rms = mem.at("qk_rms", base + 14400, [P, HPC])
    rstd = mem.at("qk_rstd", base + 14464, [P, HPC])
    gain = mem.at("qk_gain", base + 14528, [P, 4])
    ident = io["ident"]
    mm = [ctx.enter_context(nc.psum_tensor(f"qk_mm{i}", [P, BANK], F32)) for i in range(3)]
    pT = [ctx.enter_context(nc.psum_tensor(f"qk_T{i}", [P, CT, P], F32)) for i in range(3)]
    raw_in = [sem(f"qk_raw_in{i}") for i in range(2)]
    names = ("whi", "wlo", "w_used", "sp_passed", "pool_passed", "mm_done", "sq_done", "summed", "rms_done",
             "rstd_done", "freed", "turned", "evac", "gains_in", "gains", "stored", "v_done", "pe_passed")
    (whi, wlo, w_used, sp_passed, pool_passed, mm_done, sq_done, summed, rms_done,
     rstd_done, freed, turned, evac, gains_in, gains, stored, v_done, pe_passed) = (sem("qk_" + n) for n in names)
    v_stored = [sem(f"qk_v_stored{i}") for i in range(3)]
    v_free = sem("qk_v_free")
    w_cols = io["w_in"][0].rearrange("(k p) c -> p k c", p=P)

    PASSES = dict(q=(0, 0, NB), k=(2, 2 * NB, NB + 1), v=(4, 2 * NB + 2 * (NB + 1), NB + 1))

    def rows(t):
        return META if t == NB else P

    def toks(t):
        return slice(t * P, t * P + rows(t))

    with nc.Block() as block:
        @block.sync
        def _(sp):
            with nc.allow_non_contiguous_dma(reason="64-element gain columns"):
                for c, g in enumerate(("q_norm_g", "k_norm_g")):
                    for h in range(2):
                        sp.dma_start(gain[h * HD:(h + 1) * HD, c:c + 1],
                                     io[g].rearrange("o d -> d o")).then_inc(gains_in, 16)
            for c0, first in ((0, "Q"), (2, "K"), (4, "V")):
                with sp.Fori(0, 2) as c:
                    for half in range(2):
                        gate(sp, wlo, 8 * c + (8 * c0 + 4 * half + 4), sp_passed)
                        sp.dma_start(raw[half][:], w_cols[:, 4 * half:4 * half + 4,
                                                          bass.ds(c * BANK + COL[first], BANK)])\
                          .then_inc(raw_in[half], 16)

        @block.gpsimd
        def _(pool):
            for name, dst in (("q", io["qT"]), ("k", io["kT"])):
                n0, g0, blocks = PASSES[name]
                width = SEQ if name == "q" else L
                heads = dst.rearrange("(c ct h) d t -> h c d ct t", c=2, h=2)
                with pool.Fori(0, 2) as c:
                    gate(pool, evac, blocks * c + (g0 + blocks + 2), pool_passed)
                    for h in range(2):
                        pool.dma_start(heads[h, bass.ds(c, 1), 0:HD].rearrange("a d ct t -> (a d) ct t"),
                                       turned_sb[h * HD:(h + 1) * HD, bass.ds(c, 1), :, 0:width]
                                       .rearrange("p a ct t -> p (a ct) t")).then_inc(stored, 16)
                pool.wait_ge(stored, 64 if name == "q" else 128)
                pool.sem_inc(v_free, 1)
            for c in range(2):
                for t in range(NB + 1):
                    u = 9 * c + t
                    pool.wait_ge(v_done, u + 1)
                    pool.dma_start(io["v"][toks(t), c * BANK:(c + 1) * BANK],
                                   v_sb[t % 3][0:rows(t), :]).then_inc(v_stored[t % 3], 16)
                    if u >= 1:
                        pool.wait_ge(v_stored[(t - 1) % 3], 16 * (3 * ((u - 1) // 9) + ((u - 1) % 9) // 3 + 1))
                        pool.sem_inc(v_free, 1)
            pool.wait_ge(v_stored[2], 96)

        def split_hi(act, n, blocks_before):
            for k in range(KT):
                if k % 4 == 0:
                    act.wait_ge(raw_in[k // 4], 16 * n + 16)
                if k < KT - 1:
                    act.wait_ge(w_used, 7 * n + (k + 1))
                elif blocks_before is not None:
                    act.wait_ge(mm_done, blocks_before)
                act.activation(w_hi[:, k, :], raw[k // 4][:, k % 4, :], ACT.Copy).then_inc(whi, 1)

        def split_lo(dve, n):
            for k in range(KT):
                dve.wait_ge(whi, 8 * n + (k + 1))
                dve.tensor_tensor(w_lo[:, k, :], raw[k // 4][:, k % 4, :], f32(w_hi[:, k, :]),
                                  ALU.subtract).then_inc(wlo, 1)

        @block.scalar
        def _(act):
            def front(g, t):
                r = rows(t)
                act.wait_ge(mm_done, g + (t + 1))
                act.wait_ge(summed, g + (t + 1))
                act.activation(sq[0:r, :], mm[t % 3][0:r, :], ACT.Square).then_inc(sq_done, 1)
                act.wait_ge(summed, g + (t + 2))
                act.activation(rms[0:r, :], ss[0:r, :], ACT.Sqrt, scale=1.0 / HD,
                               bias=io["eps"][0:r, :]).then_inc(rms_done, 1)

            def back(g, t, c, gcol):
                r = rows(t)
                act.wait_ge(turned, g + (t + 3))
                act.activation(turned_sb[:, bass.ds(c, 1), :, toks(t)].rearrange("p a ct t -> p (a ct) t"),
                               pT[t % 3][:, :, 0:r], ACT.Copy,
                               scale=gain[:, gcol:gcol + 1]).then_inc(evac, 1)

            act.sem_inc(evac, 2)
            split_hi(act, 0, None)
            act.wait_ge(gains, 1)
            for gcol, name in ((2, "q"), (1, "k")):
                n0, g0, blocks = PASSES[name]
                if name == "k":
                    act.wait_ge(v_free, 1)
                with act.Fori(0, 2) as c:
                    g = blocks * c + g0
                    for t in range(blocks - 1):
                        front(g, t)
                        if t:
                            back(g, t - 1, c, gcol)
                    split_hi(act, c + (n0 + 1), g + blocks)
                    front(g, blocks - 1)
                    back(g, blocks - 2, c, gcol)
                    back(g, blocks - 1, c, gcol)
            n0, g0, blocks = PASSES["v"]
            for c in range(2):
                for t in range(blocks):
                    if c == 0 and t == blocks - 1:
                        split_hi(act, n0 + 1, g0 + blocks)
                    u = blocks * c + t
                    act.wait_ge(mm_done, g0 + u + 1)
                    if u >= 3:
                        act.wait_ge(v_free, 2 + u - 2)
                    act.activation(v_sb[t % 3][0:rows(t), :], mm[t % 3][0:rows(t), :],
                                   ACT.Copy).then_inc(v_done, 1)

        @block.vector
        def _(dve):
            dve.sem_inc(wlo, 8)
            dve.sem_inc(summed, 1)
            dve.sem_inc(freed, 2)
            split_lo(dve, 0)
            dve.wait_ge(gains_in, 64)
            dve.tensor_scalar(gain[:, 2:3], gain[:, 0:1], HD ** -0.5, None, ALU.mult).then_inc(gains, 1)

            def norm(g, t):
                r = rows(t)
                dve.wait_ge(sq_done, g + (t + 1))
                dve.tensor_reduce(ss[0:r, :], sq[0:r, :].rearrange("p (h d) -> p h d", d=HD), AX.X,
                                  ALU.add).then_inc(summed, 1)
                dve.wait_ge(rms_done, g + (t + 1))
                dve.reciprocal(rstd[0:r, :], rms[0:r, :]).then_inc(rstd_done, 1)
                dve.wait_ge(rstd_done, g + (t + 1))
                dve.wait_ge(turned, g + (t + 1))
                dve.tensor_tensor(qn[t % 3][0:r, :].rearrange("p (h d) -> p h d", d=HD),
                                  mm[t % 3][0:r, :].rearrange("p (h d) -> p h d", d=HD),
                                  rstd[0:r, :].unsqueeze(2).to_broadcast([r, HPC, HD]),
                                  ALU.mult).then_inc(freed, 1)

            for name in ("q", "k"):
                n0, g0, blocks = PASSES[name]
                with dve.Fori(0, 2) as c:
                    g = blocks * c + g0
                    for t in range(blocks - 1):
                        norm(g, t)
                    split_lo(dve, c + (n0 + 1))
                    norm(g, blocks - 1)
            split_lo(dve, 5)

        @block.tensor
        def _(pe):
            pe.sem_inc(w_used, 7)
            pe.sem_inc(turned, 2)

            def product(n, g, t, last_block, v=None):
                r = rows(t)
                if v is None:
                    pe.wait_ge(freed, g + (t + 1))
                else:
                    pe.wait_ge(freed, PASSES["v"][1] + 2)
                    if v >= 2:
                        pe.wait_ge(v_done, v - 1)
                for k in range(KT):
                    if t == 0:
                        pe.wait_ge(wlo, 8 * n + (k + 9))
                    x_hi, x_lo = h_hi[:, k, toks(t)], h_lo[:, k, toks(t)]
                    pe.matmul(mm[t % 3][0:r, :], x_hi, w_lo[:, k, :], start=(k == 0), stop=False)
                    pe.matmul(mm[t % 3][0:r, :], x_lo, w_hi[:, k, :], start=False, stop=False)
                    last = pe.matmul(mm[t % 3][0:r, :], x_hi, w_hi[:, k, :], start=False, stop=(k == KT - 1))
                    if t == last_block and k < KT - 1:
                        last.then_inc(w_used, 1)
                last.then_inc(mm_done, 1)

            def turn(g, t):
                r = rows(t)
                pe.wait_ge(freed, g + (t + 3))
                pe.wait_ge(evac, g + (t + 1))
                if r < P:
                    pe.sem_inc(pe_passed, 1)
                for ct in range(CT):
                    last = pe.transpose(pT[t % 3][:, ct, 0:r], qn[t % 3][0:r, ct * P:(ct + 1) * P],
                                        ident[0:r, 0:r])
                last.then_inc(turned, 1)

            for name in ("q", "k"):
                n0, g0, blocks = PASSES[name]
                with pe.Fori(0, 2) as c:
                    g = blocks * c + g0
                    for t in range(blocks):
                        product(c + n0, g, t, blocks - 1)
                        if t:
                            turn(g, t - 1)
                    turn(g, blocks - 1)
            n0, g0, blocks = PASSES["v"]
            for c in range(2):
                for t in range(blocks):
                    product(n0 + c, g0 + blocks * c, t, blocks - 1, v=blocks * c + t)


def attention(nc, mem, sem, ctx, io, aT):
    a_hi, a_lo = aT
    QB = BANK // P
    KB = NB + 1
    base = 65536
    q_sb = [mem.at(f"at_q{i}", base + 4096 * i, [HD + 2, SEQ]) for i in range(2)]
    base += 8192
    k_sb = [mem.at(f"at_k{i}", base + 4160 * i, [HD + 2, L]) for i in range(2)]
    base += 8320
    v_sb = [mem.at(f"at_v{i}", base + 2304 * i, [P, KB, HD]) for i in range(2)]
    base += 4608
    probs = mem.at("at_p", base, [P, 2 * QB, L])
    base += 33280
    pt_sb = [mem.at(f"at_pt{i}", base + 2048 * i, [P, BANK]) for i in range(2)]
    base += 4096
    top = mem.at("at_top", base, [P, 2 * QB])
    ntop = mem.at("at_ntop", base + 32, [P, 2 * QB])
    rsum = mem.at("at_rsum", base + 64, [P, 2 * QB])
    inv = mem.at("at_inv", base + 96, [P, 2 * QB])
    eye = mem.at("at_eye", base + 128, [P, P], BF16)
    mask = mem.at("at_mask", base + 384, [P, P], BF16)
    ident = io["ident"]
    ps = [ctx.enter_context(nc.psum_tensor(f"at_s{i}", [P, 3 * BANK], F32)) for i in range(2)]
    pT = ctx.enter_context(nc.psum_tensor("at_T", [P, BANK], F32))
    po = ctx.enter_context(nc.psum_tensor("at_o", [P, BANK], F32))
    qk_in = [sem(f"at_qk_in{i}") for i in range(2)]
    v_in = [sem(f"at_v_in{i}") for i in range(2)]
    names = ("consts", "s_done", "top_done", "ntop_done", "exp_done", "inv_done", "p_done",
             "t_done", "pt_done", "pv_done", "o_hi", "o_done", "sp_passed", "pool_passed", "pe_passed")
    (consts, s_done, top_done, ntop_done, exp_done, inv_done, p_done,
     t_done, pt_done, pv_done, o_hi, o_done, sp_passed, pool_passed, pe_passed) = (sem("at_" + n) for n in names)

    STEPS = [(h, c) for h in range(2) for c in range(2)]
    KBS = [list(range(QB)) + [NB], list(range(NB)) + [NB]]
    BEFORE = [0, QB + 1]
    PER_HEAD = QB + 1 + NB + 1
    SCREDIT, VCREDIT = 2 * NB, 2 * PER_HEAD

    def first_q(c, kb):
        return max(0, kb - QB * c) if kb < NB else 0

    def krows(kb):
        return META if kb == NB else P

    def pt_index(hp, h, c, n):
        return 2 * PER_HEAD * hp + (PER_HEAD * h + BEFORE[c] + n)

    def schedule(hp, prev, score, turn_block, finish):
        for st, (h, c) in enumerate(STEPS):
            ph, pc = STEPS[st - 1]
            php = hp if st else prev
            blocks = list(enumerate(KBS[pc])) if php is not None else []
            cut = len(blocks) // 2
            score(hp, h, c, 0)
            score(hp, h, c, 1)
            for n, kb in blocks[:cut]:
                turn_block(php, ph, pc, n, kb)
            score(hp, h, c, 2)
            score(hp, h, c, 3)
            for n, kb in blocks[cut:]:
                turn_block(php, ph, pc, n, kb)
            if blocks:
                finish(php, ph, pc)

    def last_step(score, turn_block, finish):
        for n, kb in enumerate(KBS[1]):
            turn_block(H // 2 - 1, 1, 1, n, kb)
        finish(H // 2 - 1, 1, 1)

    def blk(hp, h, c, j):
        return 16 * hp + (8 * h + QB * c + j)

    def run(eng, *work):
        schedule(0, None, *work)
        with eng.Fori(1, H // 2) as hp:
            schedule(hp, hp - 1, *work)
        last_step(*work)

    with nc.Block() as block:
        @block.sync
        def _(sp):
            with sp.Fori(0, H // 2) as hp:
                for h in range(2):
                    gate(sp, s_done, 2 * NB * hp + (NB * (h - 1) + SCREDIT), sp_passed)
                    sp.dma_start(q_sb[h][:], io["qT"][bass.ds(2 * hp + h, 1)].rearrange("a d t -> (a d) t"))\
                      .then_inc(qk_in[h], 16)
                    sp.dma_start(k_sb[h][:], io["kT"][bass.ds(2 * hp + h, 1)].rearrange("a d t -> (a d) t"))\
                      .then_inc(qk_in[h], 16)
                    gate(sp, pv_done, 2 * PER_HEAD * hp + (PER_HEAD * (h - 1) + VCREDIT), sp_passed)
                    v = io["v"][:, bass.ds(hp * P + h * HD, HD)]
                    sp.dma_start(v_sb[h][:, 0:NB, :], v[0:SEQ].rearrange("(b p) d -> p b d", p=P))\
                      .then_inc(v_in[h], 16)
                    sp.dma_start(v_sb[h][0:META, NB, :], v[SEQ:L]).then_inc(v_in[h], 16)

        @block.gpsimd
        def _(pool):
            pool.memset(eye[:], 0.0).then_inc(consts, 1)
            pool.memset(mask[:], 0.0).then_inc(consts, 1)
            pool.wait_ge(consts, 2)
            pool.affine_select(out=eye[:], in_=eye[:], compare_op=ALU.not_equal, fill=1.0, base=0,
                               pattern=[[-1, P]], channel_multiplier=1).then_inc(consts, 1)
            pool.affine_select(out=mask[:], in_=mask[:], compare_op=ALU.is_ge, fill=NEG, base=0,
                               pattern=[[-1, P]], channel_multiplier=1).then_inc(consts, 1)

            def normalise(hp, h, c, j):
                n = P * (QB * c + j + 1) + META
                slot = QB * c + j
                gate(pool, inv_done, blk(hp, h, c, j) + 1, pool_passed)
                pool.tensor_scalar(probs[:, slot, 0:n], probs[:, slot, 0:n], inv[:, slot:slot + 1], 1.0,
                                   ALU.mult, ALU.mult).then_inc(p_done, 1)

            with pool.Fori(0, H // 2) as hp:
                for h, c in STEPS:
                    for j in range(QB):
                        normalise(hp, h, c, j)

        def evacuate(eng, hp, h, c, n, kb):
            cols = slice(P * first_q(c, kb), BANK)
            index = pt_index(hp, h, c, n)
            slot = (BEFORE[c] + n) % 2
            eng.wait_ge(t_done, index + 1)
            eng.wait_ge(pv_done, index + (VCREDIT - 1))
            dst, src = pt_sb[slot][0:krows(kb), cols], pT[0:krows(kb), cols]
            if slot == 0:
                eng.activation(dst, src, ACT.Copy).then_inc(pt_done, 1)
            else:
                eng.tensor_copy(dst, src).then_inc(pt_done, 1)

        def out_of(a, hp, h, c):
            return a[h * HD:(h + 1) * HD, bass.ds(hp, 1), c * BANK:(c + 1) * BANK]

        @block.scalar
        def _(act):
            def exp(hp, h, c, j):
                n = P * (QB * c + j + 1) + META
                slot, b = QB * c + j, blk(hp, h, c, j)
                if j == 0 and (h or not isinstance(hp, int)):
                    act.wait_ge(t_done, pt_index(hp, h - 1, c, len(KBS[c])))
                act.wait_ge(ntop_done, b + 1)
                act.activation(probs[:, slot, 0:n], ps[j % 2][:, 0:n], ACT.Exp, bias=ntop[:, slot:slot + 1],
                               accum_out=rsum[:, slot:slot + 1]).then_inc(exp_done, 1)

            def turn_block(hp, h, c, n, kb):
                if (BEFORE[c] + n) % 2 == 0:
                    evacuate(act, hp, h, c, n, kb)

            def finish(hp, h, c):
                act.wait_ge(pv_done, pt_index(hp, h, c, len(KBS[c])) + VCREDIT)
                act.activation(out_of(a_hi, hp, h, c), po[h * HD:(h + 1) * HD, :].unsqueeze(1), ACT.Copy).then_inc(o_hi, 1)

            act.sem_inc(exp_done, 2)
            run(act, exp, turn_block, finish)

        @block.vector
        def _(dve):
            dve.sem_inc(pt_done, 1)
            dve.sem_inc(o_done, 1)

            def recip(hp, h, c, j):
                slot = QB * c + j
                dve.wait_ge(exp_done, blk(hp, h, c, j) + 3)
                dve.reciprocal(inv[:, slot:slot + 1], rsum[:, slot:slot + 1]).then_inc(inv_done, 1)

            def maximum(hp, h, c, j):
                n = P * (QB * c + j + 1) + META
                slot, b = QB * c + j, blk(hp, h, c, j)
                dve.wait_ge(s_done, b + (SCREDIT + 1))
                dve.tensor_reduce(top[:, slot:slot + 1], ps[j % 2][:, 0:n], AX.X, ALU.max).then_inc(top_done, 1)
                dve.wait_ge(top_done, b + 1)
                dve.tensor_scalar(ntop[:, slot:slot + 1], top[:, slot:slot + 1], -1.0, None,
                                  ALU.mult).then_inc(ntop_done, 1)
                if j % 2:
                    recip(hp, h, c, j - 1)
                    recip(hp, h, c, j)

            def turn_block(hp, h, c, n, kb):
                if (BEFORE[c] + n) % 2 == 1:
                    evacuate(dve, hp, h, c, n, kb)

            def finish(hp, h, c):
                dve.wait_ge(o_hi, 4 * hp + (2 * h + c + 1))
                dve.tensor_tensor(out_of(a_lo, hp, h, c), po[h * HD:(h + 1) * HD, :].unsqueeze(1),
                                  f32(out_of(a_hi, hp, h, c)), ALU.subtract).then_inc(o_done, 1)

            run(dve, maximum, turn_block, finish)

        @block.tensor
        def _(pe):
            pe.sem_inc(s_done, SCREDIT)
            pe.sem_inc(pv_done, VCREDIT)
            pe.wait_ge(consts, 4)

            def score(hp, h, c, j):
                i = QB * c + j
                n = P * (i + 1)
                s = ps[j % 2]
                if j == 0 and c == 0:
                    pe.wait_ge(qk_in[h], 32 * hp + 32)
                pe.wait_ge(exp_done, blk(hp, h, c, j) + 1)
                qi = q_sb[h][:, i * P:(i + 1) * P]
                for a in range(0, n, BANK):
                    b = min(n, a + BANK)
                    pe.matmul(s[:, a:b], qi, k_sb[h][:, a:b], start=True, stop=(b < n))
                pe.matmul(s[:, n - P:n], eye[:], mask[:], start=False, stop=True)
                last = pe.matmul(s[:, n:n + META], qi, k_sb[h][:, SEQ:L], start=True, stop=True)
                last.then_inc(s_done, 1)

            def turn_block(hp, h, c, n, kb):
                index = pt_index(hp, h, c, n)
                r, j0 = krows(kb), first_q(c, kb)
                slot = (BEFORE[c] + n) % 2
                pe.wait_ge(pt_done, index + 1)
                for j in range(j0, QB):
                    if n == 0:
                        pe.wait_ge(p_done, blk(hp, h, c, j) + 1)
                    i = QB * c + j
                    col = kb * P if kb < NB else P * (i + 1)
                    last = pe.transpose(pT[0:r, j * P:(j + 1) * P], probs[:, i, col:col + r], ident[:])
                last.then_inc(t_done, 1)
                pe.wait_ge(pt_done, index + 2)
                if n == 0:
                    pe.wait_ge(o_done, 4 * hp + (2 * h + c + 1))
                    if c == 0:
                        pe.wait_ge(v_in[h], 32 * hp + 32)
                if r < P:
                    pe.sem_inc(pe_passed, 1)
                cols = slice(P * j0, BANK)
                pe.matmul(po[h * HD:(h + 1) * HD, cols], v_sb[h][0:r, kb, :], pt_sb[slot][0:r, cols],
                          start=(n == 0), stop=(n == len(KBS[c]) - 1)).then_inc(pv_done, 1)

            def finish(hp, h, c):
                pass

            run(pe, score, turn_block, finish)


def merge(nc, mem, sem, ctx, io, aT, mT):
    m_hi, m_lo = mT
    base = 65536
    ring = WeightUnits(mem, sem, "mg", base, 2)
    base += 2 * 12288
    part = [mem.at(f"mg_part{i}", base + 4096 * i, [P, SEQ]) for i in range(2)]
    sgb = [mem.at(f"mg_sgb{i}", base + 8192 + 4096 * i, [P, SEQ]) for i in range(2)]
    gated = mem.at("mg_gated", base + 16384, [P, SEQ])
    merged = mem.at("mg_merged", base + 20480, [P, SEQ])
    out = [ctx.enter_context(nc.psum_tensor(f"mg_o{i}", [P, SEQ], F32)) for i in range(2)]
    tiles_in = [sem(f"mg_tiles_in{i}") for i in range(2)]
    read, merged_done, hi_done, lo_done = (sem("mg_" + s) for s in ("read", "merged_done", "hi", "lo"))
    halves = [slice(0, BANK), slice(BANK, SEQ)]

    with nc.Block() as block:
        @block.sync
        def _(sp):
            with sp.Fori(0, KT // 2) as i:
                for u in range(2):
                    m = 2 * i + u
                    ring.load(sp, io["w_att_out"][0][:, bass.ds(m * P, P)], m, u)
                    gate(sp, merged_done, m + 1, ring.passed)
                    for dst, src in ((part[u], io["part"]), (sgb[u], io["sgb"])):
                        sp.dma_start(dst[:], src[bass.ds(m, 1)].rearrange("a p t -> p (a t)"))\
                          .then_inc(tiles_in[u], 16)

        @block.scalar
        def _(act):
            def merged_hi(m):
                act.wait_ge(merged_done, m + 3)
                act.activation(m_hi[:, bass.ds(m, 1), :], merged[:].unsqueeze(1), ACT.Copy).then_inc(hi_done, 1)

            ring.split_hi(act, 0, 0, 0)
            with act.Fori(0, KT // 2 - 1) as i:
                for u in range(2):
                    ring.split_hi(act, 2 * i + (u + 1), 1 - u, i + u)
                    merged_hi(2 * i + u)
            ring.split_hi(act, KT - 1, 1, KT // 2 - 1)
            merged_hi(KT - 2)
            merged_hi(KT - 1)

        @block.vector
        def _(dve):
            dve.sem_inc(ring.lo_done, 2)
            dve.sem_inc(merged_done, 2)

            def merged_lo(m, u, use):
                dve.wait_ge(ring.used, m + 3)
                dve.wait_ge(tiles_in[u], 32 * use + 32)
                dve.tensor_tensor(gated[:], out[u][:], sgb[u][:], ALU.mult).then_inc(read, 1)
                dve.wait_ge(read, m + 1)
                dve.tensor_tensor(merged[:], gated[:], part[u][:], ALU.add).then_inc(merged_done, 1)
                dve.wait_ge(hi_done, m + 1)
                dve.tensor_tensor(m_lo[:, bass.ds(m, 1), :], merged[:].unsqueeze(1),
                                  f32(m_hi[:, bass.ds(m, 1), :]), ALU.subtract).then_inc(lo_done, 1)

            ring.split_lo(dve, 0, 0)
            with dve.Fori(0, KT // 2 - 1) as i:
                for u in range(2):
                    ring.split_lo(dve, 2 * i + (u + 1), 1 - u)
                    merged_lo(2 * i + u, u, i)
            ring.split_lo(dve, KT - 1, 1)
            merged_lo(KT - 2, 0, KT // 2 - 1)
            merged_lo(KT - 1, 1, KT // 2 - 1)

        @block.tensor
        def _(pe):
            pe.sem_inc(ring.used, 2)
            with pe.Fori(0, KT // 2) as i:
                for u in range(2):
                    m = 2 * i + u
                    pe.wait_ge(merged_done, m + 1)
                    ring.product(pe, m, u, aT, [out[u][:, c] for c in halves], halves)


def residual(nc, mem, sem, ctx, io, mT, x2n, logits, retired):
    m_hi, m_lo = mT
    NR = NG + NE
    raw = mem.at("rs_raw", 0, [P, KT // 4, D])
    w_hi = mem.at("rs_whi", 8192, [P, KT, D], F32R)
    w_lo = mem.at("rs_wlo", 40960, [P, KT, D], F32R)
    base = 106496
    x_sb = [mem.at(f"rs_x{i}", base + 4096 * i, [P, D]) for i in range(2)]
    g_b = mem.at("rs_g", base + 8192, [P, D])
    t_hi = mem.at("rs_thi", base + 12288, [P, KT, P], F32R)
    t_lo = mem.at("rs_tlo", base + 16384, [P, KT, P], F32R)
    sq = mem.at("rs_sq", base + 20480, [P, D])
    base += 24576
    wr = mem.at("rs_wr", base, [P, KT, NR])
    wr_hi = mem.at("rs_wrhi", base + 1152, [P, KT, NR], F32R)
    wr_lo = mem.at("rs_wrlo", base + 2304, [P, KT, NR], F32R)
    br = mem.at("rs_br", base + 3456, [P, NR])
    stat = mem.at("rs_stat", base + 3648, [P, 8])
    ident = io["ident"]
    py = [ctx.enter_context(nc.psum_tensor(f"rs_y{i}", [P, D], F32)) for i in range(2)]
    pT = ctx.enter_context(nc.psum_tensor("rs_T", [P, KT, P], F32))
    pl = ctx.enter_context(nc.psum_tensor("rs_l", [P, BANK], F32))
    names = ("raw_in", "consts_in", "whi", "wlo", "y_done", "x2_done", "squared", "rms", "recip", "xn_done",
             "turned", "t_hi", "t_lo", "logits_mm", "logits_done", "x2_stored", "wr_hi", "wr_lo")
    (raw_in, consts_in, whi, wlo, y_done, x2_done, squared, rms, recip, xn_done,
     turned, thi_done, tlo_done, logits_mm, logits_done, x2_stored, wrhi_done, wrlo_done) = (
        sem("rs_" + n) for n in names)
    x_in = [sem(f"rs_x_in{i}") for i in range(2)]
    x_blocks = io["x"].rearrange("b (t p) d -> (b t) p d", p=P)
    w_o = io["w_merge_out"][0].rearrange("(k p) c -> p k c", p=P)

    with nc.Block() as block:
        @block.sync
        def _(sp):
            for q in range(4):
                if q:
                    sp.wait_ge(wlo, 2 * q)
                sp.dma_start(raw[:], w_o[:, 2 * q:2 * q + 2, :]).then_inc(raw_in, 16)
                if q == 0:
                    sp.dma_start(wr[:, :, 0:NG], io["w_router_group"][0].rearrange("(k p) c -> p k c", p=P)).then_inc(consts_in, 16)
                    sp.dma_start(wr[:, :, NG:NR], io["w_router_expert"][0].rearrange("(k p) c -> p k c", p=P)).then_inc(consts_in, 16)
                    sp.dma_start(br[:, 0:NG], io["b_router_group"].partition_broadcast(P)).then_inc(consts_in, 16)
                    sp.dma_start(br[:, NG:NR], io["b_router_expert"].partition_broadcast(P)).then_inc(consts_in, 16)
                    sp.dma_start(g_b[:], io["norm2_g"].partition_broadcast(P)).then_inc(consts_in, 16)
            for t in range(NB):
                if t >= 2:
                    sp.wait_ge(x2_stored, 16 * (t - 1))
                    sp.wait_ge(xn_done, t - 1)
                sp.dma_start(x_sb[t % 2][:], x_blocks[t]).then_inc(x_in[t % 2], 16)

        @block.gpsimd
        def _(pool):
            for s in retired:
                pool.sem_clear(s)
            for t in range(NB):
                pool.wait_ge(x2_done, 2 * t + 2)
                pool.dma_start(io["x2"][t * P:(t + 1) * P, :], x_sb[t % 2][:]).then_inc(x2_stored, 16)
                pool.wait_ge(x2_stored, 16 * t + 16)

        @block.scalar
        def _(act):
            for k in range(KT):
                if k % 2 == 0:
                    act.wait_ge(raw_in, 8 * k + 16)
                act.activation(w_hi[:, k, :], raw[:, k % 2, :], ACT.Copy).then_inc(whi, 1)
            act.wait_ge(consts_in, 80)
            act.activation(wr_hi[:], wr[:], ACT.Copy).then_inc(wrhi_done, 1)

            def front(t):
                act.wait_ge(x2_done, 2 * t + 2)
                act.activation(sq[:], x_sb[t % 2][:], ACT.Square, accum_out=stat[:, 0:1]).then_inc(squared, 1)
                act.wait_ge(squared, t + 1)
                act.activation(stat[:, 2:3], stat[:, 0:1], ACT.Sqrt, scale=1.0 / D,
                               bias=io["eps"][:]).then_inc(rms, 1)

            def back(t):
                act.wait_ge(turned, t + 1)
                if t:
                    act.wait_ge(logits_mm, t)
                act.activation(t_hi[:], pT[:], ACT.Copy).then_inc(thi_done, 1)

            front(0)
            for t in range(1, NB):
                front(t)
                back(t - 1)
            back(NB - 1)

        @block.vector
        def _(dve):
            for k in range(KT):
                dve.wait_ge(whi, k + 1)
                dve.tensor_tensor(w_lo[:, k, :], raw[:, k % 2, :], f32(w_hi[:, k, :]), ALU.subtract).then_inc(wlo, 1)
            dve.wait_ge(wrhi_done, 1)
            dve.tensor_tensor(wr_lo[:], wr[:], f32(wr_hi[:]), ALU.subtract).then_inc(wrlo_done, 1)

            def front(t):
                dve.wait_ge(y_done, t + 1)
                dve.wait_ge(x_in[t % 2], 16 * (t // 2) + 16)
                for c in range(2):
                    cols = slice(c * BANK, (c + 1) * BANK)
                    dve.tensor_tensor(x_sb[t % 2][:, cols], py[t % 2][:, cols], x_sb[t % 2][:, cols],
                                      ALU.add).then_inc(x2_done, 1)
                dve.wait_ge(rms, t + 1)
                dve.reciprocal(stat[:, 4:5], stat[:, 2:3]).then_inc(recip, 1)
                dve.wait_ge(recip, t + 1)
                dve.scalar_tensor_tensor(out=x2n[:, t, :], in0=x_sb[t % 2][:], scalar=stat[:, 4:5], in1=g_b[:],
                                         op0=ALU.mult, op1=ALU.mult).then_inc(xn_done, 1)

            def back(t):
                dve.wait_ge(thi_done, t + 1)
                dve.tensor_tensor(t_lo[:], pT[:], f32(t_hi[:]), ALU.subtract).then_inc(tlo_done, 1)
                dve.wait_ge(logits_mm, t + 1)
                dve.tensor_tensor(logits[:, t, :], pl[:, 0:NR], br[:], ALU.add).then_inc(logits_done, 1)

            front(0)
            for t in range(1, NB):
                front(t)
                back(t - 1)
            back(NB - 1)

        @block.tensor
        def _(pe):
            def product(t):
                for k in range(KT):
                    if t == 0:
                        pe.wait_ge(wlo, k + 1)
                    elif k == 0 and t >= 2:
                        pe.wait_ge(x2_done, 2 * t - 2)
                    for c in range(2):
                        cols = slice(c * BANK, (c + 1) * BANK)
                        rows = slice(t * P, (t + 1) * P)
                        last = split3(pe, py[t % 2][:, cols], m_hi[:, k, rows], m_lo[:, k, rows],
                                      w_hi[:, k, cols], w_lo[:, k, cols], k == 0, k == KT - 1)
                last.then_inc(y_done, 1)

            def route(t):
                pe.wait_ge(xn_done, t + 1)
                if t:
                    pe.wait_ge(tlo_done, t)
                for k in range(KT):
                    last = pe.transpose(pT[:, k, :], x2n[:, t, k * P:(k + 1) * P], ident[:])
                last.then_inc(turned, 1)

            def score(t):
                pe.wait_ge(tlo_done, t + 1)
                if t:
                    pe.wait_ge(logits_done, t)
                else:
                    pe.wait_ge(wrlo_done, 1)
                for k in range(KT):
                    last = split3(pe, pl[:, 0:NR], t_hi[:, k, :], t_lo[:, k, :], wr_hi[:, k, :], wr_lo[:, k, :],
                                  k == 0, k == KT - 1)
                last.then_inc(logits_mm, 1)

            product(0)
            for t in range(1, NB):
                product(t)
                if t >= 2:
                    score(t - 2)
                route(t - 1)
            score(NB - 2)
            route(NB - 1)
            score(NB - 1)


def route(nc, mem, sem, ctx, io, x2n, logits, dest, weights, table):
    W = 2 ** 100
    offset = [0]

    def tile(name, *shape, dtype=F32):
        t = mem.at("rt_" + name, offset[0], [P, *shape], dtype)
        n = 4
        for d in shape:
            n *= d
        offset[0] += (n + 31) // 32 * 32
        return t

    jrev4, jrev32, j32 = tile("jrev4", NB, NG), tile("jrev32", NB, NE), tile("j32", NE)
    step128 = tile("step128", NB, NE)
    before, pidx, pidx128 = tile("before", P), tile("pidx", 1), tile("pidx128", 1)
    iot = tile("iot", NB, NE, dtype=I32)
    iot4, iotj, iot8, iotp = (tile("iot4", NB, NG, dtype=I32), tile("iotj", NE, dtype=I32),
                              tile("iot8", NB, NE, dtype=I32), tile("iotp", 1, dtype=I32))
    gmax, gsum, gsel = tile("gmax", NB), tile("gsum", NB), tile("gsel", NB)
    d4, e4, oh4, c4 = (tile(n, NB, NG) for n in ("d4", "e4", "oh4", "c4"))
    lem, lem2, d32, c32, oh1, oh2, both = (tile(n, NB, NE) for n in ("lem", "lem2", "d32", "c32", "oh1", "oh2", "both"))
    m1, m2, dm, em, sel, w1 = (tile(n, NB) for n in ("m1", "m2", "dm", "em", "sel", "w1"))
    tot, pos, hit = tile("tot", NB, NE), tile("pos", NB, NE), tile("hit", NB, NE)
    pre = tile("pre", NB + 1, NE)
    inc, start, nblk, bend, bst, lo, ind, rowv = (tile(n, NE) for n in ("inc", "start", "nblk", "bend", "bst", "lo", "ind", "rowv"))
    destf, tabf, tabi = tile("destf", 2, NB), tile("tabf", 4), tile("tabi", 4, dtype=I32)
    zero = tile("zero", D)
    ones = io["onesp"]
    p_rank = ctx.enter_context(nc.psum_tensor("rt_rank", [P, BANK], F32))
    p_tot = ctx.enter_context(nc.psum_tensor("rt_tot", [P, BANK], F32))
    names = ("chain", "consts", "iotas", "d4_done", "e4_done", "dm_done", "em_done", "both_done", "ranked", "dest_done", "tab_done",
             "tab_stored", "tab_in", "scattered", "zeroed")
    (chain, consts, iotas, d4_done, e4_done, dm_done, em_done, both_done, ranked, dest_done, tab_done,
     tab_stored, tab_in, scattered, zeroed) = (sem("rt_" + n) for n in names)
    lg, le = logits[:, :, 0:NG], logits[:, :, NG:NG + NE]

    def wide(ap, n):
        return ap.unsqueeze(2).to_broadcast([P, ap.shape[1], n])

    with nc.Block() as block:
        @block.sync
        def _(sp):
            sp.wait_ge(iotas, 7)
            sp.dma_start(io["xs"][SLOTS:XROWS, :], zero[:]).then_inc(zeroed, 16)
            sp.wait_ge(tab_done, 1)
            sp.dma_start(io["tab"], tabi[:]).then_inc(tab_stored, 16)
            sp.wait_ge(tab_stored, 16)
            sp.dma_start(table[:], io["tab"].rearrange("(o p) c -> o (p c)", o=1)).then_inc(tab_in, 16)
            sp.wait_ge(tab_in, 16)
            sp.wait_ge(zeroed, 16)

        @block.gpsimd
        def _(pool):
            pool.iota(iot[:], pattern=[[0, NB], [-1, NE]], base=NE, channel_multiplier=0).then_inc(iotas, 1)
            pool.iota(iot4[:], pattern=[[0, NB], [-1, NG]], base=NG, channel_multiplier=0).then_inc(iotas, 1)
            pool.iota(iotj[:], pattern=[[1, NE]], base=0, channel_multiplier=0).then_inc(iotas, 1)
            pool.iota(iot8[:], pattern=[[P, NB], [0, NE]], base=0, channel_multiplier=0).then_inc(iotas, 1)
            pool.iota(iotp[:], pattern=[[0, 1]], base=0, channel_multiplier=1).then_inc(iotas, 1)
            pool.memset(zero[:], 0.0).then_inc(iotas, 1)
            pool.memset(before[:], 1.0).then_inc(consts, 1)
            pool.wait_ge(consts, 1)
            pool.affine_select(out=before[:], in_=before[:], compare_op=ALU.is_gt, fill=0.0, base=0,
                               pattern=[[1, P]], channel_multiplier=-1).then_inc(iotas, 1)
            pool.wait_ge(dest_done, 1)
            for b in range(NB):
                for c in range(2):
                    pool.indirect_dma_start(io["xs"], bass.IndirectOffsetOnAxis(ap=dest[:, c, b:b + 1], axis=0),
                                            x2n[:, b, :], None).then_inc(scattered, 16)
            pool.wait_ge(scattered, 16 * 2 * NB)

        @block.scalar
        def _(act):
            act.wait_ge(d4_done, 1)
            act.activation(e4[:], d4[:], ACT.Exp).then_inc(e4_done, 1)
            act.wait_ge(dm_done, 1)
            act.activation(em[:], dm[:], ACT.Exp).then_inc(em_done, 1)

        @block.vector
        def _(dve):
            count = [0]

            def link(ins):
                count[0] += 1
                ins.then_inc(chain, 1)
                dve.wait_ge(chain, count[0])

            dve.wait_ge(iotas, 7)
            for dst, src in ((jrev32, iot), (jrev4, iot4), (j32, iotj), (step128, iot8), (pidx, iotp)):
                link(dve.tensor_copy(dst[:], src[:]))
            link(dve.tensor_scalar(pidx128[:], pidx[:], float(P), None, ALU.mult))
            link(dve.tensor_reduce(gmax[:], lg, AX.X, ALU.max))
            dve.tensor_tensor(d4[:], lg, wide(gmax[:], NG), ALU.subtract).then_inc(d4_done, 1)
            dve.wait_ge(d4_done, 1)
            link(dve.scalar_tensor_tensor(out=c4[:], in0=d4[:], scalar=0.0, in1=jrev4[:], op0=ALU.is_ge, op1=ALU.mult))
            link(dve.tensor_reduce(gsel[:], c4[:], AX.X, ALU.max))
            link(dve.tensor_tensor(oh4[:], jrev4[:], wide(gsel[:], NG), ALU.is_equal))
            link(dve.tensor_scalar(oh4[:], oh4[:], -1.0, float(W), ALU.add, ALU.mult))
            link(dve.tensor_copy(lem[:], le))
            link(dve.tensor_tensor(lem[:].rearrange("p b (g e) -> p (b g) e", g=NG),
                                   lem[:].rearrange("p b (g e) -> p (b g) e", g=NG),
                                   wide(oh4[:].rearrange("p b g -> p (b g)"), EPG), ALU.add))

            def pick(logit, top, onehot):
                link(dve.tensor_reduce(top[:], logit[:], AX.X, ALU.max))
                link(dve.tensor_tensor(d32[:], logit[:], wide(top[:], NE), ALU.subtract))
                link(dve.scalar_tensor_tensor(out=c32[:], in0=d32[:], scalar=0.0, in1=jrev32[:],
                                              op0=ALU.is_ge, op1=ALU.mult))
                link(dve.tensor_reduce(sel[:], c32[:], AX.X, ALU.max))
                link(dve.tensor_tensor(onehot[:], jrev32[:], wide(sel[:], NE), ALU.is_equal))

            pick(lem, m1, oh1)
            link(dve.scalar_tensor_tensor(out=lem2[:], in0=oh1[:], scalar=-2.0 * W, in1=lem[:],
                                          op0=ALU.mult, op1=ALU.add))
            pick(lem2, m2, oh2)
            dve.tensor_tensor(dm[:], m2[:], m1[:], ALU.subtract).then_inc(dm_done, 1)
            dve.tensor_tensor(both[:], oh1[:], oh2[:], ALU.add).then_inc(both_done, 1)
            dve.wait_ge(e4_done, 1)
            link(dve.tensor_reduce(gsum[:], e4[:], AX.X, ALU.add))
            dve.wait_ge(em_done, 1)
            link(dve.scalar_tensor_tensor(out=w1[:], in0=em[:], scalar=1.0, in1=gsum[:], op0=ALU.add, op1=ALU.mult))
            link(dve.reciprocal(weights[:, 0, :], w1[:]))
            link(dve.tensor_tensor(weights[:, 1, :], weights[:, 0, :], em[:], ALU.mult))
            dve.wait_ge(ranked, 1)
            link(dve.tensor_copy(tot[:], p_tot[:, 0:NB * NE].rearrange("p (b e) -> p b e", b=NB)))
            link(dve.memset(pre[:, 0, :], 0.0))
            for b in range(NB):
                link(dve.tensor_tensor(pre[:, b + 1, :], pre[:, b, :], tot[:, b, :], ALU.add))
            total = pre[:, NB, :]
            link(dve.tensor_tensor_scan(inc[:], ones[:, 0:NE], total, 0.0, ALU.mult, ALU.add))
            link(dve.tensor_tensor(start[:], inc[:], total, ALU.subtract))
            link(dve.tensor_tensor(pos[:], p_rank[:, 0:NB * NE].rearrange("p (b e) -> p b e", b=NB),
                                   pre[:, 0:NB, :], ALU.add))
            link(dve.tensor_tensor(pos[:], pos[:], start[:].unsqueeze(1).to_broadcast([P, NB, NE]), ALU.add))
            for c, oh in enumerate((oh1, oh2)):
                link(dve.tensor_tensor(hit[:], oh[:], pos[:], ALU.mult))
                link(dve.tensor_reduce(destf[:, c, :], hit[:], AX.X, ALU.add))
            dve.tensor_copy(dest[:], destf[:]).then_inc(dest_done, 1)
            link(dve.tensor_tensor(hit[:], total.unsqueeze(1).to_broadcast([P, NB, NE]), step128[:], ALU.is_gt))
            link(dve.tensor_reduce(nblk[:], hit[:].rearrange("p b e -> p e b"), AX.X, ALU.add))
            link(dve.tensor_tensor_scan(bend[:], ones[:, 0:NE], nblk[:], 0.0, ALU.mult, ALU.add))
            link(dve.tensor_tensor(bst[:], bend[:], nblk[:], ALU.subtract))
            link(dve.tensor_scalar(lo[:], bst[:], pidx[:], None, ALU.is_le))
            link(dve.scalar_tensor_tensor(out=ind[:], in0=bend[:], scalar=pidx[:], in1=lo[:],
                                          op0=ALU.is_gt, op1=ALU.mult))
            link(dve.scalar_tensor_tensor(out=rowv[:], in0=bst[:], scalar=-float(P), in1=start[:],
                                          op0=ALU.mult, op1=ALU.add))
            link(dve.scalar_tensor_tensor(out=rowv[:], in0=rowv[:], scalar=pidx128[:], in1=ind[:],
                                          op0=ALU.add, op1=ALU.mult))
            link(dve.tensor_reduce(tabf[:, 1:2], rowv[:], AX.X, ALU.add))
            link(dve.tensor_tensor(lo[:], ind[:], j32[:], ALU.mult))
            link(dve.tensor_reduce(tabf[:, 0:1], lo[:], AX.X, ALU.add))
            link(dve.tensor_scalar(tabf[:, 2:3], bend[:, NE - 1:NE], -2.0, None, ALU.add))
            link(dve.tensor_copy(tabf[:, 3:4], pidx[:]))
            dve.tensor_copy(tabi[:], tabf[:]).then_inc(tab_done, 1)

        @block.tensor
        def _(pe):
            pe.wait_ge(both_done, 1)
            rhs = both[:].rearrange("p b e -> p (b e)")
            pe.matmul(p_rank[:, 0:NB * NE], before[:], rhs, start=True, stop=True)
            pe.matmul(p_tot[:, 0:NB * NE], ones[:, 0:P], rhs, start=True, stop=True).then_inc(ranked, 1)


def experts(nc, mem, sem, ctx, io, table):
    HALF = KT // 2 * DE
    base = 0
    raw, w_hi, w_lo = [], [], []
    for i in range(6):
        raw.append(mem.at(f"ex_raw{i}", base, [P, HALF]))
        base += 4 * HALF
    for dst, name in ((w_hi, "whi"), (w_lo, "wlo")):
        for i in range(3):
            dst.append(mem.at(f"ex_{name}{i}", base, [P, 2 * HALF], F32R))
            base += 8 * HALF
    x_sb = mem.at("ex_x", base, [P, D])
    x_hi = mem.at("ex_xhi", base + 4096, [P, KT, P], F32R)
    x_lo = mem.at("ex_xlo", base + 8192, [P, KT, P], F32R)
    h_hi = mem.at("ex_hhi", base + 12288, [P, KE, P], F32R)
    h_lo = mem.at("ex_hlo", base + 14336, [P, KE, P], F32R)
    act_g = mem.at("ex_silu", base + 16384, [P, DE])
    h_sb = mem.at("ex_h", base + 18432, [P, DE])
    y_sb = mem.at("ex_y", base + 20480, [P, D])
    ident = io["ident"]
    p_gate, p_up = (ctx.enter_context(nc.psum_tensor("ex_p" + n, [P, DE], F32)) for n in ("gate", "up"))
    p_y = ctx.enter_context(nc.psum_tensor("ex_py", [P, D], F32))
    p_xT = ctx.enter_context(nc.psum_tensor("ex_pxT", [P, KT, P], F32))
    p_hT = ctx.enter_context(nc.psum_tensor("ex_phT", [P, KE, P], F32))
    raw_in = [sem(f"ex_raw_in{i}") for i in range(6)]
    names = ("x_in", "whi", "wlo", "gate_done", "up_done", "down_done", "x_turned", "x_hi", "x_lo", "silu_done",
             "h_done", "h_turned", "h_hi", "h_lo", "y0_done", "y1_done", "stored", "y_free", "passed", "pool_passed")
    (x_in, whi, wlo, gate_done, up_done, down_done, x_turned, xhi_done, xlo_done, silu_done,
     h_done, h_turned, hhi_done, hlo_done, y0_done, y1_done, stored, y_free, passed, pool_passed) = (
        sem("ex_" + n) for n in names)
    GATE, UP, DOWN = 0, 1, 2
    products = ((GATE, gate_done), (UP, up_done), (DOWN, down_done))

    def order(unit, b, last=False):
        if unit != DOWN and isinstance(b, int) and b == 0:
            return 2 * unit
        return 6 * b + (4 if last else (-2, 0, 8)[unit])

    def entry(eng, b, column, most):
        at = slice(4 * b + column, 4 * b + column + 1) if isinstance(b, int) else bass.ds(4 * b + column, 1)
        return eng.value_load(table[0:1, at], min_val=0, max_val=most)

    def blocks(eng):
        return eng.value_load(table[0:1, 2:3], min_val=SLOTS // P - 2, max_val=MAXBLK - 2) + 2

    with nc.Block() as block:
        @block.sync
        def _(sp):
            def load_x(b):
                row = entry(sp, b, 1, SLOTS)
                if not (isinstance(b, int) and b == 0):
                    gate(sp, x_turned, b, passed)
                sp.dma_start(x_sb[:], io["xs"][bass.ds(row, P), :]).then_inc(x_in, 16)

            def load(unit, b, e):
                for s in range(2):
                    if not (isinstance(b, int) and b == 0):
                        before = order(unit, 0) if isinstance(b, int) and b == 1 else order(unit, b - 1)
                        gate(sp, wlo, before + s + 1, passed)
                    w = io[("w_exp_gate", "w_exp_up", "w_exp_down")[unit]][0][bass.ds(e, 1)]
                    w = w.rearrange("o (s k p) c -> s p (o k) c", s=2, p=P)[s]
                    dst = raw[2 * unit + s][:].rearrange("p (k c) -> p k c", c=D if unit == DOWN else DE)
                    sp.dma_start(dst, w).then_inc(raw_in[2 * unit + s], 16)

            n = blocks(sp)
            load_x(0)
            e = entry(sp, 0, 0, NE - 1)
            load(GATE, 0, e)
            load(UP, 0, e)
            load_x(1)

            def step(b):
                e = entry(sp, b, 0, NE - 1)
                load(GATE, b, e)
                load(UP, b, e)
                load_x(b + 1)
                load(DOWN, b - 1, entry(sp, b - 1, 0, NE - 1))

            step(1)
            with sp.Fori(2, n) as b:
                step(b)
            load(DOWN, n - 1, entry(sp, n - 1, 0, NE - 1))

        @block.gpsimd
        def _(pool):
            pool.sem_inc(y_free, 1)
            n = blocks(pool)
            with pool.Fori(0, n) as b:
                row = entry(pool, b, 1, SLOTS)
                gate(pool, y0_done, b + 1, pool_passed)
                gate(pool, y1_done, b + 1, pool_passed)
                pool.dma_start(io["ys"][bass.ds(row, P), :], y_sb[:]).then_inc(stored, 16)
                pool.wait_ge(stored, 16 * b + 16)
                pool.sem_inc(y_free, 1)

        @block.scalar
        def _(act):
            def split(unit, b, first=False):
                done = products[unit][1]
                for s in range(2):
                    act.wait_ge(raw_in[2 * unit + s], 16 * b + 16)
                    if s == 0 and not first:
                        act.wait_ge(done, b)
                    act.activation(w_hi[unit][:, s * HALF:(s + 1) * HALF], raw[2 * unit + s][:],
                                   ACT.Copy).then_inc(whi, 1)

            def x_split(b):
                act.wait_ge(x_turned, b + 1)
                act.activation(x_hi[:], p_xT[:], ACT.Copy).then_inc(xhi_done, 1)

            def y_out(b):
                act.wait_ge(down_done, b + 1)
                act.wait_ge(y_free, b + 1)
                act.activation(y_sb[:, 0:BANK], p_y[:, 0:BANK], ACT.Copy).then_inc(y0_done, 1)

            def silu(b, first=False):
                act.wait_ge(gate_done, b + 1)
                if not first:
                    act.wait_ge(h_done, b)
                act.activation(act_g[:], p_gate[:], ACT.Silu).then_inc(silu_done, 1)

            n = blocks(act)
            x_split(0)
            split(GATE, 0, first=True)
            split(UP, 0, first=True)
            silu(0, first=True)
            x_split(1)

            def step(b, first=False):
                split(GATE, b)
                if not first:
                    y_out(b - 2)
                split(UP, b)
                act.wait_ge(h_turned, b)
                act.activation(h_hi[:], p_hT[:], ACT.Copy).then_inc(hhi_done, 1)
                silu(b)
                split(DOWN, b - 1, first)
                x_split(b + 1)

            step(1, first=True)
            with act.Fori(2, n) as b:
                step(b)
            y_out(n - 2)
            act.wait_ge(h_turned, n)
            act.activation(h_hi[:], p_hT[:], ACT.Copy).then_inc(hhi_done, 1)
            split(DOWN, n - 1)
            y_out(n - 1)

        @block.vector
        def _(dve):
            def split(unit, b, last=False):
                for s in range(2):
                    dve.wait_ge(whi, order(unit, b, last) + (s + 1))
                    cols = slice(s * HALF, (s + 1) * HALF)
                    dve.tensor_tensor(w_lo[unit][:, cols], raw[2 * unit + s][:], f32(w_hi[unit][:, cols]),
                                      ALU.subtract).then_inc(wlo, 1)

            def x_split(b):
                dve.wait_ge(xhi_done, b + 1)
                dve.tensor_tensor(x_lo[:], p_xT[:], f32(x_hi[:]), ALU.subtract).then_inc(xlo_done, 1)

            def h_split(b):
                dve.wait_ge(hhi_done, b + 1)
                dve.tensor_tensor(h_lo[:], p_hT[:], f32(h_hi[:]), ALU.subtract).then_inc(hlo_done, 1)

            def hidden(b, first=False):
                dve.wait_ge(silu_done, b + 1)
                dve.wait_ge(up_done, b + 1)
                if not first:
                    dve.wait_ge(h_turned, b)
                dve.tensor_tensor(h_sb[:], p_up[:], act_g[:], ALU.mult).then_inc(h_done, 1)

            def y_out(b):
                dve.wait_ge(down_done, b + 1)
                dve.wait_ge(y_free, b + 1)
                dve.tensor_copy(y_sb[:, BANK:D], p_y[:, BANK:D]).then_inc(y1_done, 1)

            n = blocks(dve)
            x_split(0)
            split(GATE, 0)
            split(UP, 0)
            x_split(1)

            def step(b, first=False):
                hidden(b - 1, first)
                split(GATE, b)
                if not first:
                    y_out(b - 2)
                split(UP, b)
                h_split(b - 1)
                split(DOWN, b - 1)
                x_split(b + 1)

            step(1, first=True)
            with dve.Fori(2, n) as b:
                step(b)
            hidden(n - 1)
            y_out(n - 2)
            h_split(n - 1)
            split(DOWN, n - 1, last=True)
            y_out(n - 1)

        @block.tensor
        def _(pe):
            def product(unit, b, x, outs, final=False):
                kt = KE if unit == DOWN else KT
                for k in range(kt):
                    if k % (kt // 2) == 0:
                        pe.wait_ge(wlo, order(unit, b, final) + (2 * k // kt + 1))
                    for i, out in enumerate(outs):
                        cols = slice((k * len(outs) + i) * BANK, (k * len(outs) + i + 1) * BANK)
                        last = split3(pe, out, x[0][:, k, :], x[1][:, k, :], w_hi[unit][:, cols], w_lo[unit][:, cols],
                                      k == 0, k == kt - 1)
                last.then_inc(products[unit][1], 1)

            def turn_x(b):
                pe.wait_ge(x_in, 16 * b + 16)
                if not (isinstance(b, int) and b == 0):
                    pe.wait_ge(xlo_done, b)
                for k in range(KT):
                    last = pe.transpose(p_xT[:, k, :], x_sb[:, k * P:(k + 1) * P], ident[:])
                last.then_inc(x_turned, 1)

            def turn_h(b):
                pe.wait_ge(h_done, b + 1)
                for k in range(KE):
                    last = pe.transpose(p_hT[:, k, :], h_sb[:, k * P:(k + 1) * P], ident[:])
                last.then_inc(h_turned, 1)

            def gate_product(b):
                pe.wait_ge(xlo_done, b + 1)
                if not (isinstance(b, int) and b == 0):
                    pe.wait_ge(silu_done, b)
                product(GATE, b, (x_hi, x_lo), [p_gate[:]])

            def down_product(b, first=False, final=False):
                pe.wait_ge(hlo_done, b + 1)
                if not first:
                    pe.wait_ge(y0_done, b)
                    pe.wait_ge(y1_done, b)
                product(DOWN, b, (h_hi, h_lo), [p_y[:, 0:BANK], p_y[:, BANK:D]], final)

            n = blocks(pe)
            turn_x(0)
            gate_product(0)
            product(UP, 0, (x_hi, x_lo), [p_up[:]])
            turn_x(1)

            def step(b, first=False):
                gate_product(b)
                turn_h(b - 1)
                product(UP, b, (x_hi, x_lo), [p_up[:]])
                turn_x(b + 1)
                down_product(b - 1, first)

            step(1, first=True)
            with pe.Fori(2, n) as b:
                step(b)
            turn_h(n - 1)
            down_product(n - 1, final=True)


def combine(nc, mem, sem, ctx, io, dest, weights):
    x2 = mem.at("cb_x2", 0, [P, NB, D])
    y = [mem.at(f"cb_y{c}", 32768 * (c + 1), [P, NB, D]) for c in range(2)]
    x2_in, y_in, half_done, done, out_stored = (sem("cb_" + n) for n in ("x2_in", "y_in", "half", "done", "out_stored"))

    with nc.Block() as block:
        @block.sync
        def _(sp):
            sp.dma_start(x2[:], io["x2"].rearrange("(b p) d -> p b d", p=P)).then_inc(x2_in, 16)
            for b in range(NB):
                sp.wait_ge(done, b + 1)
                sp.dma_start(io["out"][0][b * P:(b + 1) * P, :], x2[:, b, :]).then_inc(out_stored, 16)
            sp.wait_ge(out_stored, 16 * NB)

        @block.gpsimd
        def _(pool):
            for b in range(NB):
                for c in range(2):
                    pool.indirect_dma_start(y[c][:, b, :], None, io["ys"][0:SLOTS, :],
                                            bass.IndirectOffsetOnAxis(ap=dest[:, c, b:b + 1], axis=0)).then_inc(y_in, 16)

        @block.vector
        def _(dve):
            dve.wait_ge(x2_in, 16)
            dve.wait_ge(y_in, 32 * NB)
            for b in range(NB):
                dve.scalar_tensor_tensor(out=x2[:, b, :], in0=y[0][:, b, :], scalar=weights[:, 0, b:b + 1],
                                         in1=x2[:, b, :], op0=ALU.mult, op1=ALU.add).then_inc(half_done, 1)
                dve.wait_ge(half_done, b + 1)
                dve.scalar_tensor_tensor(out=x2[:, b, :], in0=y[1][:, b, :], scalar=weights[:, 1, b:b + 1],
                                         in1=x2[:, b, :], op0=ALU.mult, op1=ALU.add).then_inc(done, 1)


def program(nc, io, upto=99):
    mem = Memory(nc)
    scratch = dict(qT=[H, HD + 2, SEQ], kT=[H, HD + 2, L], v=[L, D], part=[KT, P, SEQ], sgb=[KT, P, SEQ],
                   x2=[SEQ, D], xs=[XROWS, D], ys=[XROWS, D])
    io["tab"] = nc.dram_tensor("tab_scratch", [P, 4], I32).ap()
    for name, shape in scratch.items():
        io[name] = nc.dram_tensor(name + "_scratch", shape, F32).ap()
    with ExitStack() as ctx:
        retired = ExitStack()
        first = []

        def sem(name):
            return ctx.enter_context(nc.semaphore(name))

        def early_sem(name):
            if name.endswith("stored"):
                return sem(name)
            first.append(retired.enter_context(nc.semaphore(name)))
            return first[-1]

        io["ident"] = mem.at("ident", mem.size - 512, [P, P])
        io["eps"] = mem.at("eps", mem.size - 576, [P, 1])
        io["one"] = mem.at("one", mem.size - 544, [P, 1])
        io["onesp"] = mem.at("onesp", mem.size - 576 - 4160, [P, L])
        h_hi = mem.at("h_hi", 0, [P, KT, L], F32R)
        h_lo = mem.at("h_lo", 33280, [P, KT, L], F32R)
        with ExitStack() as c:
            norm1(nc, mem, early_sem, c, io, (h_hi, h_lo))
        if upto < 1:
            return
        c_hi = mem.at("c_hi", 66560, [P, KT, SEQ], F32R)
        c_lo = mem.at("c_lo", 99328, [P, KT, SEQ], F32R)
        with ExitStack() as c:
            conv_merge(nc, mem, early_sem, c, io, (h_hi, h_lo), (c_hi, c_lo))
        if upto < 2:
            return
        with ExitStack() as c:
            qkv(nc, mem, sem, c, io, (h_hi, h_lo))
        if upto < 3:
            return
        a_hi = mem.at("a_hi", 0, [P, KT, SEQ], F32R)
        a_lo = mem.at("a_lo", 32768, [P, KT, SEQ], F32R)
        with ExitStack() as c:
            attention(nc, mem, sem, c, io, (a_hi, a_lo))
        if upto < 4:
            return
        m_hi = mem.at("m_hi", 142336, [P, KT, SEQ], F32R)
        m_lo = mem.at("m_lo", 175104, [P, KT, SEQ], F32R)
        with ExitStack() as c:
            merge(nc, mem, sem, c, io, (a_hi, a_lo), (m_hi, m_lo))
        if upto < 5:
            return
        x2n = mem.at("x2n", 73728, [P, NB, D])
        logits = mem.at("logits", 140800, [P, NB, NG + NE])
        with ExitStack() as c:
            residual(nc, mem, sem, c, io, (m_hi, m_lo), x2n, logits, first)
        retired.close()
        if upto < 6:
            return
        dest = mem.at("dest", 207872, [P, 2, NB], I32)
        weights = mem.at("weights", 207936, [P, 2, NB])
        table = mem.at("table", 205824, [1, 4 * P], I32)
        with ExitStack() as c:
            route(nc, mem, sem, c, io, x2n, logits, dest, weights, table)
        if upto < 7:
            return
        with ExitStack() as c:
            experts(nc, mem, sem, c, io, table)
        if upto < 8:
            return
        with ExitStack() as c:
            combine(nc, mem, sem, c, io, dest, weights)


_INS = ['x', 'meta_tokens', 'norm1_g', 'w_in', 'b_forget', 'conv_w', 'w_conv_out', 'q_norm_g', 'k_norm_g',
        'w_att_out', 'w_merge_out', 'norm2_g', 'w_router_group', 'b_router_group', 'w_router_expert',
        'b_router_expert', 'w_exp_gate', 'w_exp_up', 'w_exp_down']


def kernel(**inputs):
    import numpy as _np
    import concourse.bacc as _bacc
    from concourse import mybir as _mybir
    from concourse.bass_utils import run_bass_kernel_spmd as _run

    nc = _bacc.Bacc("TRN2", target_bir_lowering=False, num_devices=1)
    arrays, io = {}, {}
    for name in _INS:
        a = _np.ascontiguousarray(inputs[name])
        arrays[f"in_{name}_dram"] = a
        io[name] = nc.dram_tensor(f"in_{name}_dram", a.shape, _mybir.dt.from_np(a.dtype), kind="ExternalInput").ap()
    io["out"] = nc.dram_tensor("out_0_dram", (1, 1024, 1024), F32, kind="ExternalOutput").ap()
    program(nc, io)
    r = _run(nc, [arrays], core_ids=[0])
    return r.results[0]["out_0_dram"]
```

```python
from contextlib import ExitStack

import concourse.bass as bass
from concourse import mybir

F32 = mybir.dt.float32
F32R = mybir.dt.float32r
BF16 = mybir.dt.bfloat16
I32 = mybir.dt.int32
ALU = mybir.AluOpType
ACT = mybir.ActivationFunctionType
AX = mybir.AxisListType

P = 128
BANK = 512
D = 1024
KT = D // P
SEQ = 1024
NB = SEQ // P
META = 16
L = SEQ + META
H, HD = 16, 64
NG, EPG = 4, 8
NE = NG * EPG
DE = 512
KE = DE // P
EPS = 1e-6
SLOTS = 2 * SEQ
XROWS = SLOTS + P
MAXBLK = SLOTS // P + NE - 1
NEG = -float(2 ** 100)
COL = dict(B=0, C=D, U=2 * D, Q=3 * D, K=4 * D, V=5 * D, F=6 * D, GA=6 * D + H, GB=7 * D + H)


class Memory:

    def __init__(self, nc):
        self.nc = nc
        self.base = (nc.sbuf_base + 63) // 64 * 64
        self.size = nc.sbuf_top - self.base

    def at(self, name, offset, shape, dtype=F32):
        n = 4
        for s in shape[1:]:
            n *= s
        if dtype == BF16:
            n //= 2
        assert offset + n <= self.size, (name, offset + n, self.size)
        return self.nc.alloc_sbuf_tensor_at(name, shape, dtype, offset=self.base + offset)


def f32(ap):
    return ap.bitcast(F32)


def gate(eng, sem, value, passed):
    eng.wait_ge(sem, value)
    eng.sem_inc(passed, 1)


def split3(eng, out, w_hi, w_lo, x_hi, x_lo, start, stop):
    eng.matmul(out, w_lo, x_hi, start=start, stop=False)
    eng.matmul(out, w_hi, x_lo, start=False, stop=False)
    return eng.matmul(out, w_hi, x_hi, start=False, stop=stop)


def norm1(nc, mem, sem, ctx, io, hT):
    h_hi, h_lo = hT
    base = 66560
    x_sb = [mem.at(f"n1_x{i}", base + 4096 * i, [P, D]) for i in range(2)]
    xn = [mem.at(f"n1_xn{i}", base + 8192 + 4096 * i, [P, D]) for i in range(2)]
    g_b = mem.at("n1_g", base + 16384, [P, D])
    sq = mem.at("n1_sq", base + 20480, [P, D])
    stat = mem.at("n1_stat", base + 24576, [P, 8])
    epsc = io["eps"]
    ident = io["ident"]
    pT = [ctx.enter_context(nc.psum_tensor(f"n1_T{i}", [P, KT, P], F32)) for i in range(2)]
    x_in = [sem(f"n1_x_in{i}") for i in range(2)]
    g_in, consts = sem("n1_g_in"), sem("n1_consts")
    squared, rms, recip, xn_done, turned, hi_done, lo_done = (
        sem("n1_" + s) for s in ("squared", "rms", "recip", "xn_done", "turned", "hi", "lo"))
    x_blocks = io["x"].rearrange("b (t p) d -> (b t) p d", p=P)

    def rows(n):
        return META if isinstance(n, int) and n == NB else P

    def hcols(n, r):
        return slice(SEQ, L) if r == META else bass.ds(n * P, P)

    with nc.Block() as block:
        @block.sync
        def _(sp):
            sp.dma_start(g_b[:], io["norm1_g"].partition_broadcast(P)).then_inc(g_in, 16)

            def load(n, s):
                r = rows(n)
                sp.wait_ge(xn_done, n + 1)
                src = io["meta_tokens"] if r == META else x_blocks[bass.ds(n, 1)].rearrange("a p d -> p (a d)")
                sp.dma_start(x_sb[s][0:r, :], src).then_inc(x_in[s], 16)

            load(0, 0)
            with sp.Fori(0, 3) as i:
                load(2 * i + 1, 1)
                load(2 * i + 2, 0)
            load(7, 1)
            load(8, 0)

        @block.gpsimd
        def _(pool):
            pool.memset(ident[:], 0.0).then_inc(consts, 1)
            pool.memset(io["onesp"][:], 1.0)
            pool.memset(io["one"][:], 1.0)
            pool.memset(epsc[:], EPS).then_inc(consts, 1)
            pool.wait_ge(consts, 2)
            pool.affine_select(out=ident[:], in_=ident[:], compare_op=ALU.not_equal, fill=1.0,
                               base=0, pattern=[[-1, P]], channel_multiplier=1).then_inc(consts, 1)

        @block.scalar
        def _(act):
            def front(n, s):
                r = rows(n)
                act.wait_ge(x_in[s], 16 * ((n + 2 - s) // 2) if isinstance(n, int) else 8 * (n - s) + 16)
                act.activation(sq[0:r, :], x_sb[s][0:r, :], ACT.Square,
                               accum_out=stat[0:r, s:s + 1]).then_inc(squared, 1)
                act.wait_ge(squared, n + 1)
                act.wait_ge(recip, n + 1)
                act.activation(stat[0:r, 2 + s:3 + s], stat[0:r, s:s + 1], ACT.Sqrt,
                               scale=1.0 / D, bias=epsc[0:r, :]).then_inc(rms, 1)

            def back(n, s):
                r = rows(n)
                act.wait_ge(turned, n + 3)
                act.activation(h_hi[:, :, hcols(n, r)], pT[s][:, :, 0:r], ACT.Copy).then_inc(hi_done, 1)

            act.wait_ge(consts, 2)
            front(0, 0)
            with act.Fori(0, 3) as i:
                front(2 * i + 1, 1)
                back(2 * i, 0)
                front(2 * i + 2, 0)
                back(2 * i + 1, 1)
            front(7, 1)
            back(6, 0)
            front(8, 0)
            back(7, 1)
            back(8, 0)

        @block.vector
        def _(dve):
            dve.sem_inc(xn_done, 2)
            dve.sem_inc(recip, 2)
            dve.sem_inc(lo_done, 2)

            def front(n, s):
                r = rows(n)
                dve.wait_ge(rms, n + 1)
                dve.reciprocal(stat[0:r, 4 + s:5 + s], stat[0:r, 2 + s:3 + s]).then_inc(recip, 1)
                dve.wait_ge(recip, n + 3)
                dve.wait_ge(turned, n + 1)
                dve.scalar_tensor_tensor(out=xn[s][0:r, :], in0=x_sb[s][0:r, :],
                                         scalar=stat[0:r, 4 + s:5 + s], in1=g_b[0:r, :],
                                         op0=ALU.mult, op1=ALU.mult).then_inc(xn_done, 1)

            def back(n, s):
                r = rows(n)
                dve.wait_ge(hi_done, n + 1)
                dve.tensor_tensor(h_lo[:, :, hcols(n, r)], pT[s][:, :, 0:r],
                                  f32(h_hi[:, :, hcols(n, r)]), ALU.subtract).then_inc(lo_done, 1)

            dve.wait_ge(g_in, 16)
            front(0, 0)
            with dve.Fori(0, 3) as i:
                front(2 * i + 1, 1)
                back(2 * i, 0)
                front(2 * i + 2, 0)
                back(2 * i + 1, 1)
            front(7, 1)
            back(6, 0)
            front(8, 0)
            back(7, 1)
            back(8, 0)

        @block.tensor
        def _(pe):
            pe.sem_inc(turned, 2)
            pe.wait_ge(consts, 3)

            def turn(n, s):
                r = rows(n)
                pe.wait_ge(xn_done, n + 3)
                pe.wait_ge(lo_done, n + 1)
                for k in range(KT):
                    last = pe.transpose(pT[s][:, k, 0:r], xn[s][0:r, k * P:(k + 1) * P], ident[0:r, 0:r])
                last.then_inc(turned, 1)

            turn(0, 0)
            with pe.Fori(0, 3) as i:
                turn(2 * i + 1, 1)
                turn(2 * i + 2, 0)
            turn(7, 1)
            turn(8, 0)


class WeightUnits:

    def __init__(self, mem, sem, name, base, slots):
        self.slots = slots
        self.raw = [mem.at(f"{name}_raw{i}", base + 4096 * i, [P, KT, P]) for i in range(slots)]
        base += 4096 * slots
        self.hi = [mem.at(f"{name}_whi{i}", base + 4096 * i, [P, KT, P], F32R) for i in range(slots)]
        base += 4096 * slots
        self.lo = [mem.at(f"{name}_wlo{i}", base + 4096 * i, [P, KT, P], F32R) for i in range(slots)]
        self.raw_in = [sem(f"{name}_raw_in{i}") for i in range(slots)]
        self.hi_done, self.lo_done, self.used, self.passed = (
            sem(f"{name}_{s}") for s in ("whi", "wlo", "wused", "passed"))

    def load(self, sp, source, n, s):
        gate(sp, self.lo_done, n + 1, self.passed)
        sp.dma_start(self.raw[s][:], source.rearrange("(k p) c -> p k c", p=P)).then_inc(self.raw_in[s], 16)

    def split_hi(self, act, n, s, use):
        act.wait_ge(self.raw_in[s], 16 * use + 16)
        act.wait_ge(self.used, n + 1)
        act.activation(self.hi[s][:], self.raw[s][:], ACT.Copy).then_inc(self.hi_done, 1)

    def split_lo(self, dve, n, s):
        dve.wait_ge(self.hi_done, n + 1)
        dve.tensor_tensor(self.lo[s][:], self.raw[s][:], f32(self.hi[s][:]),
                          ALU.subtract).then_inc(self.lo_done, 1)

    def product(self, pe, n, s, x, outs, cols):
        pe.wait_ge(self.lo_done, n + 1 + self.slots)
        last = None
        for k in range(KT):
            for step, (w, y) in enumerate(((self.lo, x[0]), (self.hi, x[1]), (self.hi, x[0]))):
                for out, c in zip(outs, cols):
                    last = pe.matmul(out, w[s][:, k, :], y[:, k, c], start=(k == 0 and step == 0),
                                     stop=(k == KT - 1 and step == 2))
        last.then_inc(self.used, 1)


def conv_merge(nc, mem, sem, ctx, io, hT, cT):
    h_hi, h_lo = hT
    conv_hi_sb, conv_lo_sb = cT
    base = 132096
    ring = WeightUnits(mem, sem, "cm", base, 3)
    base += 3 * 12288
    forget = WeightUnits(mem, sem, "cf", base, 1)
    c_sb = mem.at("cm_c", base, [P, SEQ + 2])
    z = mem.at("cm_z", base + 4160, [P, SEQ + 2])
    y0 = mem.at("cm_y0", base + 8320, [P, SEQ])
    y1 = mem.at("cm_y1", base + 12416, [P, SEQ])
    cv = mem.at("cm_cv", base + 16512, [P, SEQ])
    sga, part, sgb = c_sb, y0, y1
    fx = mem.at("cm_fx", base + 20608, [H, L])
    fa = mem.at("cm_fa", base + 24768, [H, L])
    cw = mem.at("cm_cw", base + 28928, [P, KT, 3])
    bf = mem.at("cm_bf", base + 29024, [H, 1])
    c_hi = mem.at("cm_fhi", base + 29056, [H, L], F32R)
    c_lo = mem.at("cm_flo", base + 33216, [H, L], F32R)
    ones = io["onesp"]
    out = [ctx.enter_context(nc.psum_tensor(f"cm_o{i}", [P, SEQ], F32)) for i in range(3)]
    mt = [ctx.enter_context(nc.psum_tensor(f"cm_m{i}", [P, BANK], F32)) for i in range(2)]
    halves = [slice(0, BANK), slice(BANK, SEQ)]
    out_of = [[o[:, c] for c in halves] for o in out]
    consts_in = sem("cm_consts")
    evac = [sem(f"cm_evac{i}") for i in range(3)]
    y0_done, y1_done, conv_hi, conv_lo, fchain, f_out, stored = (
        sem("cm_" + s) for s in ("y0", "y1", "conv_hi", "conv_lo", "fchain", "f_out", "stored"))
    sgb_done, part_done, part_stored, sgb_stored, passed, part_free, sgb_free = (
        sem("cm_" + s) for s in ("sgb", "part", "part_stored", "sgb_stored", "pool_passed", "part_free", "sgb_free"))
    w_in, w_conv = io["w_in"][0], io["w_conv_out"][0]

    with nc.Block() as block:
        @block.sync
        def _(sp):
            with nc.allow_non_contiguous_dma(reason="small tables, one element each"):
                sp.dma_start(bf[:], io["b_forget"].rearrange("o h -> h o")).then_inc(consts_in, 16)
                for i in range(3):
                    sp.dma_start(cw[:, :, i], io["conv_w"][0, i].rearrange("(m p) -> p m", p=P)).then_inc(consts_in, 16)
            forget.load(sp, w_in[:, COL["F"]:COL["F"] + P], 0, 0)
            with sp.Fori(0, KT) as m:
                for s, first in enumerate((COL["C"], COL["U"], COL["B"])):
                    ring.load(sp, w_in[:, bass.ds(m * P + first, P)], 3 * m + s, s)
            with sp.Fori(0, KT) as m:
                ring.load(sp, w_in[:, bass.ds(m * P + COL["GA"], P)], 3 * m + 24, 0)
                ring.load(sp, w_conv[:, bass.ds(m * P, P)], 3 * m + 25, 1)
                ring.load(sp, w_in[:, bass.ds(m * P + COL["GB"], P)], 3 * m + 26, 2)

        @block.gpsimd
        def _(pool):
            pool.wait_ge(fchain, 10)
            one_rows = ones[0:H, :].bitcast(F32R)
            for r, c in enumerate((c_hi, c_lo)):
                pool.dma_start(io["qb"][:, HD + r, :], c[:, 0:SEQ]).then_inc(stored, 16)
                pool.dma_start(io["qb"][:, HD + 2 + r, :], one_rows[:, 0:SEQ]).then_inc(stored, 16)
                pool.dma_start(io["kb"][:, HD + r, :], one_rows).then_inc(stored, 16)
            for r, c in enumerate((fa, fx)):
                c = c[:].bitcast(F32R)
                pool.dma_start(io["kb"][:, HD + 2 + r, 0:META], c[:, SEQ:L]).then_inc(stored, 16)
                pool.dma_start(io["kb"][:, HD + 2 + r, META:L], c[:, 0:SEQ]).then_inc(stored, 16)
            with pool.Fori(0, KT) as m:
                gate(pool, part_done, m + 2, passed)
                pool.dma_start(io["part"][bass.ds(m, 1)].rearrange("a p t -> p (a t)"), part[:]).then_inc(part_stored, 16)
                gate(pool, sgb_done, m + 2, passed)
                pool.dma_start(io["sgb"][bass.ds(m, 1)].rearrange("a p t -> p (a t)"), sgb[:]).then_inc(sgb_stored, 16)
                pool.wait_ge(part_stored, 16 * m + 16)
                pool.sem_inc(part_free, 1)
                pool.wait_ge(sgb_stored, 16 * m + 16)
                pool.sem_inc(sgb_free, 1)
            pool.wait_ge(stored, 160)

        @block.scalar
        def _(act):
            act.wait_ge(forget.raw_in[0], 16)
            forget.split_hi(act, 0, 0, 0)
            ring.split_hi(act, 0, 0, 0)
            ring.split_hi(act, 1, 1, 0)
            act.wait_ge(fchain, 1)
            act.activation(fa[:], fa[:], ACT.Exp, scale=-1.0).then_inc(fchain, 1)
            act.wait_ge(fchain, 2)
            act.activation(fa[:], fa[:], ACT.Ln, bias=io["one"][0:H, :]).then_inc(fchain, 1)
            act.sem_inc(sgb_free, 1)
            act.sem_inc(sgb_done, 1)
            act.wait_ge(consts_in, 64)

            with act.Fori(0, KT) as m:
                ring.split_hi(act, 3 * m + 2, 2, m)
                act.wait_ge(ring.used, 3 * m + 4)
                act.wait_ge(evac[1], m + 1)
                act.activation(c_sb[:, 0:2], mt[0][:, 0:2], ACT.Copy)
                act.activation(c_sb[:, 2:], out[0][:], ACT.Copy).then_inc(evac[0], 1)
                ring.split_hi(act, 3 * m + 3, 0, m + 1)
                act.wait_ge(evac[1], m + 2)
                act.activation(y0[:], z[:, 0:SEQ], ACT.Copy,
                               scale=cw[:, bass.ds(m, 1), 0]).then_inc(y0_done, 1)
                ring.split_hi(act, 3 * m + 4, 1, m + 1)
                act.wait_ge(evac[2], m + 2)
                act.activation(conv_hi_sb[:, bass.ds(m, 1), :], cv[:], ACT.Copy).then_inc(conv_hi, 1)

            def gates(m, more):
                ring.split_hi(act, 3 * m + 26, 2, m + 8)
                act.wait_ge(ring.used, 3 * m + 28)
                act.wait_ge(evac[1], m + 9)
                act.activation(sga[:, 0:SEQ], out[0][:], ACT.Sigmoid).then_inc(evac[0], 1)
                if more:
                    ring.split_hi(act, 3 * m + 27, 0, m + 9)
                    ring.split_hi(act, 3 * m + 28, 1, m + 9)
                act.wait_ge(ring.used, 3 * m + 30)
                act.wait_ge(sgb_free, m + 1)
                act.activation(sgb[:], out[2][:], ACT.Sigmoid).then_inc(sgb_done, 1)

            with act.Fori(0, KT - 1) as m:
                gates(m, True)
            gates(KT - 1, False)

        @block.vector
        def _(dve):
            dve.sem_inc(forget.lo_done, 1)
            dve.sem_inc(ring.lo_done, 3)
            dve.sem_inc(evac[0], 1)
            dve.sem_inc(evac[1], 1)
            dve.sem_inc(part_free, 1)
            dve.sem_inc(part_done, 1)
            forget.split_lo(dve, 0, 0)
            ring.split_lo(dve, 0, 0)
            ring.split_lo(dve, 1, 1)
            dve.wait_ge(forget.used, 2)
            dve.wait_ge(consts_in, 64)
            dve.tensor_scalar(fx[:, SEQ:L], mt[1][0:H, 0:META], bf[:], None, ALU.add)
            dve.tensor_scalar(fx[:, 0:SEQ], out[2][0:H, :], bf[:], None, ALU.add).then_inc(evac[2], 1)
            dve.wait_ge(evac[2], 1)
            dve.scalar_tensor_tensor(out=fa[:], in0=fx[:], scalar=-1.0, in1=fx[:],
                                     op0=ALU.mult, op1=ALU.max).then_inc(fchain, 1)
            dve.wait_ge(fchain, 3)
            dve.scalar_tensor_tensor(out=fx[:], in0=fx[:], scalar=0.0, in1=fa[:],
                                     op0=ALU.min, op1=ALU.subtract).then_inc(fchain, 1)
            dve.wait_ge(fchain, 4)
            dve.tensor_tensor_scan(fa[:, SEQ:L], ones[0:H, 0:META], fx[:, SEQ:L], 0.0,
                                   ALU.mult, ALU.add).then_inc(f_out, 1)
            dve.wait_ge(f_out, 1)
            dve.tensor_tensor_scan(fa[:, 0:SEQ], ones[0:H, 0:SEQ], fx[:, 0:SEQ], fa[:, L - 1:L],
                                   ALU.mult, ALU.add).then_inc(fchain, 1)
            dve.wait_ge(fchain, 5)
            dve.tensor_copy(c_hi[:], fa[:]).then_inc(fchain, 1)
            dve.wait_ge(fchain, 6)
            dve.tensor_tensor(c_lo[:], fa[:], f32(c_hi[:]), ALU.subtract).then_inc(fchain, 1)
            dve.wait_ge(fchain, 7)
            dve.sem_inc(fchain, 1)
            dve.tensor_scalar(fa[:].bitcast(F32R), f32(c_hi[:]), -1.0, None, ALU.mult).then_inc(fchain, 1)
            dve.tensor_scalar(fx[:].bitcast(F32R), f32(c_lo[:]), -1.0, None, ALU.mult).then_inc(fchain, 1)

            with dve.Fori(0, KT) as m:
                ring.split_lo(dve, 3 * m + 2, 2)
                ring.split_lo(dve, 3 * m + 3, 0)
                dve.wait_ge(ring.used, 3 * m + 5)
                dve.wait_ge(evac[0], m + 2)
                dve.tensor_tensor(z[:, 0:2], mt[1][:, 0:2], c_sb[:, 0:2], ALU.mult)
                dve.tensor_tensor(z[:, 2:], out[1][:], c_sb[:, 2:], ALU.mult).then_inc(evac[1], 1)
                dve.wait_ge(evac[1], m + 2)
                dve.wait_ge(y0_done, m + 1)
                dve.scalar_tensor_tensor(out=y1[:], in0=z[:, 1:SEQ + 1], scalar=cw[:, bass.ds(m, 1), 1],
                                         in1=y0[:], op0=ALU.mult, op1=ALU.add).then_inc(y1_done, 1)
                dve.wait_ge(y1_done, 2 * m + 1)
                dve.scalar_tensor_tensor(out=y1[:], in0=z[:, 2:SEQ + 2], scalar=cw[:, bass.ds(m, 1), 2],
                                         in1=y1[:], op0=ALU.mult, op1=ALU.add).then_inc(y1_done, 1)
                ring.split_lo(dve, 3 * m + 4, 1)
                dve.wait_ge(y1_done, 2 * m + 2)
                dve.wait_ge(ring.used, 3 * m + 6)
                dve.tensor_tensor(cv[:], out[2][:], y1[:], ALU.mult).then_inc(evac[2], 1)
                dve.wait_ge(conv_hi, m + 1)
                dve.tensor_tensor(conv_lo_sb[:, bass.ds(m, 1), :], cv[:], f32(conv_hi_sb[:, bass.ds(m, 1), :]),
                                  ALU.subtract).then_inc(conv_lo, 1)

            def gated(m, more):
                ring.split_lo(dve, 3 * m + 26, 2)
                if more:
                    ring.split_lo(dve, 3 * m + 27, 0)
                dve.wait_ge(ring.used, 3 * m + 29)
                dve.wait_ge(evac[0], m + 10)
                dve.wait_ge(part_free, m + 1)
                dve.tensor_tensor(part[:], out[1][:], sga[:, 0:SEQ], ALU.mult).then_inc(part_done, 1)
                dve.wait_ge(part_done, m + 2)
                dve.sem_inc(evac[1], 1)
                if more:
                    ring.split_lo(dve, 3 * m + 28, 1)

            with dve.Fori(0, KT - 1) as m:
                gated(m, True)
            gated(KT - 1, False)

        @block.tensor
        def _(pe):
            pe.sem_inc(forget.used, 1)
            pe.sem_inc(ring.used, 3)
            meta2 = slice(L - 2, L)
            forget.product(pe, 0, 0, hT, [out[2][:, c] for c in halves] + [mt[1][:, 0:META]],
                           halves + [slice(SEQ, L)])
            with pe.Fori(0, KT) as m:
                pe.wait_ge(evac[0], m + 1)
                ring.product(pe, 3 * m, 0, hT, out_of[0] + [mt[0][:, 0:2]], halves + [meta2])
                pe.wait_ge(evac[1], m + 1)
                pe.wait_ge(evac[2], m + 1)
                ring.product(pe, 3 * m + 1, 1, hT, out_of[1] + [mt[1][:, 0:2]], halves + [meta2])
                ring.product(pe, 3 * m + 2, 2, hT, out_of[2], halves)
            pe.wait_ge(conv_lo, KT)
            with pe.Fori(0, KT) as m:
                pe.wait_ge(evac[0], m + 9)
                ring.product(pe, 3 * m + 24, 0, hT, out_of[0], halves)
                pe.wait_ge(evac[1], m + 9)
                ring.product(pe, 3 * m + 25, 1, cT, out_of[1], halves)
                pe.wait_ge(evac[2], 9)
                pe.wait_ge(sgb_done, m + 1)
                ring.product(pe, 3 * m + 26, 2, hT, out_of[2], halves)


def qkv(nc, mem, sem, ctx, io, hT):
    h_hi, h_lo = hT
    HPC = BANK // HD
    CT = BANK // P
    base = 66560
    raw = [mem.at(f"qk_raw{i}", base + 8192 * i, [P, KT // 2, BANK]) for i in range(2)]
    w_hi = mem.at("qk_whi", base + 16384, [P, KT, BANK], F32R)
    w_lo = mem.at("qk_wlo", base + 32768, [P, KT, BANK], F32R)
    base += 49152
    t_hi = mem.at("qk_thi", base, [P, 2, CT, L], F32R)
    t_lo = mem.at("qk_tlo", base + 33280, [P, 2, CT, L], F32R)
    base += 66560
    qn = [mem.at(f"qk_qn{i}", base + 2048 * i, [P, BANK]) for i in range(3)]
    v_sb = [mem.at(f"qk_v{i}", base + 6144 + 2048 * i, [P, BANK]) for i in range(3)]
    sq = mem.at("qk_sq", base + 12288, [P, BANK])
    ss = mem.at("qk_ss", base + 14336, [P, HPC])
    rms = mem.at("qk_rms", base + 14400, [P, HPC])
    rstd = mem.at("qk_rstd", base + 14464, [P, HPC])
    gain = mem.at("qk_gain", base + 14528, [P, 4])
    ident = io["ident"]
    mm = [ctx.enter_context(nc.psum_tensor(f"qk_mm{i}", [P, BANK], F32)) for i in range(3)]
    pT = [ctx.enter_context(nc.psum_tensor(f"qk_T{i}", [P, CT, P], F32)) for i in range(3)]
    raw_in = [sem(f"qk_raw_in{i}") for i in range(2)]
    names = ("whi", "wlo", "w_used", "sp_passed", "pool_passed", "mm_done", "sq_done", "summed", "rms_done",
             "rstd_done", "freed", "turned", "t_hi_done", "evac", "gains_in", "gains", "stored", "v_done", "pe_passed")
    (whi, wlo, w_used, sp_passed, pool_passed, mm_done, sq_done, summed, rms_done,
     rstd_done, freed, turned, t_hi_done, evac, gains_in, gains, stored, v_done, pe_passed) = (sem("qk_" + n) for n in names)
    v_stored = [sem(f"qk_v_stored{i}") for i in range(3)]
    v_free = sem("qk_v_free")
    w_cols = io["w_in"][0].rearrange("(k p) c -> p k c", p=P)

    PASSES = dict(q=(0, 0, NB), k=(2, 2 * NB, NB + 1), v=(4, 2 * NB + 2 * (NB + 1), NB + 1))

    def rows(t):
        return META if t == NB else P

    def toks(t):
        return slice(t * P, t * P + rows(t))

    def turned_cols(tile, c, t, gcol):
        first = t * P if gcol == 2 else META + t * P if t < NB else 0
        return tile[:, bass.ds(c, 1), :, first:first + rows(t)].rearrange("p a ct t -> p (a ct) t")

    with nc.Block() as block:
        @block.sync
        def _(sp):
            with nc.allow_non_contiguous_dma(reason="64-element gain columns"):
                for c, g in enumerate(("q_norm_g", "k_norm_g")):
                    for h in range(2):
                        sp.dma_start(gain[h * HD:(h + 1) * HD, c:c + 1],
                                     io[g].rearrange("o d -> d o")).then_inc(gains_in, 16)
            for c0, first in ((0, "Q"), (2, "K"), (4, "V")):
                with sp.Fori(0, 2) as c:
                    for half in range(2):
                        gate(sp, wlo, 8 * c + (8 * c0 + 4 * half + 4), sp_passed)
                        sp.dma_start(raw[half][:], w_cols[:, 4 * half:4 * half + 4,
                                                          bass.ds(c * BANK + COL[first], BANK)])\
                          .then_inc(raw_in[half], 16)

        @block.gpsimd
        def _(pool):
            for name in ("q", "k"):
                n0, g0, blocks = PASSES[name]
                width = SEQ if name == "q" else L
                with pool.Fori(0, 2) as c:
                    gate(pool, evac, blocks * c + (g0 + blocks + 2), pool_passed)
                    places = ((("qa", 0, t_hi), ("qa", HD, t_lo), ("qb", 0, t_hi)) if name == "q" else
                              (("ka", 0, t_hi), ("kb", 0, t_lo)))
                    for part, row, tile in places:
                        heads = io[part][:, row:row + HD, :].rearrange("(c ct h) d t -> h c d ct t", c=2, h=2)
                        for h in range(2):
                            pool.dma_start(heads[h, bass.ds(c, 1)].rearrange("a d ct t -> (a d) ct t"),
                                           tile[h * HD:(h + 1) * HD, bass.ds(c, 1), :, 0:width]
                                           .rearrange("p a ct t -> p (a ct) t")).then_inc(stored, 16)
                pool.wait_ge(stored, 192 if name == "q" else 320)
                pool.sem_inc(v_free, 1)
            for c in range(2):
                for t in range(NB + 1):
                    u = 9 * c + t
                    pool.wait_ge(v_done, u + 1)
                    pool.dma_start(io["v"][toks(t), c * BANK:(c + 1) * BANK],
                                   v_sb[t % 3][0:rows(t), :]).then_inc(v_stored[t % 3], 16)
                    if u >= 1:
                        pool.wait_ge(v_stored[(t - 1) % 3], 16 * (3 * ((u - 1) // 9) + ((u - 1) % 9) // 3 + 1))
                        pool.sem_inc(v_free, 1)
            pool.wait_ge(v_stored[2], 96)

        def split_hi(act, n, blocks_before):
            for k in range(KT):
                if k % 4 == 0:
                    act.wait_ge(raw_in[k // 4], 16 * n + 16)
                if k < KT - 1:
                    act.wait_ge(w_used, 7 * n + (k + 1))
                elif blocks_before is not None:
                    act.wait_ge(mm_done, blocks_before)
                act.activation(w_hi[:, k, :], raw[k // 4][:, k % 4, :], ACT.Copy).then_inc(whi, 1)

        def split_lo(dve, n):
            for k in range(KT):
                dve.wait_ge(whi, 8 * n + (k + 1))
                dve.tensor_tensor(w_lo[:, k, :], raw[k // 4][:, k % 4, :], f32(w_hi[:, k, :]),
                                  ALU.subtract).then_inc(wlo, 1)

        @block.scalar
        def _(act):
            def front(g, t):
                r = rows(t)
                act.wait_ge(mm_done, g + (t + 1))
                act.wait_ge(summed, g + (t + 1))
                act.activation(sq[0:r, :], mm[t % 3][0:r, :], ACT.Square).then_inc(sq_done, 1)
                act.wait_ge(summed, g + (t + 2))
                act.activation(rms[0:r, :], ss[0:r, :], ACT.Sqrt, scale=1.0 / HD,
                               bias=io["eps"][0:r, :]).then_inc(rms_done, 1)

            def back(g, t, c, gcol):
                act.wait_ge(turned, g + (t + 3))
                act.activation(turned_cols(t_hi, c, t, gcol), pT[t % 3][:, :, 0:rows(t)], ACT.Copy,
                               scale=gain[:, gcol:gcol + 1]).then_inc(t_hi_done, 1)

            split_hi(act, 0, None)
            act.wait_ge(gains, 1)
            for gcol, name in ((2, "q"), (1, "k")):
                n0, g0, blocks = PASSES[name]
                if name == "k":
                    act.wait_ge(v_free, 1)
                with act.Fori(0, 2) as c:
                    g = blocks * c + g0
                    for t in range(blocks - 1):
                        front(g, t)
                        if t:
                            back(g, t - 1, c, gcol)
                    split_hi(act, c + (n0 + 1), g + blocks)
                    front(g, blocks - 1)
                    back(g, blocks - 2, c, gcol)
                    back(g, blocks - 1, c, gcol)
            n0, g0, blocks = PASSES["v"]
            for c in range(2):
                for t in range(blocks):
                    if c == 0 and t == blocks - 1:
                        split_hi(act, n0 + 1, g0 + blocks)
                    u = blocks * c + t
                    act.wait_ge(mm_done, g0 + u + 1)
                    if u >= 3:
                        act.wait_ge(v_free, 2 + u - 2)
                    act.activation(v_sb[t % 3][0:rows(t), :], mm[t % 3][0:rows(t), :],
                                   ACT.Copy).then_inc(v_done, 1)

        @block.vector
        def _(dve):
            dve.sem_inc(wlo, 8)
            dve.sem_inc(summed, 1)
            dve.sem_inc(freed, 2)
            split_lo(dve, 0)
            dve.wait_ge(gains_in, 64)
            dve.tensor_scalar(gain[:, 2:3], gain[:, 0:1], HD ** -0.5, None, ALU.mult).then_inc(gains, 1)

            def norm(g, t):
                r = rows(t)
                dve.wait_ge(sq_done, g + (t + 1))
                dve.tensor_reduce(ss[0:r, :], sq[0:r, :].rearrange("p (h d) -> p h d", d=HD), AX.X,
                                  ALU.add).then_inc(summed, 1)
                dve.wait_ge(rms_done, g + (t + 1))
                dve.reciprocal(rstd[0:r, :], rms[0:r, :]).then_inc(rstd_done, 1)
                dve.wait_ge(rstd_done, g + (t + 1))
                dve.wait_ge(turned, g + (t + 1))
                dve.tensor_tensor(qn[t % 3][0:r, :].rearrange("p (h d) -> p h d", d=HD),
                                  mm[t % 3][0:r, :].rearrange("p (h d) -> p h d", d=HD),
                                  rstd[0:r, :].unsqueeze(2).to_broadcast([r, HPC, HD]),
                                  ALU.mult).then_inc(freed, 1)

            def back(g, t, c, gcol):
                dve.wait_ge(t_hi_done, g + (t + 1))
                dve.scalar_tensor_tensor(out=turned_cols(t_lo, c, t, gcol), in0=pT[t % 3][:, :, 0:rows(t)],
                                         scalar=gain[:, gcol:gcol + 1], in1=f32(turned_cols(t_hi, c, t, gcol)),
                                         op0=ALU.mult, op1=ALU.subtract).then_inc(evac, 1)

            dve.sem_inc(evac, 2)
            dve.wait_ge(gains, 1)
            for gcol, name in ((2, "q"), (1, "k")):
                n0, g0, blocks = PASSES[name]
                with dve.Fori(0, 2) as c:
                    g = blocks * c + g0
                    for t in range(blocks - 1):
                        norm(g, t)
                        if t:
                            back(g, t - 1, c, gcol)
                    split_lo(dve, c + (n0 + 1))
                    norm(g, blocks - 1)
                    back(g, blocks - 2, c, gcol)
                    back(g, blocks - 1, c, gcol)
            split_lo(dve, 5)

        @block.tensor
        def _(pe):
            pe.sem_inc(w_used, 7)
            pe.sem_inc(turned, 2)

            def product(n, g, t, last_block, v=None):
                r = rows(t)
                if v is None:
                    pe.wait_ge(freed, g + (t + 1))
                else:
                    pe.wait_ge(freed, PASSES["v"][1] + 2)
                    if v >= 2:
                        pe.wait_ge(v_done, v - 1)
                for k in range(KT):
                    if t == 0:
                        pe.wait_ge(wlo, 8 * n + (k + 9))
                    x_hi, x_lo = h_hi[:, k, toks(t)], h_lo[:, k, toks(t)]
                    pe.matmul(mm[t % 3][0:r, :], x_hi, w_lo[:, k, :], start=(k == 0), stop=False)
                    pe.matmul(mm[t % 3][0:r, :], x_lo, w_hi[:, k, :], start=False, stop=False)
                    last = pe.matmul(mm[t % 3][0:r, :], x_hi, w_hi[:, k, :], start=False, stop=(k == KT - 1))
                    if t == last_block and k < KT - 1:
                        last.then_inc(w_used, 1)
                last.then_inc(mm_done, 1)

            def turn(g, t):
                r = rows(t)
                pe.wait_ge(freed, g + (t + 3))
                pe.wait_ge(evac, g + (t + 1))
                if r < P:
                    pe.sem_inc(pe_passed, 1)
                for ct in range(CT):
                    last = pe.transpose(pT[t % 3][:, ct, 0:r], qn[t % 3][0:r, ct * P:(ct + 1) * P],
                                        ident[0:r, 0:r])
                last.then_inc(turned, 1)

            for name in ("q", "k"):
                n0, g0, blocks = PASSES[name]
                with pe.Fori(0, 2) as c:
                    g = blocks * c + g0
                    for t in range(blocks):
                        product(c + n0, g, t, blocks - 1)
                        if t:
                            turn(g, t - 1)
                    turn(g, blocks - 1)
            n0, g0, blocks = PASSES["v"]
            for c in range(2):
                for t in range(blocks):
                    product(n0 + c, g0 + blocks * c, t, blocks - 1, v=blocks * c + t)


def attention(nc, mem, sem, ctx, io, aT):
    a_hi, a_lo = aT
    QB = BANK // P
    CROW, MROW = HD, 96
    MR = 2 * NB
    base = 65536
    tiles = {}
    for name, rows, cols in (("qa", P, SEQ), ("qb", MROW + MR, SEQ), ("ka", P, L), ("kb", MROW + MR, L)):
        tiles[name] = [mem.at(f"at_{name}{i}", base + 4160 * i, [rows, cols], F32R) for i in range(2)]
        base += 8320
    qa, qb, ka, kb_sb = (tiles[n] for n in ("qa", "qb", "ka", "kb"))
    v_sb = [mem.at(f"at_v{i}", base + 4608 * i, [P, NB + 1, P]) for i in range(2)]
    base += 9216
    pt_sb = [mem.at(f"at_pt{i}", base + 2048 * i, [P, BANK]) for i in range(4)]
    base += 8192
    o_raw, sums = ([mem.at(f"at_{n}{c}", base + 4096 * k + 2048 * c, [P, BANK]) for c in range(2)]
                   for k, n in enumerate(("raw", "sums")))
    o_sb = [mem.at(f"at_out{c}", base + 8192 + 2048 * c, [P, BANK]) for c in range(2)]
    base += 12288
    top3 = mem.at("at_top3", base, [P, NB, 3])
    top = mem.at("at_top", base + 96, [P, NB])
    ntop_hi = mem.at("at_ntop_hi", base + 128, [P, NB], F32R)
    nt = mem.at("at_nt", base + 160, [P, MROW + MR])
    sel = mem.at("at_sel", base + 608, [P, NB])
    eye = mem.at("at_eye", base + 640, [P, P], BF16)
    mask = mem.at("at_mask", base + 896, [P, P], BF16)
    maskT = mem.at("at_maskT", base + 1152, [P, P], BF16)
    zero = mem.at("at_zero", base + 1408, [P, L])
    ident = io["ident"]
    ps = [ctx.enter_context(nc.psum_tensor(f"at_s{i}", [P, BANK], F32)) for i in range(2)]
    pst = [ctx.enter_context(nc.psum_tensor(f"at_st{i}", [P, BANK], F32)) for i in range(2)]
    po = [ctx.enter_context(nc.psum_tensor(f"at_o{c}", [P, BANK], F32)) for c in range(2)]
    pm = ctx.enter_context(nc.psum_tensor("at_m", [P, BANK], F32))
    qk_in = [sem(f"at_qk_in{i}") for i in range(2)]
    v_in = [sem(f"at_v_in{i}") for i in range(2)]
    names = ("consts", "masks", "rows", "s_done", "max_done", "chain", "nt_done", "m_turned", "m_done", "st_done",
             "exp_done", "pv_done", "o_done", "inverted", "divided", "o_hi", "o_lo", "sp_passed", "pool_passed", "pe_passed")
    (consts, masks, rows_done, s_done, max_done, chain, nt_done, m_turned, m_done, st_done,
     exp_done, pv_done, o_done, inverted, divided, o_hi, o_lo, sp_passed, pool_passed, pe_passed) = (sem("at_" + n) for n in names)

    BLOCKS = [(c, kb) for c in range(2) for kb in [*range(QB * (c + 1)), NB]]
    NBL = len(BLOCKS)
    HALF0 = QB + 1
    PIECES = []
    for i in reversed(range(NB)):
        n = META + P * (i + 1)
        parts = -(-n // BANK)
        size = -(-n // parts // 8) * 8
        for q in range(parts):
            PIECES.append((i, q, q * size, min(n, (q + 1) * size) - q * size))
    NPC = len(PIECES)
    assert NPC == NBL and NPC % 2 == 0
    FIRST_PIECES = 6
    assert FIRST_PIECES + NPC // 2 == NBL - 1
    LAG = 3
    CREDIT = 2 * NBL

    def geometry(c, kb):
        first = max(0, kb - QB * c) if kb < NB else 0
        return slice(P * first, BANK), (META if kb == NB else P), (0 if kb == NB else META + P * kb)

    def at(hp, par, n=0):
        return 2 * NBL * hp + (NBL * par + n)

    def need(eng, s, value):
        if not isinstance(value, int) or value > 0:
            eng.wait_ge(s, value)

    def pieces_of(n):
        first = 2 * (n - FIRST_PIECES)
        return range(first, first + 2) if 0 <= first < NPC else ()

    def after(hp, par):
        return (hp, 1) if par == 0 else (hp + 1, 0)

    def before(hp, par):
        return (hp, 0) if par == 1 else (hp - 1, 1)

    def run(eng, head):
        head(0, 0, first=True)
        head(0, 1)
        with eng.Fori(1, H // 2 - 1) as hp:
            head(hp, 0)
            head(hp, 1)
        head(H // 2 - 1, 0)
        head(H // 2 - 1, 1, last=True)

    with nc.Block() as block:
        @block.sync
        def _(sp):
            with sp.Fori(0, H // 2) as hp:
                for par in range(2):
                    if par == 0:
                        sp.wait_ge(masks, 2)
                    gate(sp, pv_done, at(hp, par - 1) + CREDIT, sp_passed)
                    v = io["v"][:, bass.ds(hp * P + par * HD, HD)]
                    cols = slice(par * HD, (par + 1) * HD)
                    sp.dma_start(v_sb[par][:, 0:NB, cols], v[0:SEQ].rearrange("(b p) d -> p b d", p=P))\
                      .then_inc(v_in[par], 16)
                    sp.dma_start(v_sb[par][0:META, NB, cols], v[SEQ:L]).then_inc(v_in[par], 16)

        @block.gpsimd
        def _(pool):
            pool.memset(zero[:], 0.0).then_inc(consts, 1)
            for par in range(2):
                pool.memset(v_sb[par][:, :, (1 - par) * HD:(2 - par) * HD], 1.0).then_inc(masks, 1)
            for tile in (eye, mask, maskT):
                pool.memset(tile[:], 0.0).then_inc(masks, 1)
            pool.memset(sel[:], 1.0).then_inc(masks, 1)
            pool.wait_ge(masks, 6)
            pool.affine_select(out=eye[:], in_=eye[:], compare_op=ALU.not_equal, fill=1.0, base=0,
                               pattern=[[-1, P]], channel_multiplier=1).then_inc(masks, 1)
            pool.affine_select(out=mask[:], in_=mask[:], compare_op=ALU.is_ge, fill=NEG, base=0,
                               pattern=[[-1, P]], channel_multiplier=1).then_inc(masks, 1)
            pool.affine_select(out=maskT[:], in_=maskT[:], compare_op=ALU.is_ge, fill=NEG, base=0,
                               pattern=[[1, P]], channel_multiplier=-1).then_inc(masks, 1)
            pool.affine_select(out=sel[:], in_=sel[:], compare_op=ALU.is_ge, fill=0.0, base=-MROW,
                               pattern=[[-2, NB]], channel_multiplier=1).then_inc(masks, 1)
            pool.wait_ge(masks, 10)
            pool.affine_select(out=sel[:], in_=sel[:], compare_op=ALU.is_ge, fill=0.0, base=MROW + 1,
                               pattern=[[2, NB]], channel_multiplier=-1).then_inc(masks, 1)
            pool.wait_ge(rows_done, 1)

            def load(hp, par):
                gate(pool, st_done, at(hp, par - 1) + CREDIT, pool_passed)
                head = bass.ds(2 * hp + par, 1)
                for dst, name in ((qa[par][:], "qa"), (qb[par][0:CROW + 4, :], "qb"), (kb_sb[par][0:CROW + 4, :], "kb")):
                    pool.dma_start(dst, io[name][head].rearrange("a d t -> (a d) t")).then_inc(qk_in[par], 16)
                k_hi = io["ka"][head].rearrange("a d t -> (a d) t").unsqueeze(0).to_broadcast([2, HD, L])
                pool.dma_start(ka[par][:], k_hi).then_inc(qk_in[par], 16)

            def head(hp, par, first=False, last=False):
                if not last:
                    load(*after(hp, par))

            load(0, 0)
            run(pool, head)

        @block.scalar
        def _(act):
            act.wait_ge(consts, 1)
            for par in range(2):
                act.activation(qb[par][CROW:MROW, :], zero[CROW:MROW, 0:SEQ], ACT.Copy)
                act.activation(kb_sb[par][CROW:MROW, :], zero[CROW:MROW, :], ACT.Copy)
                last = act.activation(kb_sb[par][MROW:MROW + MR, :], io["onesp"][MROW:MROW + MR, :], ACT.Copy)
            last.then_inc(rows_done, 1)

            def exp(hp, par, n):
                c, kb = BLOCKS[n]
                cols, r, _ = geometry(c, kb)
                act.wait_ge(st_done, at(hp, par, n) + (CREDIT + 1))
                act.wait_ge(pv_done, at(hp, par, n) + (CREDIT - 3))
                act.activation(pt_sb[(NBL * par + n) % 4][0:r, cols], pst[n % 2][0:r, cols],
                               ACT.Exp).then_inc(exp_done, 1)

            def copy_out(hp, par, c):
                act.wait_ge(pv_done, at(hp, par, NBL if c else HALF0) + CREDIT)
                if par == 0:
                    need(act, divided, 2 * hp + (c - 1))
                o, other = slice(par * HD, (par + 1) * HD), slice((1 - par) * HD, (2 - par) * HD)
                act.activation(o_raw[c][o, :], po[c][o, :], ACT.Copy).then_inc(o_done, 1)
                act.activation(sums[c][o, :], po[c][other, :], ACT.Copy).then_inc(o_done, 1)

            def out_hi(hp, c):
                act.wait_ge(divided, 2 * hp + (c + 1))
                act.activation(a_hi[:, bass.ds(hp, 1), c * BANK:(c + 1) * BANK],
                               o_sb[c][:].unsqueeze(1), ACT.Copy).then_inc(o_hi, 1)

            def head(hp, par, first=False, last=False):
                for n in range(NBL):
                    exp(hp, par, n)
                    if n == 1 and not first:
                        copy_out(*before(hp, par), 1)
                    if n == HALF0 + LAG:
                        copy_out(hp, par, 0)
                    if par == 0 and not first and n in (3, 5):
                        out_hi(hp - 1, (n - 3) // 2)

            run(act, head)
            copy_out(H // 2 - 1, 1, 1)
            out_hi(H // 2 - 1, 0)
            out_hi(H // 2 - 1, 1)

        @block.vector
        def _(dve):
            dve.sem_inc(o_lo, 2)
            dve.memset(top3[:], NEG).then_inc(chain, 1)
            dve.memset(nt[:], 0.0).then_inc(chain, 1)
            dve.wait_ge(chain, 2)
            dve.wait_ge(masks, 11)

            def piece(hp, par, p):
                i, q, _, width = PIECES[p]
                dve.wait_ge(s_done, at(hp, par, p) + 1)
                dve.tensor_reduce(top3[:, i, q:q + 1], ps[p % 2][:, 0:width], AX.X, ALU.max).then_inc(max_done, 1)

            def maxima(hp, par):
                g = 8 * hp + 4 * par
                pairs = nt[:, MROW:].rearrange("p (i two) -> p two i", two=2)
                dve.wait_ge(max_done, at(hp, par, NPC))
                dve.wait_ge(chain, g + 2)
                dve.tensor_reduce(top[:], top3[:], AX.X, ALU.max).then_inc(chain, 1)
                dve.wait_ge(chain, g + 3)
                dve.tensor_scalar(ntop_hi[:], top[:], -1.0, None, ALU.mult).then_inc(chain, 1)
                dve.wait_ge(chain, g + 4)
                dve.tensor_copy(pairs[:, 0, :], f32(ntop_hi[:])).then_inc(chain, 1)
                dve.scalar_tensor_tensor(out=pairs[:, 1, :], in0=top[:], scalar=-1.0, in1=f32(ntop_hi[:]),
                                         op0=ALU.mult, op1=ALU.subtract).then_inc(chain, 1)
                dve.wait_ge(chain, g + 6)
                dve.sem_inc(nt_done, 1)

            def spread(hp, par):
                dve.wait_ge(m_turned, 2 * hp + (par + 1))
                rows = slice(MROW, MROW + MR)
                dve.tensor_tensor(qb[par][rows, :].rearrange("p (i t) -> p i t", t=P),
                                  pm[rows, 0:P].unsqueeze(1).to_broadcast([MR, NB, P]),
                                  sel[rows, :].unsqueeze(2).to_broadcast([MR, NB, P]), ALU.mult).then_inc(m_done, 1)

            def invert(hp, c, quarter):
                if quarter == 0:
                    dve.wait_ge(o_done, 8 * hp + (2 * c + 6))
                cols = slice(quarter * P, (quarter + 1) * P)
                dve.reciprocal(sums[c][:, cols], sums[c][:, cols]).then_inc(inverted, 1)

            def divide(hp, c):
                dve.wait_ge(inverted, 8 * hp + (4 * c + 4))
                dve.wait_ge(o_lo, 2 * hp + (c + 1))
                dve.tensor_tensor(o_sb[c][:], o_raw[c][:], sums[c][:], ALU.mult).then_inc(divided, 1)

            def out_lo(hp, c):
                dve.wait_ge(o_hi, 2 * hp + (c + 1))
                where = (slice(0, P), bass.ds(hp, 1), slice(c * BANK, (c + 1) * BANK))
                dve.tensor_tensor(a_lo[where], o_sb[c][:].unsqueeze(1), f32(a_hi[where]),
                                  ALU.subtract).then_inc(o_lo, 1)

            def head(hp, par, first=False, last=False):
                for n in range(NBL):
                    if par == 0 and not first and n < 4:
                        c = n // 2
                        invert(hp - 1, c, 2 * (n % 2))
                        invert(hp - 1, c, 2 * (n % 2) + 1)
                        if n % 2:
                            divide(hp - 1, c)
                    if not last:
                        for p in pieces_of(n):
                            piece(*after(hp, par), p)
                    if par == 0 and not first and n in (4, 6):
                        out_lo(hp - 1, (n - 4) // 2)
                if not last:
                    maxima(*after(hp, par))
                    spread(*after(hp, par))

            for p in range(NPC):
                piece(0, 0, p)
            maxima(0, 0)
            spread(0, 0)

            run(dve, head)
            for c in range(2):
                for quarter in range(4):
                    invert(H // 2 - 1, c, quarter)
                divide(H // 2 - 1, c)
                out_lo(H // 2 - 1, c)

        @block.tensor
        def _(pe):
            pe.sem_inc(st_done, CREDIT)
            pe.sem_inc(pv_done, CREDIT)
            pe.wait_ge(masks, 11)
            pe.wait_ge(rows_done, 1)

            def piece(hp, par, p):
                i, q, a, width = PIECES[p]
                if p == 0:
                    pe.wait_ge(qk_in[par], 64 * hp + 64)
                need(pe, max_done, at(hp, par, p) - 1)
                out, rows = ps[p % 2][:, 0:width], slice(i * P, (i + 1) * P)
                masked = a + width == META + P * (i + 1)
                pe.matmul(out, qa[par][:, rows], ka[par][:, a:a + width], start=True, stop=False)
                last = pe.matmul(out, qb[par][0:CROW + 4, rows], kb_sb[par][0:CROW + 4, a:a + width],
                                 start=False, stop=not masked)
                if masked:
                    last = pe.matmul(ps[p % 2][:, width - P:width], eye[:], mask[:], start=False, stop=True)
                last.then_inc(s_done, 1)

            def scores(hp, par, n):
                c, kb = BLOCKS[n]
                cols, r, a = geometry(c, kb)
                queries = slice(c * BANK + cols.start, (c + 1) * BANK)
                if n == 0:
                    pe.wait_ge(m_done, 2 * hp + (par + 1))
                need(pe, exp_done, at(hp, par, n) - 1)
                if r < P:
                    pe.sem_inc(pe_passed, 1)
                diagonal = QB * c <= kb < NB
                out = pst[n % 2][0:r, cols]
                pe.matmul(out, ka[par][:, a:a + r], qa[par][:, queries], start=True, stop=False)
                last = pe.matmul(out, kb_sb[par][:, a:a + r], qb[par][:, queries], start=False, stop=not diagonal)
                if diagonal:
                    last = pe.matmul(pst[n % 2][:, cols.start:cols.start + P], eye[:], maskT[:],
                                     start=False, stop=True)
                last.then_inc(st_done, 1)

            def values(hp, par, n):
                c, kb = BLOCKS[n]
                cols, r, _ = geometry(c, kb)
                first = n in (0, HALF0)
                if n == 0:
                    pe.wait_ge(v_in[par], 32 * hp + 32)
                if first:
                    need(pe, o_done, 8 * hp + (4 * par + 2 * c - 2))
                pe.wait_ge(exp_done, at(hp, par, n) + 1)
                if r < P:
                    pe.sem_inc(pe_passed, 1)
                pe.matmul(po[c][:, cols], v_sb[par][0:r, kb, :], pt_sb[(NBL * par + n) % 4][0:r, cols],
                          start=first, stop=(kb == NB)).then_inc(pv_done, 1)

            def turn(hp, par):
                pe.wait_ge(nt_done, 2 * hp + (par + 1))
                pe.sem_inc(pe_passed, 1)
                pe.transpose(pm[0:MROW + MR, 0:P], nt[:], ident[:]).then_inc(m_turned, 1)

            def head(hp, par, first=False, last=False):
                for n in range(NBL):
                    scores(hp, par, n)
                    if not last:
                        for p in pieces_of(n):
                            piece(*after(hp, par), p)
                    if n >= LAG:
                        values(hp, par, n - LAG)
                if not last:
                    turn(*after(hp, par))
                for n in range(NBL - LAG, NBL):
                    values(hp, par, n)

            for p in range(NPC):
                piece(0, 0, p)
            turn(0, 0)
            run(pe, head)


def merge(nc, mem, sem, ctx, io, aT, mT):
    m_hi, m_lo = mT
    base = 65536
    ring = WeightUnits(mem, sem, "mg", base, 2)
    base += 2 * 12288
    part = [mem.at(f"mg_part{i}", base + 4096 * i, [P, SEQ]) for i in range(2)]
    sgb = [mem.at(f"mg_sgb{i}", base + 8192 + 4096 * i, [P, SEQ]) for i in range(2)]
    gated = mem.at("mg_gated", base + 16384, [P, SEQ])
    merged = mem.at("mg_merged", base + 20480, [P, SEQ])
    out = [ctx.enter_context(nc.psum_tensor(f"mg_o{i}", [P, SEQ], F32)) for i in range(2)]
    tiles_in = [sem(f"mg_tiles_in{i}") for i in range(2)]
    read, merged_done, hi_done, lo_done = (sem("mg_" + s) for s in ("read", "merged_done", "hi", "lo"))
    halves = [slice(0, BANK), slice(BANK, SEQ)]

    with nc.Block() as block:
        @block.sync
        def _(sp):
            with sp.Fori(0, KT // 2) as i:
                for u in range(2):
                    m = 2 * i + u
                    ring.load(sp, io["w_att_out"][0][:, bass.ds(m * P, P)], m, u)
                    gate(sp, merged_done, m + 1, ring.passed)
                    for dst, src in ((part[u], io["part"]), (sgb[u], io["sgb"])):
                        sp.dma_start(dst[:], src[bass.ds(m, 1)].rearrange("a p t -> p (a t)"))\
                          .then_inc(tiles_in[u], 16)

        @block.scalar
        def _(act):
            def merged_hi(m):
                act.wait_ge(merged_done, m + 3)
                act.activation(m_hi[:, bass.ds(m, 1), :], merged[:].unsqueeze(1), ACT.Copy).then_inc(hi_done, 1)

            ring.split_hi(act, 0, 0, 0)
            with act.Fori(0, KT // 2 - 1) as i:
                for u in range(2):
                    ring.split_hi(act, 2 * i + (u + 1), 1 - u, i + u)
                    merged_hi(2 * i + u)
            ring.split_hi(act, KT - 1, 1, KT // 2 - 1)
            merged_hi(KT - 2)
            merged_hi(KT - 1)

        @block.vector
        def _(dve):
            dve.sem_inc(ring.lo_done, 2)
            dve.sem_inc(merged_done, 2)

            def merged_lo(m, u, use):
                dve.wait_ge(ring.used, m + 3)
                dve.wait_ge(tiles_in[u], 32 * use + 32)
                dve.tensor_tensor(gated[:], out[u][:], sgb[u][:], ALU.mult).then_inc(read, 1)
                dve.wait_ge(read, m + 1)
                dve.tensor_tensor(merged[:], gated[:], part[u][:], ALU.add).then_inc(merged_done, 1)
                dve.wait_ge(hi_done, m + 1)
                dve.tensor_tensor(m_lo[:, bass.ds(m, 1), :], merged[:].unsqueeze(1),
                                  f32(m_hi[:, bass.ds(m, 1), :]), ALU.subtract).then_inc(lo_done, 1)

            ring.split_lo(dve, 0, 0)
            with dve.Fori(0, KT // 2 - 1) as i:
                for u in range(2):
                    ring.split_lo(dve, 2 * i + (u + 1), 1 - u)
                    merged_lo(2 * i + u, u, i)
            ring.split_lo(dve, KT - 1, 1)
            merged_lo(KT - 2, 0, KT // 2 - 1)
            merged_lo(KT - 1, 1, KT // 2 - 1)

        @block.tensor
        def _(pe):
            pe.sem_inc(ring.used, 2)
            with pe.Fori(0, KT // 2) as i:
                for u in range(2):
                    m = 2 * i + u
                    pe.wait_ge(merged_done, m + 1)
                    ring.product(pe, m, u, aT, [out[u][:, c] for c in halves], halves)


def residual(nc, mem, sem, ctx, io, mT, x2n, logits, retired):
    m_hi, m_lo = mT
    NR = NG + NE
    raw = mem.at("rs_raw", 0, [P, KT // 4, D])
    w_hi = mem.at("rs_whi", 8192, [P, KT, D], F32R)
    w_lo = mem.at("rs_wlo", 40960, [P, KT, D], F32R)
    base = 106496
    x_sb = [mem.at(f"rs_x{i}", base + 4096 * i, [P, D]) for i in range(2)]
    g_b = mem.at("rs_g", base + 8192, [P, D])
    t_hi = mem.at("rs_thi", base + 12288, [P, KT, P], F32R)
    t_lo = mem.at("rs_tlo", base + 16384, [P, KT, P], F32R)
    sq = mem.at("rs_sq", base + 20480, [P, D])
    base += 24576
    wr = mem.at("rs_wr", base, [P, KT, NR])
    wr_hi = mem.at("rs_wrhi", base + 1152, [P, KT, NR], F32R)
    wr_lo = mem.at("rs_wrlo", base + 2304, [P, KT, NR], F32R)
    br = mem.at("rs_br", base + 3456, [P, NR])
    stat = mem.at("rs_stat", base + 3648, [P, 8])
    ident = io["ident"]
    py = [ctx.enter_context(nc.psum_tensor(f"rs_y{i}", [P, D], F32)) for i in range(2)]
    pT = ctx.enter_context(nc.psum_tensor("rs_T", [P, KT, P], F32))
    pl = ctx.enter_context(nc.psum_tensor("rs_l", [P, BANK], F32))
    names = ("raw_in", "consts_in", "whi", "wlo", "y_done", "x2_done", "squared", "rms", "recip", "xn_done",
             "turned", "t_hi", "t_lo", "logits_mm", "logits_done", "x2_stored", "wr_hi", "wr_lo")
    (raw_in, consts_in, whi, wlo, y_done, x2_done, squared, rms, recip, xn_done,
     turned, thi_done, tlo_done, logits_mm, logits_done, x2_stored, wrhi_done, wrlo_done) = (
        sem("rs_" + n) for n in names)
    x_in = [sem(f"rs_x_in{i}") for i in range(2)]
    x_blocks = io["x"].rearrange("b (t p) d -> (b t) p d", p=P)
    w_o = io["w_merge_out"][0].rearrange("(k p) c -> p k c", p=P)

    with nc.Block() as block:
        @block.sync
        def _(sp):
            for q in range(4):
                if q:
                    sp.wait_ge(wlo, 2 * q)
                sp.dma_start(raw[:], w_o[:, 2 * q:2 * q + 2, :]).then_inc(raw_in, 16)
                if q == 0:
                    sp.dma_start(wr[:, :, 0:NG], io["w_router_group"][0].rearrange("(k p) c -> p k c", p=P)).then_inc(consts_in, 16)
                    sp.dma_start(wr[:, :, NG:NR], io["w_router_expert"][0].rearrange("(k p) c -> p k c", p=P)).then_inc(consts_in, 16)
                    sp.dma_start(br[:, 0:NG], io["b_router_group"].partition_broadcast(P)).then_inc(consts_in, 16)
                    sp.dma_start(br[:, NG:NR], io["b_router_expert"].partition_broadcast(P)).then_inc(consts_in, 16)
                    sp.dma_start(g_b[:], io["norm2_g"].partition_broadcast(P)).then_inc(consts_in, 16)
            for t in range(NB):
                if t >= 2:
                    sp.wait_ge(x2_stored, 16 * (t - 1))
                    sp.wait_ge(xn_done, t - 1)
                sp.dma_start(x_sb[t % 2][:], x_blocks[t]).then_inc(x_in[t % 2], 16)

        @block.gpsimd
        def _(pool):
            for s in retired:
                pool.sem_clear(s)
            for t in range(NB):
                pool.wait_ge(x2_done, 2 * t + 2)
                pool.dma_start(io["x2"][t * P:(t + 1) * P, :], x_sb[t % 2][:]).then_inc(x2_stored, 16)
                pool.wait_ge(x2_stored, 16 * t + 16)

        @block.scalar
        def _(act):
            for k in range(KT):
                if k % 2 == 0:
                    act.wait_ge(raw_in, 8 * k + 16)
                act.activation(w_hi[:, k, :], raw[:, k % 2, :], ACT.Copy).then_inc(whi, 1)
            act.wait_ge(consts_in, 80)
            act.activation(wr_hi[:], wr[:], ACT.Copy).then_inc(wrhi_done, 1)

            def front(t):
                act.wait_ge(x2_done, 2 * t + 2)
                act.activation(sq[:], x_sb[t % 2][:], ACT.Square, accum_out=stat[:, 0:1]).then_inc(squared, 1)
                act.wait_ge(squared, t + 1)
                act.activation(stat[:, 2:3], stat[:, 0:1], ACT.Sqrt, scale=1.0 / D,
                               bias=io["eps"][:]).then_inc(rms, 1)

            def back(t):
                act.wait_ge(turned, t + 1)
                if t:
                    act.wait_ge(logits_mm, t)
                act.activation(t_hi[:], pT[:], ACT.Copy).then_inc(thi_done, 1)

            front(0)
            for t in range(1, NB):
                front(t)
                back(t - 1)
            back(NB - 1)

        @block.vector
        def _(dve):
            for k in range(KT):
                dve.wait_ge(whi, k + 1)
                dve.tensor_tensor(w_lo[:, k, :], raw[:, k % 2, :], f32(w_hi[:, k, :]), ALU.subtract).then_inc(wlo, 1)
            dve.wait_ge(wrhi_done, 1)
            dve.tensor_tensor(wr_lo[:], wr[:], f32(wr_hi[:]), ALU.subtract).then_inc(wrlo_done, 1)

            def front(t):
                dve.wait_ge(y_done, t + 1)
                dve.wait_ge(x_in[t % 2], 16 * (t // 2) + 16)
                for c in range(2):
                    cols = slice(c * BANK, (c + 1) * BANK)
                    dve.tensor_tensor(x_sb[t % 2][:, cols], py[t % 2][:, cols], x_sb[t % 2][:, cols],
                                      ALU.add).then_inc(x2_done, 1)
                dve.wait_ge(rms, t + 1)
                dve.reciprocal(stat[:, 4:5], stat[:, 2:3]).then_inc(recip, 1)
                dve.wait_ge(recip, t + 1)
                dve.scalar_tensor_tensor(out=x2n[:, t, :], in0=x_sb[t % 2][:], scalar=stat[:, 4:5], in1=g_b[:],
                                         op0=ALU.mult, op1=ALU.mult).then_inc(xn_done, 1)

            def back(t):
                dve.wait_ge(thi_done, t + 1)
                dve.tensor_tensor(t_lo[:], pT[:], f32(t_hi[:]), ALU.subtract).then_inc(tlo_done, 1)
                dve.wait_ge(logits_mm, t + 1)
                dve.tensor_tensor(logits[:, t, :], pl[:, 0:NR], br[:], ALU.add).then_inc(logits_done, 1)

            front(0)
            for t in range(1, NB):
                front(t)
                back(t - 1)
            back(NB - 1)

        @block.tensor
        def _(pe):
            def product(t):
                for k in range(KT):
                    if t == 0:
                        pe.wait_ge(wlo, k + 1)
                    elif k == 0 and t >= 2:
                        pe.wait_ge(x2_done, 2 * t - 2)
                    for c in range(2):
                        cols = slice(c * BANK, (c + 1) * BANK)
                        rows = slice(t * P, (t + 1) * P)
                        last = split3(pe, py[t % 2][:, cols], m_hi[:, k, rows], m_lo[:, k, rows],
                                      w_hi[:, k, cols], w_lo[:, k, cols], k == 0, k == KT - 1)
                last.then_inc(y_done, 1)

            def route(t):
                pe.wait_ge(xn_done, t + 1)
                if t:
                    pe.wait_ge(tlo_done, t)
                for k in range(KT):
                    last = pe.transpose(pT[:, k, :], x2n[:, t, k * P:(k + 1) * P], ident[:])
                last.then_inc(turned, 1)

            def score(t):
                pe.wait_ge(tlo_done, t + 1)
                if t:
                    pe.wait_ge(logits_done, t)
                else:
                    pe.wait_ge(wrlo_done, 1)
                for k in range(KT):
                    last = split3(pe, pl[:, 0:NR], t_hi[:, k, :], t_lo[:, k, :], wr_hi[:, k, :], wr_lo[:, k, :],
                                  k == 0, k == KT - 1)
                last.then_inc(logits_mm, 1)

            product(0)
            for t in range(1, NB):
                product(t)
                if t >= 2:
                    score(t - 2)
                route(t - 1)
            score(NB - 2)
            route(NB - 1)
            score(NB - 1)


def route(nc, mem, sem, ctx, io, x2n, logits, dest, weights, table):
    W = 2 ** 100
    offset = [0]

    def tile(name, *shape, dtype=F32):
        t = mem.at("rt_" + name, offset[0], [P, *shape], dtype)
        n = 4
        for d in shape:
            n *= d
        offset[0] += (n + 31) // 32 * 32
        return t

    jrev4, jrev32, j32 = tile("jrev4", NB, NG), tile("jrev32", NB, NE), tile("j32", NE)
    step128 = tile("step128", NB, NE)
    before, pidx, pidx128 = tile("before", P), tile("pidx", 1), tile("pidx128", 1)
    iot = tile("iot", NB, NE, dtype=I32)
    iot4, iotj, iot8, iotp = (tile("iot4", NB, NG, dtype=I32), tile("iotj", NE, dtype=I32),
                              tile("iot8", NB, NE, dtype=I32), tile("iotp", 1, dtype=I32))
    gmax, gsum, gsel = tile("gmax", NB), tile("gsum", NB), tile("gsel", NB)
    d4, e4, oh4, c4 = (tile(n, NB, NG) for n in ("d4", "e4", "oh4", "c4"))
    lem, lem2, d32, c32, oh1, oh2, both = (tile(n, NB, NE) for n in ("lem", "lem2", "d32", "c32", "oh1", "oh2", "both"))
    m1, m2, dm, em, sel, w1 = (tile(n, NB) for n in ("m1", "m2", "dm", "em", "sel", "w1"))
    tot, pos, hit = tile("tot", NB, NE), tile("pos", NB, NE), tile("hit", NB, NE)
    pre = tile("pre", NB + 1, NE)
    inc, start, nblk, bend, bst, lo, ind, rowv = (tile(n, NE) for n in ("inc", "start", "nblk", "bend", "bst", "lo", "ind", "rowv"))
    destf, tabf, tabi = tile("destf", 2, NB), tile("tabf", 4), tile("tabi", 4, dtype=I32)
    zero = tile("zero", D)
    ones = io["onesp"]
    p_rank = ctx.enter_context(nc.psum_tensor("rt_rank", [P, BANK], F32))
    p_tot = ctx.enter_context(nc.psum_tensor("rt_tot", [P, BANK], F32))
    names = ("chain", "consts", "iotas", "d4_done", "e4_done", "dm_done", "em_done", "both_done", "ranked", "dest_done", "tab_done",
             "tab_stored", "tab_in", "scattered", "zeroed")
    (chain, consts, iotas, d4_done, e4_done, dm_done, em_done, both_done, ranked, dest_done, tab_done,
     tab_stored, tab_in, scattered, zeroed) = (sem("rt_" + n) for n in names)
    lg, le = logits[:, :, 0:NG], logits[:, :, NG:NG + NE]

    def wide(ap, n):
        return ap.unsqueeze(2).to_broadcast([P, ap.shape[1], n])

    with nc.Block() as block:
        @block.sync
        def _(sp):
            sp.wait_ge(iotas, 7)
            sp.dma_start(io["xs"][SLOTS:XROWS, :], zero[:]).then_inc(zeroed, 16)
            sp.wait_ge(tab_done, 1)
            sp.dma_start(io["tab"], tabi[:]).then_inc(tab_stored, 16)
            sp.wait_ge(tab_stored, 16)
            sp.dma_start(table[:], io["tab"].rearrange("(o p) c -> o (p c)", o=1)).then_inc(tab_in, 16)
            sp.wait_ge(tab_in, 16)
            sp.wait_ge(zeroed, 16)

        @block.gpsimd
        def _(pool):
            pool.iota(iot[:], pattern=[[0, NB], [-1, NE]], base=NE, channel_multiplier=0).then_inc(iotas, 1)
            pool.iota(iot4[:], pattern=[[0, NB], [-1, NG]], base=NG, channel_multiplier=0).then_inc(iotas, 1)
            pool.iota(iotj[:], pattern=[[1, NE]], base=0, channel_multiplier=0).then_inc(iotas, 1)
            pool.iota(iot8[:], pattern=[[P, NB], [0, NE]], base=0, channel_multiplier=0).then_inc(iotas, 1)
            pool.iota(iotp[:], pattern=[[0, 1]], base=0, channel_multiplier=1).then_inc(iotas, 1)
            pool.memset(zero[:], 0.0).then_inc(iotas, 1)
            pool.memset(before[:], 1.0).then_inc(consts, 1)
            pool.wait_ge(consts, 1)
            pool.affine_select(out=before[:], in_=before[:], compare_op=ALU.is_gt, fill=0.0, base=0,
                               pattern=[[1, P]], channel_multiplier=-1).then_inc(iotas, 1)
            pool.wait_ge(dest_done, 1)
            for b in range(NB):
                for c in range(2):
                    pool.indirect_dma_start(io["xs"], bass.IndirectOffsetOnAxis(ap=dest[:, c, b:b + 1], axis=0),
                                            x2n[:, b, :], None).then_inc(scattered, 16)
            pool.wait_ge(scattered, 16 * 2 * NB)

        @block.scalar
        def _(act):
            act.wait_ge(d4_done, 1)
            act.activation(e4[:], d4[:], ACT.Exp).then_inc(e4_done, 1)
            act.wait_ge(dm_done, 1)
            act.activation(em[:], dm[:], ACT.Exp).then_inc(em_done, 1)

        @block.vector
        def _(dve):
            count = [0]

            def link(ins):
                count[0] += 1
                ins.then_inc(chain, 1)
                dve.wait_ge(chain, count[0])

            dve.wait_ge(iotas, 7)
            for dst, src in ((jrev32, iot), (jrev4, iot4), (j32, iotj), (step128, iot8), (pidx, iotp)):
                link(dve.tensor_copy(dst[:], src[:]))
            link(dve.tensor_scalar(pidx128[:], pidx[:], float(P), None, ALU.mult))
            link(dve.tensor_reduce(gmax[:], lg, AX.X, ALU.max))
            dve.tensor_tensor(d4[:], lg, wide(gmax[:], NG), ALU.subtract).then_inc(d4_done, 1)
            dve.wait_ge(d4_done, 1)
            link(dve.scalar_tensor_tensor(out=c4[:], in0=d4[:], scalar=0.0, in1=jrev4[:], op0=ALU.is_ge, op1=ALU.mult))
            link(dve.tensor_reduce(gsel[:], c4[:], AX.X, ALU.max))
            link(dve.tensor_tensor(oh4[:], jrev4[:], wide(gsel[:], NG), ALU.is_equal))
            link(dve.tensor_scalar(oh4[:], oh4[:], -1.0, float(W), ALU.add, ALU.mult))
            link(dve.tensor_copy(lem[:], le))
            link(dve.tensor_tensor(lem[:].rearrange("p b (g e) -> p (b g) e", g=NG),
                                   lem[:].rearrange("p b (g e) -> p (b g) e", g=NG),
                                   wide(oh4[:].rearrange("p b g -> p (b g)"), EPG), ALU.add))

            def pick(logit, top, onehot):
                link(dve.tensor_reduce(top[:], logit[:], AX.X, ALU.max))
                link(dve.tensor_tensor(d32[:], logit[:], wide(top[:], NE), ALU.subtract))
                link(dve.scalar_tensor_tensor(out=c32[:], in0=d32[:], scalar=0.0, in1=jrev32[:],
                                              op0=ALU.is_ge, op1=ALU.mult))
                link(dve.tensor_reduce(sel[:], c32[:], AX.X, ALU.max))
                link(dve.tensor_tensor(onehot[:], jrev32[:], wide(sel[:], NE), ALU.is_equal))

            pick(lem, m1, oh1)
            link(dve.scalar_tensor_tensor(out=lem2[:], in0=oh1[:], scalar=-2.0 * W, in1=lem[:],
                                          op0=ALU.mult, op1=ALU.add))
            pick(lem2, m2, oh2)
            dve.tensor_tensor(dm[:], m2[:], m1[:], ALU.subtract).then_inc(dm_done, 1)
            dve.tensor_tensor(both[:], oh1[:], oh2[:], ALU.add).then_inc(both_done, 1)
            dve.wait_ge(e4_done, 1)
            link(dve.tensor_reduce(gsum[:], e4[:], AX.X, ALU.add))
            dve.wait_ge(em_done, 1)
            link(dve.scalar_tensor_tensor(out=w1[:], in0=em[:], scalar=1.0, in1=gsum[:], op0=ALU.add, op1=ALU.mult))
            link(dve.reciprocal(weights[:, 0, :], w1[:]))
            link(dve.tensor_tensor(weights[:, 1, :], weights[:, 0, :], em[:], ALU.mult))
            dve.wait_ge(ranked, 1)
            link(dve.tensor_copy(tot[:], p_tot[:, 0:NB * NE].rearrange("p (b e) -> p b e", b=NB)))
            link(dve.memset(pre[:, 0, :], 0.0))
            for b in range(NB):
                link(dve.tensor_tensor(pre[:, b + 1, :], pre[:, b, :], tot[:, b, :], ALU.add))
            total = pre[:, NB, :]
            link(dve.tensor_tensor_scan(inc[:], ones[:, 0:NE], total, 0.0, ALU.mult, ALU.add))
            link(dve.tensor_tensor(start[:], inc[:], total, ALU.subtract))
            link(dve.tensor_tensor(pos[:], p_rank[:, 0:NB * NE].rearrange("p (b e) -> p b e", b=NB),
                                   pre[:, 0:NB, :], ALU.add))
            link(dve.tensor_tensor(pos[:], pos[:], start[:].unsqueeze(1).to_broadcast([P, NB, NE]), ALU.add))
            for c, oh in enumerate((oh1, oh2)):
                link(dve.tensor_tensor(hit[:], oh[:], pos[:], ALU.mult))
                link(dve.tensor_reduce(destf[:, c, :], hit[:], AX.X, ALU.add))
            dve.tensor_copy(dest[:], destf[:]).then_inc(dest_done, 1)
            link(dve.tensor_tensor(hit[:], total.unsqueeze(1).to_broadcast([P, NB, NE]), step128[:], ALU.is_gt))
            link(dve.tensor_reduce(nblk[:], hit[:].rearrange("p b e -> p e b"), AX.X, ALU.add))
            link(dve.tensor_tensor_scan(bend[:], ones[:, 0:NE], nblk[:], 0.0, ALU.mult, ALU.add))
            link(dve.tensor_tensor(bst[:], bend[:], nblk[:], ALU.subtract))
            link(dve.tensor_scalar(lo[:], bst[:], pidx[:], None, ALU.is_le))
            link(dve.scalar_tensor_tensor(out=ind[:], in0=bend[:], scalar=pidx[:], in1=lo[:],
                                          op0=ALU.is_gt, op1=ALU.mult))
            link(dve.scalar_tensor_tensor(out=rowv[:], in0=bst[:], scalar=-float(P), in1=start[:],
                                          op0=ALU.mult, op1=ALU.add))
            link(dve.scalar_tensor_tensor(out=rowv[:], in0=rowv[:], scalar=pidx128[:], in1=ind[:],
                                          op0=ALU.add, op1=ALU.mult))
            link(dve.tensor_reduce(tabf[:, 1:2], rowv[:], AX.X, ALU.add))
            link(dve.tensor_tensor(lo[:], ind[:], j32[:], ALU.mult))
            link(dve.tensor_reduce(tabf[:, 0:1], lo[:], AX.X, ALU.add))
            link(dve.tensor_scalar(tabf[:, 2:3], bend[:, NE - 1:NE], -2.0, None, ALU.add))
            link(dve.tensor_copy(tabf[:, 3:4], pidx[:]))
            dve.tensor_copy(tabi[:], tabf[:]).then_inc(tab_done, 1)

        @block.tensor
        def _(pe):
            pe.wait_ge(both_done, 1)
            rhs = both[:].rearrange("p b e -> p (b e)")
            pe.matmul(p_rank[:, 0:NB * NE], before[:], rhs, start=True, stop=True)
            pe.matmul(p_tot[:, 0:NB * NE], ones[:, 0:P], rhs, start=True, stop=True).then_inc(ranked, 1)


def experts(nc, mem, sem, ctx, io, table):
    HALF = KT // 2 * DE
    base = 0
    raw, w_hi, w_lo = [], [], []
    for i in range(6):
        raw.append(mem.at(f"ex_raw{i}", base, [P, HALF]))
        base += 4 * HALF
    for dst, name in ((w_hi, "whi"), (w_lo, "wlo")):
        for i in range(3):
            dst.append(mem.at(f"ex_{name}{i}", base, [P, 2 * HALF], F32R))
            base += 8 * HALF
    x_sb = mem.at("ex_x", base, [P, D])
    x_hi = mem.at("ex_xhi", base + 4096, [P, KT, P], F32R)
    x_lo = mem.at("ex_xlo", base + 8192, [P, KT, P], F32R)
    h_hi = mem.at("ex_hhi", base + 12288, [P, KE, P], F32R)
    h_lo = mem.at("ex_hlo", base + 14336, [P, KE, P], F32R)
    act_g = mem.at("ex_silu", base + 16384, [P, DE])
    h_sb = mem.at("ex_h", base + 18432, [P, DE])
    y_sb = mem.at("ex_y", base + 20480, [P, D])
    ident = io["ident"]
    p_gate, p_up = (ctx.enter_context(nc.psum_tensor("ex_p" + n, [P, DE], F32)) for n in ("gate", "up"))
    p_y = ctx.enter_context(nc.psum_tensor("ex_py", [P, D], F32))
    p_xT = ctx.enter_context(nc.psum_tensor("ex_pxT", [P, KT, P], F32))
    p_hT = ctx.enter_context(nc.psum_tensor("ex_phT", [P, KE, P], F32))
    raw_in = [sem(f"ex_raw_in{i}") for i in range(6)]
    names = ("x_in", "whi", "wlo", "gate_done", "up_done", "down_done", "x_turned", "x_hi", "x_lo", "silu_done",
             "h_done", "h_turned", "h_hi", "h_lo", "y0_done", "y1_done", "stored", "y_free", "passed", "pool_passed")
    (x_in, whi, wlo, gate_done, up_done, down_done, x_turned, xhi_done, xlo_done, silu_done,
     h_done, h_turned, hhi_done, hlo_done, y0_done, y1_done, stored, y_free, passed, pool_passed) = (
        sem("ex_" + n) for n in names)
    GATE, UP, DOWN = 0, 1, 2
    products = ((GATE, gate_done), (UP, up_done), (DOWN, down_done))

    def order(unit, b, last=False):
        if unit != DOWN and isinstance(b, int) and b == 0:
            return 2 * unit
        return 6 * b + (4 if last else (-2, 0, 8)[unit])

    def entry(eng, b, column, most):
        at = slice(4 * b + column, 4 * b + column + 1) if isinstance(b, int) else bass.ds(4 * b + column, 1)
        return eng.value_load(table[0:1, at], min_val=0, max_val=most)

    def blocks(eng):
        return eng.value_load(table[0:1, 2:3], min_val=SLOTS // P - 2, max_val=MAXBLK - 2) + 2

    with nc.Block() as block:
        @block.sync
        def _(sp):
            def load_x(b):
                row = entry(sp, b, 1, SLOTS)
                if not (isinstance(b, int) and b == 0):
                    gate(sp, x_turned, b, passed)
                sp.dma_start(x_sb[:], io["xs"][bass.ds(row, P), :]).then_inc(x_in, 16)

            def load(unit, b, e):
                for s in range(2):
                    if not (isinstance(b, int) and b == 0):
                        before = order(unit, 0) if isinstance(b, int) and b == 1 else order(unit, b - 1)
                        gate(sp, wlo, before + s + 1, passed)
                    w = io[("w_exp_gate", "w_exp_up", "w_exp_down")[unit]][0][bass.ds(e, 1)]
                    w = w.rearrange("o (s k p) c -> s p (o k) c", s=2, p=P)[s]
                    dst = raw[2 * unit + s][:].rearrange("p (k c) -> p k c", c=D if unit == DOWN else DE)
                    sp.dma_start(dst, w).then_inc(raw_in[2 * unit + s], 16)

            n = blocks(sp)
            load_x(0)
            e = entry(sp, 0, 0, NE - 1)
            load(GATE, 0, e)
            load(UP, 0, e)
            load_x(1)

            def step(b):
                e = entry(sp, b, 0, NE - 1)
                load(GATE, b, e)
                load(UP, b, e)
                load_x(b + 1)
                load(DOWN, b - 1, entry(sp, b - 1, 0, NE - 1))

            step(1)
            with sp.Fori(2, n) as b:
                step(b)
            load(DOWN, n - 1, entry(sp, n - 1, 0, NE - 1))

        @block.gpsimd
        def _(pool):
            pool.sem_inc(y_free, 1)
            n = blocks(pool)
            with pool.Fori(0, n) as b:
                row = entry(pool, b, 1, SLOTS)
                gate(pool, y0_done, b + 1, pool_passed)
                gate(pool, y1_done, b + 1, pool_passed)
                pool.dma_start(io["ys"][bass.ds(row, P), :], y_sb[:]).then_inc(stored, 16)
                pool.wait_ge(stored, 16 * b + 16)
                pool.sem_inc(y_free, 1)

        @block.scalar
        def _(act):
            def split(unit, b, first=False):
                done = products[unit][1]
                for s in range(2):
                    act.wait_ge(raw_in[2 * unit + s], 16 * b + 16)
                    if s == 0 and not first:
                        act.wait_ge(done, b)
                    act.activation(w_hi[unit][:, s * HALF:(s + 1) * HALF], raw[2 * unit + s][:],
                                   ACT.Copy).then_inc(whi, 1)

            def x_split(b):
                act.wait_ge(x_turned, b + 1)
                act.activation(x_hi[:], p_xT[:], ACT.Copy).then_inc(xhi_done, 1)

            def y_out(b):
                act.wait_ge(down_done, b + 1)
                act.wait_ge(y_free, b + 1)
                act.activation(y_sb[:, 0:BANK], p_y[:, 0:BANK], ACT.Copy).then_inc(y0_done, 1)

            def silu(b, first=False):
                act.wait_ge(gate_done, b + 1)
                if not first:
                    act.wait_ge(h_done, b)
                act.activation(act_g[:], p_gate[:], ACT.Silu).then_inc(silu_done, 1)

            n = blocks(act)
            x_split(0)
            split(GATE, 0, first=True)
            split(UP, 0, first=True)
            silu(0, first=True)
            x_split(1)

            def step(b, first=False):
                split(GATE, b)
                if not first:
                    y_out(b - 2)
                split(UP, b)
                act.wait_ge(h_turned, b)
                act.activation(h_hi[:], p_hT[:], ACT.Copy).then_inc(hhi_done, 1)
                silu(b)
                split(DOWN, b - 1, first)
                x_split(b + 1)

            step(1, first=True)
            with act.Fori(2, n) as b:
                step(b)
            y_out(n - 2)
            act.wait_ge(h_turned, n)
            act.activation(h_hi[:], p_hT[:], ACT.Copy).then_inc(hhi_done, 1)
            split(DOWN, n - 1)
            y_out(n - 1)

        @block.vector
        def _(dve):
            def split(unit, b, last=False):
                for s in range(2):
                    dve.wait_ge(whi, order(unit, b, last) + (s + 1))
                    cols = slice(s * HALF, (s + 1) * HALF)
                    dve.tensor_tensor(w_lo[unit][:, cols], raw[2 * unit + s][:], f32(w_hi[unit][:, cols]),
                                      ALU.subtract).then_inc(wlo, 1)

            def x_split(b):
                dve.wait_ge(xhi_done, b + 1)
                dve.tensor_tensor(x_lo[:], p_xT[:], f32(x_hi[:]), ALU.subtract).then_inc(xlo_done, 1)

            def h_split(b):
                dve.wait_ge(hhi_done, b + 1)
                dve.tensor_tensor(h_lo[:], p_hT[:], f32(h_hi[:]), ALU.subtract).then_inc(hlo_done, 1)

            def hidden(b, first=False):
                dve.wait_ge(silu_done, b + 1)
                dve.wait_ge(up_done, b + 1)
                if not first:
                    dve.wait_ge(h_turned, b)
                dve.tensor_tensor(h_sb[:], p_up[:], act_g[:], ALU.mult).then_inc(h_done, 1)

            def y_out(b):
                dve.wait_ge(down_done, b + 1)
                dve.wait_ge(y_free, b + 1)
                dve.tensor_copy(y_sb[:, BANK:D], p_y[:, BANK:D]).then_inc(y1_done, 1)

            n = blocks(dve)
            x_split(0)
            split(GATE, 0)
            split(UP, 0)
            x_split(1)

            def step(b, first=False):
                hidden(b - 1, first)
                split(GATE, b)
                if not first:
                    y_out(b - 2)
                split(UP, b)
                h_split(b - 1)
                split(DOWN, b - 1)
                x_split(b + 1)

            step(1, first=True)
            with dve.Fori(2, n) as b:
                step(b)
            hidden(n - 1)
            y_out(n - 2)
            h_split(n - 1)
            split(DOWN, n - 1, last=True)
            y_out(n - 1)

        @block.tensor
        def _(pe):
            def product(unit, b, x, outs, final=False):
                kt = KE if unit == DOWN else KT
                for k in range(kt):
                    if k % (kt // 2) == 0:
                        pe.wait_ge(wlo, order(unit, b, final) + (2 * k // kt + 1))
                    for i, out in enumerate(outs):
                        cols = slice((k * len(outs) + i) * BANK, (k * len(outs) + i + 1) * BANK)
                        last = split3(pe, out, x[0][:, k, :], x[1][:, k, :], w_hi[unit][:, cols], w_lo[unit][:, cols],
                                      k == 0, k == kt - 1)
                last.then_inc(products[unit][1], 1)

            def turn_x(b):
                pe.wait_ge(x_in, 16 * b + 16)
                if not (isinstance(b, int) and b == 0):
                    pe.wait_ge(xlo_done, b)
                for k in range(KT):
                    last = pe.transpose(p_xT[:, k, :], x_sb[:, k * P:(k + 1) * P], ident[:])
                last.then_inc(x_turned, 1)

            def turn_h(b):
                pe.wait_ge(h_done, b + 1)
                for k in range(KE):
                    last = pe.transpose(p_hT[:, k, :], h_sb[:, k * P:(k + 1) * P], ident[:])
                last.then_inc(h_turned, 1)

            def gate_product(b):
                pe.wait_ge(xlo_done, b + 1)
                if not (isinstance(b, int) and b == 0):
                    pe.wait_ge(silu_done, b)
                product(GATE, b, (x_hi, x_lo), [p_gate[:]])

            def down_product(b, first=False, final=False):
                pe.wait_ge(hlo_done, b + 1)
                if not first:
                    pe.wait_ge(y0_done, b)
                    pe.wait_ge(y1_done, b)
                product(DOWN, b, (h_hi, h_lo), [p_y[:, 0:BANK], p_y[:, BANK:D]], final)

            n = blocks(pe)
            turn_x(0)
            gate_product(0)
            product(UP, 0, (x_hi, x_lo), [p_up[:]])
            turn_x(1)

            def step(b, first=False):
                gate_product(b)
                turn_h(b - 1)
                product(UP, b, (x_hi, x_lo), [p_up[:]])
                turn_x(b + 1)
                down_product(b - 1, first)

            step(1, first=True)
            with pe.Fori(2, n) as b:
                step(b)
            turn_h(n - 1)
            down_product(n - 1, final=True)


def combine(nc, mem, sem, ctx, io, dest, weights):
    x2 = mem.at("cb_x2", 0, [P, NB, D])
    y = [mem.at(f"cb_y{c}", 32768 * (c + 1), [P, NB, D]) for c in range(2)]
    x2_in, y_in, half_done, done, out_stored = (sem("cb_" + n) for n in ("x2_in", "y_in", "half", "done", "out_stored"))

    with nc.Block() as block:
        @block.sync
        def _(sp):
            sp.dma_start(x2[:], io["x2"].rearrange("(b p) d -> p b d", p=P)).then_inc(x2_in, 16)
            for b in range(NB):
                sp.wait_ge(done, b + 1)
                sp.dma_start(io["out"][0][b * P:(b + 1) * P, :], x2[:, b, :]).then_inc(out_stored, 16)
            sp.wait_ge(out_stored, 16 * NB)

        @block.gpsimd
        def _(pool):
            for b in range(NB):
                for c in range(2):
                    pool.indirect_dma_start(y[c][:, b, :], None, io["ys"][0:SLOTS, :],
                                            bass.IndirectOffsetOnAxis(ap=dest[:, c, b:b + 1], axis=0)).then_inc(y_in, 16)

        @block.vector
        def _(dve):
            dve.wait_ge(x2_in, 16)
            dve.wait_ge(y_in, 32 * NB)
            for b in range(NB):
                dve.scalar_tensor_tensor(out=x2[:, b, :], in0=y[0][:, b, :], scalar=weights[:, 0, b:b + 1],
                                         in1=x2[:, b, :], op0=ALU.mult, op1=ALU.add).then_inc(half_done, 1)
                dve.wait_ge(half_done, b + 1)
                dve.scalar_tensor_tensor(out=x2[:, b, :], in0=y[1][:, b, :], scalar=weights[:, 1, b:b + 1],
                                         in1=x2[:, b, :], op0=ALU.mult, op1=ALU.add).then_inc(done, 1)


def program(nc, io, upto=99):
    mem = Memory(nc)
    for name, rows, cols in (("qa", P, SEQ), ("qb", HD + 4, SEQ), ("ka", HD, L), ("kb", HD + 4, L)):
        io[name] = nc.dram_tensor(name + "_scratch", [H, rows, cols], F32R).ap()
    scratch = dict(v=[L, D], part=[KT, P, SEQ], sgb=[KT, P, SEQ],
                   x2=[SEQ, D], xs=[XROWS, D], ys=[XROWS, D])
    io["tab"] = nc.dram_tensor("tab_scratch", [P, 4], I32).ap()
    for name, shape in scratch.items():
        io[name] = nc.dram_tensor(name + "_scratch", shape, F32).ap()
    with ExitStack() as ctx:
        retired = ExitStack()
        first = []

        def sem(name):
            return ctx.enter_context(nc.semaphore(name))

        def early_sem(name):
            if name.endswith("stored"):
                return sem(name)
            first.append(retired.enter_context(nc.semaphore(name)))
            return first[-1]

        io["ident"] = mem.at("ident", mem.size - 512, [P, P])
        io["eps"] = mem.at("eps", mem.size - 576, [P, 1])
        io["one"] = mem.at("one", mem.size - 544, [P, 1])
        io["onesp"] = mem.at("onesp", mem.size - 576 - 4160, [P, L])
        h_hi = mem.at("h_hi", 0, [P, KT, L], F32R)
        h_lo = mem.at("h_lo", 33280, [P, KT, L], F32R)
        with ExitStack() as c:
            norm1(nc, mem, early_sem, c, io, (h_hi, h_lo))
        if upto < 1:
            return
        c_hi = mem.at("c_hi", 66560, [P, KT, SEQ], F32R)
        c_lo = mem.at("c_lo", 99328, [P, KT, SEQ], F32R)
        with ExitStack() as c:
            conv_merge(nc, mem, early_sem, c, io, (h_hi, h_lo), (c_hi, c_lo))
        if upto < 2:
            return
        with ExitStack() as c:
            qkv(nc, mem, sem, c, io, (h_hi, h_lo))
        if upto < 3:
            return
        a_hi = mem.at("a_hi", 0, [P, KT, SEQ], F32R)
        a_lo = mem.at("a_lo", 32768, [P, KT, SEQ], F32R)
        with ExitStack() as c:
            attention(nc, mem, sem, c, io, (a_hi, a_lo))
        if upto < 4:
            return
        m_hi = mem.at("m_hi", 142336, [P, KT, SEQ], F32R)
        m_lo = mem.at("m_lo", 175104, [P, KT, SEQ], F32R)
        with ExitStack() as c:
            merge(nc, mem, sem, c, io, (a_hi, a_lo), (m_hi, m_lo))
        if upto < 5:
            return
        x2n = mem.at("x2n", 73728, [P, NB, D])
        logits = mem.at("logits", 140800, [P, NB, NG + NE])
        with ExitStack() as c:
            residual(nc, mem, sem, c, io, (m_hi, m_lo), x2n, logits, first)
        retired.close()
        if upto < 6:
            return
        dest = mem.at("dest", 207872, [P, 2, NB], I32)
        weights = mem.at("weights", 207936, [P, 2, NB])
        table = mem.at("table", 205824, [1, 4 * P], I32)
        with ExitStack() as c:
            route(nc, mem, sem, c, io, x2n, logits, dest, weights, table)
        if upto < 7:
            return
        with ExitStack() as c:
            experts(nc, mem, sem, c, io, table)
        if upto < 8:
            return
        with ExitStack() as c:
            combine(nc, mem, sem, c, io, dest, weights)


_INS = ['x', 'meta_tokens', 'norm1_g', 'w_in', 'b_forget', 'conv_w', 'w_conv_out', 'q_norm_g', 'k_norm_g',
        'w_att_out', 'w_merge_out', 'norm2_g', 'w_router_group', 'b_router_group', 'w_router_expert',
        'b_router_expert', 'w_exp_gate', 'w_exp_up', 'w_exp_down']


def kernel(**inputs):
    import numpy as _np
    import concourse.bacc as _bacc
    from concourse import mybir as _mybir
    from concourse.bass_utils import run_bass_kernel_spmd as _run

    nc = _bacc.Bacc("TRN2", target_bir_lowering=False, num_devices=1)
    arrays, io = {}, {}
    for name in _INS:
        a = _np.ascontiguousarray(inputs[name])
        arrays[f"in_{name}_dram"] = a
        io[name] = nc.dram_tensor(f"in_{name}_dram", a.shape, _mybir.dt.from_np(a.dtype), kind="ExternalInput").ap()
    io["out"] = nc.dram_tensor("out_0_dram", (1, 1024, 1024), F32, kind="ExternalOutput").ap()
    program(nc, io)
    r = _run(nc, [arrays], core_ids=[0])
    return r.results[0]["out_0_dram"]
```

```python
from contextlib import ExitStack

import concourse.bass as bass
from concourse import mybir

F32 = mybir.dt.float32
F32R = mybir.dt.float32r
BF16 = mybir.dt.bfloat16
I32 = mybir.dt.int32
ALU = mybir.AluOpType
ACT = mybir.ActivationFunctionType
AX = mybir.AxisListType

P = 128
BANK = 512
D = 1024
KT = D // P
SEQ = 1024
NB = SEQ // P
META = 16
L = SEQ + META
H, HD = 16, 64
NG, EPG = 4, 8
NE = NG * EPG
DE = 512
KE = DE // P
EPS = 1e-6
SLOTS = 2 * SEQ
XROWS = SLOTS + P
MAXBLK = SLOTS // P + NE - 1
NEG = -float(2 ** 100)
MROW = 96
COL = dict(B=0, C=D, U=2 * D, Q=3 * D, K=4 * D, V=5 * D, F=6 * D, GA=6 * D + H, GB=7 * D + H)


class Memory:

    def __init__(self, nc):
        self.nc = nc
        self.base = (nc.sbuf_base + 63) // 64 * 64
        self.size = nc.sbuf_top - self.base

    def at(self, name, offset, shape, dtype=F32):
        n = 4
        for s in shape[1:]:
            n *= s
        if dtype == BF16:
            n //= 2
        assert offset + n <= self.size, (name, offset + n, self.size)
        return self.nc.alloc_sbuf_tensor_at(name, shape, dtype, offset=self.base + offset)


def f32(ap):
    return ap.bitcast(F32)


def gate(eng, sem, value, passed):
    eng.wait_ge(sem, value)
    eng.sem_inc(passed, 1)


def split3(eng, out, w_hi, w_lo, x_hi, x_lo, start, stop):
    eng.matmul(out, w_lo, x_hi, start=start, stop=False)
    eng.matmul(out, w_hi, x_lo, start=False, stop=False)
    return eng.matmul(out, w_hi, x_hi, start=False, stop=stop)


def norm1(nc, mem, sem, ctx, io, hT, units):
    h_hi, h_lo = hT
    ring, forget = units
    base = 66560
    x_sb = [mem.at(f"n1_x{i}", base + 4096 * i, [P, D]) for i in range(2)]
    xn = [mem.at(f"n1_xn{i}", base + 8192 + 4096 * i, [P, D]) for i in range(2)]
    g_b = mem.at("n1_g", base + 16384, [P, D])
    sq = mem.at("n1_sq", base + 20480, [P, D])
    stat = mem.at("n1_stat", base + 24576, [P, 8])
    epsc = io["eps"]
    ident = io["ident"]
    pT = [ctx.enter_context(nc.psum_tensor(f"n1_T{i}", [P, KT, P], F32)) for i in range(2)]
    x_in = [sem(f"n1_x_in{i}") for i in range(2)]
    g_in, consts = sem("n1_g_in"), sem("n1_consts")
    squared, rms, recip, xn_done, turned, hi_done, lo_done = (
        sem("n1_" + s) for s in ("squared", "rms", "recip", "xn_done", "turned", "hi", "lo"))
    x_blocks = io["x"].rearrange("b (t p) d -> (b t) p d", p=P)

    def rows(n):
        return META if isinstance(n, int) and n == NB else P

    def hcols(n, r):
        return slice(SEQ, L) if r == META else bass.ds(n * P, P)

    with nc.Block() as block:
        @block.sync
        def _(sp):
            sp.dma_start(g_b[:], io["norm1_g"].partition_broadcast(P)).then_inc(g_in, 16)

            def load(n, s):
                r = rows(n)
                sp.wait_ge(xn_done, n + 1)
                src = io["meta_tokens"] if r == META else x_blocks[bass.ds(n, 1)].rearrange("a p d -> p (a d)")
                sp.dma_start(x_sb[s][0:r, :], src).then_inc(x_in[s], 16)

            load(0, 0)
            with sp.Fori(0, 3) as i:
                load(2 * i + 1, 1)
                load(2 * i + 2, 0)
            load(7, 1)
            load(8, 0)
            w_in = io["w_in"][0]
            forget.load_early(sp, w_in[:, COL["F"]:COL["F"] + P], 0)
            for i, first in enumerate((COL["C"], COL["U"], COL["B"])):
                ring.load_early(sp, w_in[:, first:first + P], i)

        @block.gpsimd
        def _(pool):
            pool.memset(ident[:], 0.0).then_inc(consts, 1)
            pool.memset(io["onesp"][:], 1.0)
            pool.memset(io["one"][:], 1.0)
            pool.memset(epsc[:], EPS).then_inc(consts, 1)
            pool.wait_ge(consts, 2)
            pool.affine_select(out=ident[:], in_=ident[:], compare_op=ALU.not_equal, fill=1.0,
                               base=0, pattern=[[-1, P]], channel_multiplier=1).then_inc(consts, 1)

        @block.scalar
        def _(act):
            def front(n, s):
                r = rows(n)
                act.wait_ge(x_in[s], 16 * ((n + 2 - s) // 2) if isinstance(n, int) else 8 * (n - s) + 16)
                act.activation(sq[0:r, :], x_sb[s][0:r, :], ACT.Square,
                               accum_out=stat[0:r, s:s + 1]).then_inc(squared, 1)
                act.wait_ge(squared, n + 1)
                act.wait_ge(recip, n + 1)
                act.activation(stat[0:r, 2 + s:3 + s], stat[0:r, s:s + 1], ACT.Sqrt,
                               scale=1.0 / D, bias=epsc[0:r, :]).then_inc(rms, 1)

            def back(n, s):
                r = rows(n)
                act.wait_ge(turned, n + 3)
                act.activation(h_hi[:, :, hcols(n, r)], pT[s][:, :, 0:r], ACT.Copy).then_inc(hi_done, 1)

            act.wait_ge(consts, 2)
            front(0, 0)
            with act.Fori(0, 3) as i:
                front(2 * i + 1, 1)
                back(2 * i, 0)
                front(2 * i + 2, 0)
                back(2 * i + 1, 1)
            front(7, 1)
            back(6, 0)
            front(8, 0)
            back(7, 1)
            back(8, 0)
            forget.split_hi(act, 0, 0, 0)
            ring.split_hi(act, 0, 0, 0)
            ring.split_hi(act, 1, 1, 0)

        @block.vector
        def _(dve):
            dve.sem_inc(forget.lo_done, 1)
            dve.sem_inc(ring.lo_done, 3)
            dve.sem_inc(xn_done, 2)
            dve.sem_inc(recip, 2)
            dve.sem_inc(lo_done, 2)

            def front(n, s):
                r = rows(n)
                dve.wait_ge(rms, n + 1)
                dve.reciprocal(stat[0:r, 4 + s:5 + s], stat[0:r, 2 + s:3 + s]).then_inc(recip, 1)
                dve.wait_ge(recip, n + 3)
                dve.wait_ge(turned, n + 1)
                dve.scalar_tensor_tensor(out=xn[s][0:r, :], in0=x_sb[s][0:r, :],
                                         scalar=stat[0:r, 4 + s:5 + s], in1=g_b[0:r, :],
                                         op0=ALU.mult, op1=ALU.mult).then_inc(xn_done, 1)

            def back(n, s):
                r = rows(n)
                dve.wait_ge(hi_done, n + 1)
                dve.tensor_tensor(h_lo[:, :, hcols(n, r)], pT[s][:, :, 0:r],
                                  f32(h_hi[:, :, hcols(n, r)]), ALU.subtract).then_inc(lo_done, 1)

            dve.wait_ge(g_in, 16)
            front(0, 0)
            with dve.Fori(0, 3) as i:
                front(2 * i + 1, 1)
                back(2 * i, 0)
                front(2 * i + 2, 0)
                back(2 * i + 1, 1)
            front(7, 1)
            back(6, 0)
            front(8, 0)
            back(7, 1)
            back(8, 0)
            forget.split_lo(dve, 0, 0)
            ring.split_lo(dve, 0, 0)
            ring.split_lo(dve, 1, 1)

        @block.tensor
        def _(pe):
            pe.sem_inc(forget.used, 1)
            pe.sem_inc(ring.used, 3)
            pe.sem_inc(turned, 2)
            pe.wait_ge(consts, 3)

            def turn(n, s):
                r = rows(n)
                pe.wait_ge(xn_done, n + 3)
                pe.wait_ge(lo_done, n + 1)
                for k in range(KT):
                    last = pe.transpose(pT[s][:, k, 0:r], xn[s][0:r, k * P:(k + 1) * P], ident[0:r, 0:r])
                last.then_inc(turned, 1)

            turn(0, 0)
            with pe.Fori(0, 3) as i:
                turn(2 * i + 1, 1)
                turn(2 * i + 2, 0)
            turn(7, 1)
            turn(8, 0)


class HeadTiles:

    def __init__(self, mem, sem):
        base = 115712
        self.tiles = {}
        for name, rows, cols in (("qa", P, SEQ), ("qb", MROW + 2 * NB, SEQ), ("ka", P, L), ("kb", MROW + 2 * NB, L)):
            self.tiles[name] = [mem.at(f"at_{name}{i}", base + 4160 * i, [rows, cols], F32R) for i in range(2)]
            base += 8320
        self.loaded = [sem(f"at_qk_in{i}") for i in range(2)]
        self.rows_done = sem("at_rows")

    def constant_rows(self, act, ones):
        for par in range(2):
            qb, kb = self.tiles["qb"][par], self.tiles["kb"][par]
            act.activation(qb[HD:MROW, :], ones[HD:MROW, 0:SEQ], ACT.Copy, scale=0.0)
            act.activation(kb[HD:MROW, :], ones[HD:MROW, :], ACT.Copy, scale=0.0)
            last = act.activation(kb[MROW:MROW + 2 * NB, :], ones[MROW:MROW + 2 * NB, :], ACT.Copy)
        last.then_inc(self.rows_done, 1)

    def load(self, pool, io, head, par):
        head = slice(head, head + 1) if isinstance(head, int) else bass.ds(head, 1)
        k_hi = io["ka"][head].rearrange("a d t -> (a d) t").unsqueeze(0).to_broadcast([2, HD, L])
        pool.dma_start(self.tiles["ka"][par][:], k_hi).then_inc(self.loaded[par], 16)
        for name, rows in (("qa", P), ("qb", HD + 4), ("kb", HD + 4)):
            pool.dma_start(self.tiles[name][par][0:rows, :], io[name][head].rearrange("a d t -> (a d) t"))\
                .then_inc(self.loaded[par], 16)


class WeightUnits:

    def __init__(self, mem, sem, name, base, slots, places=None):
        self.slots = slots
        places = places or [base + 4096 * i for i in range(3 * slots)]
        self.raw = [mem.at(f"{name}_raw{i}", places[i], [P, KT, P]) for i in range(slots)]
        self.hi = [mem.at(f"{name}_whi{i}", places[slots + i], [P, KT, P], F32R) for i in range(slots)]
        self.lo = [mem.at(f"{name}_wlo{i}", places[2 * slots + i], [P, KT, P], F32R) for i in range(slots)]
        self.raw_in = [sem(f"{name}_raw_in{i}") for i in range(slots)]
        self.hi_done, self.lo_done, self.used, self.passed = (
            sem(f"{name}_{s}") for s in ("whi", "wlo", "wused", "passed"))

    def load_early(self, sp, source, s):
        sp.dma_start(self.raw[s][:], source.rearrange("(k p) c -> p k c", p=P)).then_inc(self.raw_in[s], 16)

    def load(self, sp, source, n, s):
        gate(sp, self.lo_done, n + 1, self.passed)
        sp.dma_start(self.raw[s][:], source.rearrange("(k p) c -> p k c", p=P)).then_inc(self.raw_in[s], 16)

    def split_hi(self, act, n, s, use):
        act.wait_ge(self.raw_in[s], 16 * use + 16)
        act.wait_ge(self.used, n + 1)
        act.activation(self.hi[s][:], self.raw[s][:], ACT.Copy).then_inc(self.hi_done, 1)

    def split_lo(self, dve, n, s):
        dve.wait_ge(self.hi_done, n + 1)
        dve.tensor_tensor(self.lo[s][:], self.raw[s][:], f32(self.hi[s][:]),
                          ALU.subtract).then_inc(self.lo_done, 1)

    def product(self, pe, n, s, x, outs, cols):
        pe.wait_ge(self.lo_done, n + 1 + self.slots)
        last = None
        for k in range(KT):
            for step, (w, y) in enumerate(((self.lo, x[0]), (self.hi, x[1]), (self.hi, x[0]))):
                for out, c in zip(outs, cols):
                    last = pe.matmul(out, w[s][:, k, :], y[:, k, c], start=(k == 0 and step == 0),
                                     stop=(k == KT - 1 and step == 2))
        last.then_inc(self.used, 1)


def conv_merge(nc, mem, sem, ctx, io, hT, cT, units, w_in_halves):
    h_hi, h_lo = hT
    conv_hi_sb, conv_lo_sb = cT
    base = 132096
    ring, forget = units
    base += 3 * 12288
    c_sb = mem.at("cm_c", base, [P, SEQ + 2])
    z = mem.at("cm_z", base + 4160, [P, SEQ + 2])
    y0 = mem.at("cm_y0", base + 8320, [P, SEQ])
    y1 = mem.at("cm_y1", base + 12416, [P, SEQ])
    cv = mem.at("cm_cv", base + 16512, [P, SEQ])
    sga, part, sgb = c_sb, y0, y1
    fx = mem.at("cm_fx", base + 20608, [H, L])
    fa = mem.at("cm_fa", base + 24768, [H, L])
    cw = mem.at("cm_cw", base + 28928, [P, KT, 3])
    bf = mem.at("cm_bf", base + 29024, [H, 1])
    c_hi = mem.at("cm_fhi", base + 29056, [H, L], F32R)
    c_lo = mem.at("cm_flo", base + 33216, [H, L], F32R)
    ones = io["onesp"]
    out = [ctx.enter_context(nc.psum_tensor(f"cm_o{i}", [P, SEQ], F32)) for i in range(3)]
    mt = [ctx.enter_context(nc.psum_tensor(f"cm_m{i}", [P, BANK], F32)) for i in range(2)]
    halves = [slice(0, BANK), slice(BANK, SEQ)]
    out_of = [[o[:, c] for c in halves] for o in out]
    consts_in = sem("cm_consts")
    evac = [sem(f"cm_evac{i}") for i in range(3)]
    y0_done, y1_done, conv_hi, conv_lo, fchain, f_out, stored = (
        sem("cm_" + s) for s in ("y0", "y1", "conv_hi", "conv_lo", "fchain", "f_out", "stored"))
    sgb_done, part_done, part_stored, sgb_stored, passed, part_free, sgb_free = (
        sem("cm_" + s) for s in ("sgb", "part", "part_stored", "sgb_stored", "pool_passed", "part_free", "sgb_free"))
    w_in, w_conv = io["w_in"][0], io["w_conv_out"][0]

    with nc.Block() as block:
        @block.sync
        def _(sp):
            with nc.allow_non_contiguous_dma(reason="small tables, one element each"):
                sp.dma_start(bf[:], io["b_forget"].rearrange("o h -> h o")).then_inc(consts_in, 16)
                for i in range(3):
                    sp.dma_start(cw[:, :, i], io["conv_w"][0, i].rearrange("(m p) -> p m", p=P)).then_inc(consts_in, 16)
            with sp.Fori(1, KT) as m:
                for s, first in enumerate((COL["C"], COL["U"], COL["B"])):
                    ring.load(sp, w_in[:, bass.ds(m * P + first, P)], 3 * m + s, s)
            with sp.Fori(0, KT) as m:
                ring.load(sp, w_in[:, bass.ds(m * P + COL["GA"], P)], 3 * m + 24, 0)
                ring.load(sp, w_conv[:, bass.ds(m * P, P)], 3 * m + 25, 1)
                ring.load(sp, w_in[:, bass.ds(m * P + COL["GB"], P)], 3 * m + 26, 2)
            sp.wait_ge(stored, 160)
            sp.wait_ge(conv_lo, KT)
            raw, raw_in = w_in_halves
            for half in range(2):
                sp.dma_start(raw[half][:], w_in.rearrange("(k p) c -> p k c", p=P)
                             [:, 4 * half:4 * half + 4, COL["Q"]:COL["Q"] + BANK]).then_inc(raw_in[half], 16)

        @block.gpsimd
        def _(pool):
            pool.wait_ge(fchain, 10)
            one_rows = ones[0:H, :].bitcast(F32R)
            for r, c in enumerate((c_hi, c_lo)):
                pool.dma_start(io["qb"][:, HD + r, :], c[:, 0:SEQ]).then_inc(stored, 16)
                pool.dma_start(io["qb"][:, HD + 2 + r, :], one_rows[:, 0:SEQ]).then_inc(stored, 16)
                pool.dma_start(io["kb"][:, HD + r, :], one_rows).then_inc(stored, 16)
            for r, c in enumerate((fa, fx)):
                c = c[:].bitcast(F32R)
                pool.dma_start(io["kb"][:, HD + 2 + r, 0:META], c[:, SEQ:L]).then_inc(stored, 16)
                pool.dma_start(io["kb"][:, HD + 2 + r, META:L], c[:, 0:SEQ]).then_inc(stored, 16)
            with pool.Fori(0, KT) as m:
                gate(pool, part_done, m + 2, passed)
                pool.dma_start(io["part"][bass.ds(m, 1)].rearrange("a p t -> p (a t)"), part[:]).then_inc(part_stored, 16)
                gate(pool, sgb_done, m + 2, passed)
                pool.dma_start(io["sgb"][bass.ds(m, 1)].rearrange("a p t -> p (a t)"), sgb[:]).then_inc(sgb_stored, 16)
                pool.wait_ge(part_stored, 16 * m + 16)
                pool.sem_inc(part_free, 1)
                pool.wait_ge(sgb_stored, 16 * m + 16)
                pool.sem_inc(sgb_free, 1)
            pool.wait_ge(stored, 160)

        @block.scalar
        def _(act):
            act.wait_ge(fchain, 1)
            act.activation(fa[:], fa[:], ACT.Exp, scale=-1.0).then_inc(fchain, 1)
            act.wait_ge(fchain, 2)
            act.activation(fa[:], fa[:], ACT.Ln, bias=io["one"][0:H, :]).then_inc(fchain, 1)
            act.sem_inc(sgb_free, 1)
            act.sem_inc(sgb_done, 1)
            act.wait_ge(consts_in, 64)

            with act.Fori(0, KT) as m:
                ring.split_hi(act, 3 * m + 2, 2, m)
                act.wait_ge(ring.used, 3 * m + 4)
                act.wait_ge(evac[1], m + 1)
                act.activation(c_sb[:, 0:2], mt[0][:, 0:2], ACT.Copy)
                act.activation(c_sb[:, 2:], out[0][:], ACT.Copy).then_inc(evac[0], 1)
                ring.split_hi(act, 3 * m + 3, 0, m + 1)
                act.wait_ge(evac[1], m + 2)
                act.activation(y0[:], z[:, 0:SEQ], ACT.Copy,
                               scale=cw[:, bass.ds(m, 1), 0]).then_inc(y0_done, 1)
                ring.split_hi(act, 3 * m + 4, 1, m + 1)
                act.wait_ge(evac[2], m + 2)
                act.activation(conv_hi_sb[:, bass.ds(m, 1), :], cv[:], ACT.Copy).then_inc(conv_hi, 1)

            def gates(m, more):
                ring.split_hi(act, 3 * m + 26, 2, m + 8)
                act.wait_ge(ring.used, 3 * m + 28)
                act.wait_ge(evac[1], m + 9)
                act.activation(sga[:, 0:SEQ], out[0][:], ACT.Sigmoid).then_inc(evac[0], 1)
                if more:
                    ring.split_hi(act, 3 * m + 27, 0, m + 9)
                    ring.split_hi(act, 3 * m + 28, 1, m + 9)
                act.wait_ge(ring.used, 3 * m + 30)
                act.wait_ge(sgb_free, m + 1)
                act.activation(sgb[:], out[2][:], ACT.Sigmoid).then_inc(sgb_done, 1)

            with act.Fori(0, KT - 1) as m:
                gates(m, True)
            gates(KT - 1, False)

        @block.vector
        def _(dve):
            dve.sem_inc(evac[0], 1)
            dve.sem_inc(evac[1], 1)
            dve.sem_inc(part_free, 1)
            dve.sem_inc(part_done, 1)
            dve.wait_ge(forget.used, 2)
            dve.wait_ge(consts_in, 64)
            dve.tensor_scalar(fx[:, SEQ:L], mt[1][0:H, 0:META], bf[:], None, ALU.add)
            dve.tensor_scalar(fx[:, 0:SEQ], out[2][0:H, :], bf[:], None, ALU.add).then_inc(evac[2], 1)
            dve.wait_ge(evac[2], 1)
            dve.scalar_tensor_tensor(out=fa[:], in0=fx[:], scalar=-1.0, in1=fx[:],
                                     op0=ALU.mult, op1=ALU.max).then_inc(fchain, 1)
            dve.wait_ge(fchain, 3)
            dve.scalar_tensor_tensor(out=fx[:], in0=fx[:], scalar=0.0, in1=fa[:],
                                     op0=ALU.min, op1=ALU.subtract).then_inc(fchain, 1)
            dve.wait_ge(fchain, 4)
            dve.tensor_tensor_scan(fa[:, SEQ:L], ones[0:H, 0:META], fx[:, SEQ:L], 0.0,
                                   ALU.mult, ALU.add).then_inc(f_out, 1)
            dve.wait_ge(f_out, 1)
            dve.tensor_tensor_scan(fa[:, 0:SEQ], ones[0:H, 0:SEQ], fx[:, 0:SEQ], fa[:, L - 1:L],
                                   ALU.mult, ALU.add).then_inc(fchain, 1)
            dve.wait_ge(fchain, 5)
            dve.tensor_copy(c_hi[:], fa[:]).then_inc(fchain, 1)
            dve.wait_ge(fchain, 6)
            dve.tensor_tensor(c_lo[:], fa[:], f32(c_hi[:]), ALU.subtract).then_inc(fchain, 1)
            dve.wait_ge(fchain, 7)
            dve.sem_inc(fchain, 1)
            dve.tensor_scalar(fa[:].bitcast(F32R), f32(c_hi[:]), -1.0, None, ALU.mult).then_inc(fchain, 1)
            dve.tensor_scalar(fx[:].bitcast(F32R), f32(c_lo[:]), -1.0, None, ALU.mult).then_inc(fchain, 1)

            with dve.Fori(0, KT) as m:
                ring.split_lo(dve, 3 * m + 2, 2)
                ring.split_lo(dve, 3 * m + 3, 0)
                dve.wait_ge(ring.used, 3 * m + 5)
                dve.wait_ge(evac[0], m + 2)
                dve.tensor_tensor(z[:, 0:2], mt[1][:, 0:2], c_sb[:, 0:2], ALU.mult)
                dve.tensor_tensor(z[:, 2:], out[1][:], c_sb[:, 2:], ALU.mult).then_inc(evac[1], 1)
                dve.wait_ge(evac[1], m + 2)
                dve.wait_ge(y0_done, m + 1)
                dve.scalar_tensor_tensor(out=y1[:], in0=z[:, 1:SEQ + 1], scalar=cw[:, bass.ds(m, 1), 1],
                                         in1=y0[:], op0=ALU.mult, op1=ALU.add).then_inc(y1_done, 1)
                dve.wait_ge(y1_done, 2 * m + 1)
                dve.scalar_tensor_tensor(out=y1[:], in0=z[:, 2:SEQ + 2], scalar=cw[:, bass.ds(m, 1), 2],
                                         in1=y1[:], op0=ALU.mult, op1=ALU.add).then_inc(y1_done, 1)
                ring.split_lo(dve, 3 * m + 4, 1)
                dve.wait_ge(y1_done, 2 * m + 2)
                dve.wait_ge(ring.used, 3 * m + 6)
                dve.tensor_tensor(cv[:], out[2][:], y1[:], ALU.mult).then_inc(evac[2], 1)
                dve.wait_ge(conv_hi, m + 1)
                dve.tensor_tensor(conv_lo_sb[:, bass.ds(m, 1), :], cv[:], f32(conv_hi_sb[:, bass.ds(m, 1), :]),
                                  ALU.subtract).then_inc(conv_lo, 1)

            def gated(m, more):
                ring.split_lo(dve, 3 * m + 26, 2)
                if more:
                    ring.split_lo(dve, 3 * m + 27, 0)
                dve.wait_ge(ring.used, 3 * m + 29)
                dve.wait_ge(evac[0], m + 10)
                dve.wait_ge(part_free, m + 1)
                dve.tensor_tensor(part[:], out[1][:], sga[:, 0:SEQ], ALU.mult).then_inc(part_done, 1)
                dve.wait_ge(part_done, m + 2)
                dve.sem_inc(evac[1], 1)
                if more:
                    ring.split_lo(dve, 3 * m + 28, 1)

            with dve.Fori(0, KT - 1) as m:
                gated(m, True)
            gated(KT - 1, False)

        @block.tensor
        def _(pe):
            meta2 = slice(L - 2, L)
            forget.product(pe, 0, 0, hT, [out[2][:, c] for c in halves] + [mt[1][:, 0:META]],
                           halves + [slice(SEQ, L)])
            with pe.Fori(0, KT) as m:
                pe.wait_ge(evac[0], m + 1)
                ring.product(pe, 3 * m, 0, hT, out_of[0] + [mt[0][:, 0:2]], halves + [meta2])
                pe.wait_ge(evac[1], m + 1)
                pe.wait_ge(evac[2], m + 1)
                ring.product(pe, 3 * m + 1, 1, hT, out_of[1] + [mt[1][:, 0:2]], halves + [meta2])
                ring.product(pe, 3 * m + 2, 2, hT, out_of[2], halves)
            pe.wait_ge(conv_lo, KT)
            with pe.Fori(0, KT) as m:
                pe.wait_ge(evac[0], m + 9)
                ring.product(pe, 3 * m + 24, 0, hT, out_of[0], halves)
                pe.wait_ge(evac[1], m + 9)
                ring.product(pe, 3 * m + 25, 1, cT, out_of[1], halves)
                pe.wait_ge(evac[2], 9)
                pe.wait_ge(sgb_done, m + 1)
                ring.product(pe, 3 * m + 26, 2, hT, out_of[2], halves)


def qkv(nc, mem, sem, ctx, io, hT, heads, w_in_halves):
    h_hi, h_lo = hT
    HPC = BANK // HD
    CT = BANK // P
    base = 66560
    raw, raw_in = w_in_halves
    w_hi = mem.at("qk_whi", base + 16384, [P, KT, BANK], F32R)
    w_lo = mem.at("qk_wlo", base + 32768, [P, KT, BANK], F32R)
    base += 49152
    t_hi = mem.at("qk_thi", base, [P, 2, CT, L], F32R)
    t_lo = mem.at("qk_tlo", base + 33280, [P, 2, CT, L], F32R)
    base = 66560
    qn = [mem.at(f"qk_qn{i}", base + 2048 * i, [P, BANK]) for i in range(3)]
    v_sb = [mem.at(f"qk_v{i}", base + 6144 + 2048 * i, [P, BANK]) for i in range(3)]
    sq = mem.at("qk_sq", base + 12288, [P, BANK])
    ss = mem.at("qk_ss", base + 14336, [P, HPC])
    rms = mem.at("qk_rms", base + 14400, [P, HPC])
    rstd = mem.at("qk_rstd", base + 14464, [P, HPC])
    gain = mem.at("qk_gain", base + 14528, [P, 4])
    ident = io["ident"]
    mm = [ctx.enter_context(nc.psum_tensor(f"qk_mm{i}", [P, BANK], F32)) for i in range(3)]
    pT = [ctx.enter_context(nc.psum_tensor(f"qk_T{i}", [P, CT, P], F32)) for i in range(3)]
    names = ("whi", "wlo", "w_used", "sp_passed", "pool_passed", "mm_done", "sq_done", "summed", "rms_done",
             "rstd_done", "freed", "turned", "t_hi_done", "evac", "gains_in", "gains", "stored", "v_done", "pe_passed")
    (whi, wlo, w_used, sp_passed, pool_passed, mm_done, sq_done, summed, rms_done,
     rstd_done, freed, turned, t_hi_done, evac, gains_in, gains, stored, v_done, pe_passed) = (sem("qk_" + n) for n in names)
    v_stored = [sem(f"qk_v_stored{i}") for i in range(3)]
    v_free, t_free, masks, tiles_free = (sem("qk_" + n) for n in ("v_free", "t_free", "masks", "tiles_free"))
    w_cols = io["w_in"][0].rearrange("(k p) c -> p k c", p=P)

    PASSES = dict(q=(0, 0, NB), k=(2, 2 * NB, NB + 1), v=(4, 2 * NB + 2 * (NB + 1), NB + 1))

    def rows(t):
        return META if t == NB else P

    def toks(t):
        return slice(t * P, t * P + rows(t))

    def turned_cols(tile, c, t, gcol):
        first = t * P if gcol == 2 else META + t * P if t < NB else 0
        return tile[:, bass.ds(c, 1), :, first:first + rows(t)].rearrange("p a ct t -> p (a ct) t")

    with nc.Block() as block:
        @block.sync
        def _(sp):
            with nc.allow_non_contiguous_dma(reason="64-element gain columns"):
                for c, g in enumerate(("q_norm_g", "k_norm_g")):
                    for h in range(2):
                        sp.dma_start(gain[h * HD:(h + 1) * HD, c:c + 1],
                                     io[g].rearrange("o d -> d o")).then_inc(gains_in, 16)
            def load(c, c0, first):
                for half in range(2):
                    gate(sp, wlo, 8 * c + (8 * c0 + 4 * half + 4), sp_passed)
                    sp.dma_start(raw[half][:], w_cols[:, 4 * half:4 * half + 4,
                                                      bass.ds(c * BANK + COL[first], BANK)])\
                      .then_inc(raw_in[half], 16)

            load(1, 0, "Q")
            for c0, first in ((2, "K"), (4, "V")):
                with sp.Fori(0, 2) as c:
                    load(c, c0, first)

        @block.gpsimd
        def _(pool):
            eye, mask, maskT, sel = (io[n] for n in ("eye", "mask", "maskT", "sel"))
            for tile in (eye, mask, maskT):
                pool.memset(tile[:], 0.0).then_inc(masks, 1)
            pool.memset(sel[:], 1.0).then_inc(masks, 1)
            pool.wait_ge(masks, 4)
            pool.affine_select(out=eye[:], in_=eye[:], compare_op=ALU.not_equal, fill=1.0, base=0,
                               pattern=[[-1, P]], channel_multiplier=1)
            pool.affine_select(out=mask[:], in_=mask[:], compare_op=ALU.is_ge, fill=NEG, base=0,
                               pattern=[[-1, P]], channel_multiplier=1)
            pool.affine_select(out=maskT[:], in_=maskT[:], compare_op=ALU.is_ge, fill=NEG, base=0,
                               pattern=[[1, P]], channel_multiplier=-1)
            pool.affine_select(out=sel[:], in_=sel[:], compare_op=ALU.is_ge, fill=0.0, base=-MROW,
                               pattern=[[-2, NB]], channel_multiplier=1).then_inc(masks, 1)
            pool.wait_ge(masks, 5)
            pool.affine_select(out=sel[:], in_=sel[:], compare_op=ALU.is_ge, fill=0.0, base=MROW + 1,
                               pattern=[[2, NB]], channel_multiplier=-1)
            for name in ("q", "k"):
                n0, g0, blocks = PASSES[name]
                width = SEQ if name == "q" else L
                with pool.Fori(0, 2) as c:
                    gate(pool, evac, blocks * c + (g0 + blocks + 2), pool_passed)
                    places = ((("qa", 0, t_hi), ("qa", HD, t_lo), ("qb", 0, t_hi)) if name == "q" else
                              (("ka", 0, t_hi), ("kb", 0, t_lo)))
                    for part, row, tile in places:
                        by_half = io[part][:, row:row + HD, :].rearrange("(c ct h) d t -> h c d ct t", c=2, h=2)
                        for h in range(2):
                            pool.dma_start(by_half[h, bass.ds(c, 1)].rearrange("a d ct t -> (a d) ct t"),
                                           tile[h * HD:(h + 1) * HD, bass.ds(c, 1), :, 0:width]
                                           .rearrange("p a ct t -> p (a ct) t")).then_inc(stored, 16)
                    if name == "q":
                        pool.wait_ge(stored, 96 * c + 96)
                        pool.sem_inc(t_free, 1)
            pool.wait_ge(stored, 320)
            pool.sem_inc(tiles_free, 1)
            for c in range(2):
                for t in range(NB + 1):
                    u = 9 * c + t
                    if c == 1 and t == 2:
                        pool.wait_ge(heads.rows_done, 1)
                        for par in range(2):
                            heads.load(pool, io, par, par)
                    pool.wait_ge(v_done, u + 1)
                    pool.dma_start(io["v"][toks(t), c * BANK:(c + 1) * BANK],
                                   v_sb[t % 3][0:rows(t), :]).then_inc(v_stored[t % 3], 16)
                    if u >= 1:
                        pool.wait_ge(v_stored[(t - 1) % 3], 16 * (3 * ((u - 1) // 9) + ((u - 1) % 9) // 3 + 1))
                        pool.sem_inc(v_free, 1)
            pool.wait_ge(v_stored[2], 96)

        def split_hi(act, n, blocks_before):
            for k in range(KT):
                if k % 4 == 0:
                    act.wait_ge(raw_in[k // 4], 16 * n + 16)
                if k < KT - 1:
                    act.wait_ge(w_used, 7 * n + (k + 1))
                elif blocks_before is not None:
                    act.wait_ge(mm_done, blocks_before)
                act.activation(w_hi[:, k, :], raw[k // 4][:, k % 4, :], ACT.Copy).then_inc(whi, 1)

        def split_lo(dve, n):
            for k in range(KT):
                dve.wait_ge(whi, 8 * n + (k + 1))
                dve.tensor_tensor(w_lo[:, k, :], raw[k // 4][:, k % 4, :], f32(w_hi[:, k, :]),
                                  ALU.subtract).then_inc(wlo, 1)

        @block.scalar
        def _(act):
            def front(g, t):
                r = rows(t)
                act.wait_ge(mm_done, g + (t + 1))
                act.wait_ge(summed, g + (t + 1))
                act.activation(sq[0:r, :], mm[t % 3][0:r, :], ACT.Square).then_inc(sq_done, 1)
                act.wait_ge(summed, g + (t + 2))
                act.activation(rms[0:r, :], ss[0:r, :], ACT.Sqrt, scale=1.0 / HD,
                               bias=io["eps"][0:r, :]).then_inc(rms_done, 1)

            def back(g, t, c, gcol):
                act.wait_ge(turned, g + (t + 3))
                act.activation(turned_cols(t_hi, c, t, gcol), pT[t % 3][:, :, 0:rows(t)], ACT.Copy,
                               scale=gain[:, gcol:gcol + 1]).then_inc(t_hi_done, 1)

            split_hi(act, 0, None)
            act.wait_ge(gains, 1)
            for gcol, name in ((2, "q"), (1, "k")):
                n0, g0, blocks = PASSES[name]
                with act.Fori(0, 2) as c:
                    g = blocks * c + g0
                    if name == "k":
                        act.wait_ge(t_free, c + 1)
                    for t in range(blocks - 1):
                        front(g, t)
                        if t:
                            back(g, t - 1, c, gcol)
                    split_hi(act, c + (n0 + 1), g + blocks)
                    front(g, blocks - 1)
                    back(g, blocks - 2, c, gcol)
                    back(g, blocks - 1, c, gcol)
            n0, g0, blocks = PASSES["v"]
            for c in range(2):
                for t in range(blocks):
                    if c == 1 and t == 1:
                        act.wait_ge(tiles_free, 1)
                        heads.constant_rows(act, io["onesp"])
                    if c == 0 and t == blocks - 1:
                        split_hi(act, n0 + 1, g0 + blocks)
                    u = blocks * c + t
                    act.wait_ge(mm_done, g0 + u + 1)
                    if u >= 3:
                        act.wait_ge(v_free, u - 2)
                    act.activation(v_sb[t % 3][0:rows(t), :], mm[t % 3][0:rows(t), :],
                                   ACT.Copy).then_inc(v_done, 1)

        @block.vector
        def _(dve):
            dve.sem_inc(wlo, 8)
            dve.sem_inc(summed, 1)
            dve.sem_inc(freed, 2)
            split_lo(dve, 0)
            dve.wait_ge(gains_in, 64)
            dve.tensor_scalar(gain[:, 2:3], gain[:, 0:1], HD ** -0.5, None, ALU.mult).then_inc(gains, 1)

            def norm(g, t):
                r = rows(t)
                dve.wait_ge(sq_done, g + (t + 1))
                dve.tensor_reduce(ss[0:r, :], sq[0:r, :].rearrange("p (h d) -> p h d", d=HD), AX.X,
                                  ALU.add).then_inc(summed, 1)
                dve.wait_ge(rms_done, g + (t + 1))
                dve.reciprocal(rstd[0:r, :], rms[0:r, :]).then_inc(rstd_done, 1)
                dve.wait_ge(rstd_done, g + (t + 1))
                dve.wait_ge(turned, g + (t + 1))
                dve.tensor_tensor(qn[t % 3][0:r, :].rearrange("p (h d) -> p h d", d=HD),
                                  mm[t % 3][0:r, :].rearrange("p (h d) -> p h d", d=HD),
                                  rstd[0:r, :].unsqueeze(2).to_broadcast([r, HPC, HD]),
                                  ALU.mult).then_inc(freed, 1)

            def back(g, t, c, gcol):
                dve.wait_ge(t_hi_done, g + (t + 1))
                dve.scalar_tensor_tensor(out=turned_cols(t_lo, c, t, gcol), in0=pT[t % 3][:, :, 0:rows(t)],
                                         scalar=gain[:, gcol:gcol + 1], in1=f32(turned_cols(t_hi, c, t, gcol)),
                                         op0=ALU.mult, op1=ALU.subtract).then_inc(evac, 1)

            dve.sem_inc(evac, 2)
            dve.wait_ge(gains, 1)
            for gcol, name in ((2, "q"), (1, "k")):
                n0, g0, blocks = PASSES[name]
                with dve.Fori(0, 2) as c:
                    g = blocks * c + g0
                    for t in range(blocks - 1):
                        norm(g, t)
                        if t:
                            back(g, t - 1, c, gcol)
                    split_lo(dve, c + (n0 + 1))
                    norm(g, blocks - 1)
                    back(g, blocks - 2, c, gcol)
                    back(g, blocks - 1, c, gcol)
            split_lo(dve, 5)

        @block.tensor
        def _(pe):
            pe.sem_inc(w_used, 7)
            pe.sem_inc(turned, 2)

            def product(n, g, t, last_block, v=None):
                r = rows(t)
                if v is None:
                    pe.wait_ge(freed, g + (t + 1))
                else:
                    pe.wait_ge(freed, PASSES["v"][1] + (2 if v >= 2 else 1))
                    if v >= 2:
                        pe.wait_ge(v_done, v - 1)
                for k in range(KT):
                    if t == 0:
                        pe.wait_ge(wlo, 8 * n + (k + 9))
                    x_hi, x_lo = h_hi[:, k, toks(t)], h_lo[:, k, toks(t)]
                    pe.matmul(mm[t % 3][0:r, :], x_hi, w_lo[:, k, :], start=(k == 0), stop=False)
                    pe.matmul(mm[t % 3][0:r, :], x_lo, w_hi[:, k, :], start=False, stop=False)
                    last = pe.matmul(mm[t % 3][0:r, :], x_hi, w_hi[:, k, :], start=False, stop=(k == KT - 1))
                    if t == last_block and k < KT - 1:
                        last.then_inc(w_used, 1)
                last.then_inc(mm_done, 1)

            def turn(g, t):
                r = rows(t)
                pe.wait_ge(freed, g + (t + 3))
                pe.wait_ge(evac, g + (t + 1))
                if r < P:
                    pe.sem_inc(pe_passed, 1)
                for ct in range(CT):
                    last = pe.transpose(pT[t % 3][:, ct, 0:r], qn[t % 3][0:r, ct * P:(ct + 1) * P],
                                        ident[0:r, 0:r])
                last.then_inc(turned, 1)

            behind = None
            for name in ("q", "k"):
                n0, g0, blocks = PASSES[name]
                for c in range(2):
                    for t in range(blocks):
                        product(c + n0, blocks * c + g0, t, blocks - 1)
                        if behind:
                            turn(*behind)
                        behind = (blocks * c + g0, t)
            n0, g0, blocks = PASSES["v"]
            for c in range(2):
                for t in range(blocks):
                    product(n0 + c, g0 + blocks * c, t, blocks - 1, v=blocks * c + t)
                    if behind:
                        turn(*behind)
                        behind = None


def attention(nc, mem, sem, ctx, io, aT, heads, merge_units):
    a_hi, a_lo = aT
    QB = BANK // P
    CROW = HD
    MR = 2 * NB
    base = 65536
    qa, qb, ka, kb_sb = (heads.tiles[n] for n in ("qa", "qb", "ka", "kb"))
    qk_in = heads.loaded
    v_sb = [mem.at(f"at_v{i}", base + 4608 * i, [P, NB + 1, P]) for i in range(2)]
    base += 9216
    pt_sb = [mem.at(f"at_pt{i}", base + 2048 * i, [P, BANK]) for i in range(4)]
    base += 8192
    o_raw, sums = ([mem.at(f"at_{n}{c}", base + 4096 * k + 2048 * c, [P, BANK]) for c in range(2)]
                   for k, n in enumerate(("raw", "sums")))
    o_sb = [mem.at(f"at_out{c}", base + 8192 + 2048 * c, [P, BANK]) for c in range(2)]
    base += 12288
    top3 = mem.at("at_top3", base, [P, NB, 3])
    top = mem.at("at_top", base + 96, [P, NB])
    ntop_hi = mem.at("at_ntop_hi", base + 128, [P, NB], F32R)
    nt = mem.at("at_nt", base + 160, [P, MROW + MR])
    eye, mask, maskT, sel = (io[n] for n in ("eye", "mask", "maskT", "sel"))
    ident = io["ident"]
    ps = [ctx.enter_context(nc.psum_tensor(f"at_s{i}", [P, BANK], F32)) for i in range(2)]
    pst = [ctx.enter_context(nc.psum_tensor(f"at_st{i}", [P, BANK], F32)) for i in range(3)]
    po = [ctx.enter_context(nc.psum_tensor(f"at_o{c}", [P, BANK], F32)) for c in range(2)]
    pm = ctx.enter_context(nc.psum_tensor("at_m", [P, BANK], F32))
    v_in = [sem(f"at_v_in{i}") for i in range(2)]
    names = ("consts", "s_done", "max_done", "chain", "nt_done", "m_turned", "m_done", "st_done",
             "exp_done", "pv_done", "o_done", "inverted", "divided", "o_hi", "o_lo", "sp_passed", "pool_passed", "pe_passed")
    (consts, s_done, max_done, chain, nt_done, m_turned, m_done, st_done,
     exp_done, pv_done, o_done, inverted, divided, o_hi, o_lo, sp_passed, pool_passed, pe_passed) = (sem("at_" + n) for n in names)

    BLOCKS = [(c, kb) for c in range(2) for kb in [*range(QB * (c + 1)), NB]]
    NBL = len(BLOCKS)
    HALF0 = QB + 1
    PIECES = []
    for i in reversed(range(NB)):
        n = META + P * (i + 1)
        parts = -(-n // BANK)
        size = -(-n // parts // 8) * 8
        for q in range(parts):
            PIECES.append((i, q, q * size, min(n, (q + 1) * size) - q * size))
    NPC = len(PIECES)
    assert NPC == NBL and NPC % 2 == 0 and NBL % 3 == 2
    FIRST_PIECES = 6
    assert FIRST_PIECES + NPC // 2 == NBL - 1
    LAG = 3
    CREDIT = 2 * NBL

    def geometry(c, kb):
        first = max(0, kb - QB * c) if kb < NB else 0
        return slice(P * first, BANK), (META if kb == NB else P), (0 if kb == NB else META + P * kb)

    def at(hp, par, n=0):
        return 2 * NBL * hp + (NBL * par + n)

    def need(eng, s, value):
        if not isinstance(value, int) or value > 0:
            eng.wait_ge(s, value)

    def pieces_of(n):
        first = 2 * (n - FIRST_PIECES)
        return range(first, first + 2) if 0 <= first < NPC else ()

    def pair_before(hp):
        return not isinstance(hp, int) or hp > 0

    def after(hp, par):
        return (hp, 1) if par == 0 else (hp + 1, 0)

    def before(hp, par):
        return (hp, 0) if par == 1 else (hp - 1, 1)

    def run(eng, head):
        head(0, 0, first=True)
        head(0, 1)
        with eng.Fori(1, H // 2 - 1) as hp:
            head(hp, 0)
            head(hp, 1)
        head(H // 2 - 1, 0)
        head(H // 2 - 1, 1, last=True)

    with nc.Block() as block:
        @block.sync
        def _(sp):
            with sp.Fori(0, H // 2) as hp:
                for par in range(2):
                    gate(sp, pv_done, at(hp, par - 1) + CREDIT, sp_passed)
                    v = io["v"][:, bass.ds(hp * P + par * HD, HD)]
                    cols = slice(par * HD, (par + 1) * HD)
                    sp.dma_start(v_sb[par][:, 0:NB, cols], v[0:SEQ].rearrange("(b p) d -> p b d", p=P))\
                      .then_inc(v_in[par], 16)
                    sp.dma_start(v_sb[par][0:META, NB, cols], v[SEQ:L]).then_inc(v_in[par], 16)
            for m in range(2):
                merge_units.load_early(sp, io["w_att_out"][0][:, m * P:(m + 1) * P], m)

        @block.gpsimd
        def _(pool):
            def load(hp, par):
                gate(pool, st_done, at(hp, par - 1) + CREDIT, pool_passed)
                heads.load(pool, io, 2 * hp + par, par)

            def head(hp, par, first=False, last=False):
                if not (first or last):
                    load(*after(hp, par))

            run(pool, head)

        @block.scalar
        def _(act):
            def exp(hp, par, n):
                c, kb = BLOCKS[n]
                cols, r, _ = geometry(c, kb)
                act.wait_ge(st_done, at(hp, par, n) + (CREDIT + 1))
                act.wait_ge(pv_done, at(hp, par, n) + (CREDIT - 3))
                act.activation(pt_sb[(NBL * par + n) % 4][0:r, cols], pst[n % 3][0:r, cols],
                               ACT.Exp).then_inc(exp_done, 1)

            def copy_out(hp, par, c):
                act.wait_ge(pv_done, at(hp, par, NBL if c else HALF0) + CREDIT)
                if par == 0:
                    need(act, divided, 2 * hp + (c - 1))
                o, other = slice(par * HD, (par + 1) * HD), slice((1 - par) * HD, (2 - par) * HD)
                act.activation(o_raw[c][o, :], po[c][o, :], ACT.Copy).then_inc(o_done, 1)
                act.activation(sums[c][o, :], po[c][other, :], ACT.Copy).then_inc(o_done, 1)

            def out_hi(hp, c):
                act.wait_ge(divided, 2 * hp + (c + 1))
                act.activation(a_hi[:, bass.ds(hp, 1), c * BANK:(c + 1) * BANK],
                               o_sb[c][:].unsqueeze(1), ACT.Copy).then_inc(o_hi, 1)

            def head(hp, par, first=False, last=False):
                for n in range(NBL):
                    exp(hp, par, n)
                    if n == 5 and not first:
                        copy_out(*before(hp, par), 1)
                    if n == HALF0 + LAG:
                        copy_out(hp, par, 0)
                    if n == 4 and pair_before(hp):
                        out_hi(hp - 1, par)

            run(act, head)
            merge_units.split_hi(act, 0, 0, 0)
            copy_out(H // 2 - 1, 1, 1)
            out_hi(H // 2 - 1, 0)
            out_hi(H // 2 - 1, 1)

        @block.vector
        def _(dve):
            dve.sem_inc(o_lo, 2)
            dve.sem_inc(merge_units.lo_done, 2)
            dve.memset(top3[:], NEG).then_inc(chain, 1)
            dve.memset(nt[:], 0.0).then_inc(chain, 1)
            for par in range(2):
                dve.memset(v_sb[par][:, :, (1 - par) * HD:(2 - par) * HD], 1.0).then_inc(consts, 1)
            dve.wait_ge(chain, 2)

            def piece(hp, par, p):
                i, q, _, width = PIECES[p]
                dve.wait_ge(s_done, at(hp, par, p) + 1)
                dve.tensor_reduce(top3[:, i, q:q + 1], ps[p % 2][:, 0:width], AX.X, ALU.max).then_inc(max_done, 1)

            def maxima(hp, par):
                g = 8 * hp + 4 * par
                pairs = nt[:, MROW:].rearrange("p (i two) -> p two i", two=2)
                dve.wait_ge(max_done, at(hp, par, NPC))
                dve.wait_ge(chain, g + 2)
                dve.tensor_reduce(top[:], top3[:], AX.X, ALU.max).then_inc(chain, 1)
                dve.wait_ge(chain, g + 3)
                dve.tensor_scalar(ntop_hi[:], top[:], -1.0, None, ALU.mult).then_inc(chain, 1)
                dve.wait_ge(chain, g + 4)
                dve.tensor_copy(pairs[:, 0, :], f32(ntop_hi[:])).then_inc(chain, 1)
                dve.scalar_tensor_tensor(out=pairs[:, 1, :], in0=top[:], scalar=-1.0, in1=f32(ntop_hi[:]),
                                         op0=ALU.mult, op1=ALU.subtract).then_inc(chain, 1)
                dve.wait_ge(chain, g + 6)
                dve.sem_inc(nt_done, 1)

            def spread(hp, par):
                dve.wait_ge(m_turned, 2 * hp + (par + 1))
                rows = slice(MROW, MROW + MR)
                dve.tensor_tensor(qb[par][rows, :].rearrange("p (i t) -> p i t", t=P),
                                  pm[rows, 0:P].unsqueeze(1).to_broadcast([MR, NB, P]),
                                  sel[rows, :].unsqueeze(2).to_broadcast([MR, NB, P]), ALU.mult).then_inc(m_done, 1)

            def invert(hp, c, quarter):
                if quarter == 0:
                    dve.wait_ge(o_done, 8 * hp + (2 * c + 6))
                cols = slice(quarter * P, (quarter + 1) * P)
                dve.reciprocal(sums[c][:, cols], sums[c][:, cols]).then_inc(inverted, 1)

            def divide(hp, c):
                dve.wait_ge(inverted, 8 * hp + (4 * c + 4))
                dve.wait_ge(o_lo, 2 * hp + (c + 1))
                dve.tensor_tensor(o_sb[c][:], o_raw[c][:], sums[c][:], ALU.mult).then_inc(divided, 1)

            def out_lo(hp, c):
                dve.wait_ge(o_hi, 2 * hp + (c + 1))
                where = (slice(0, P), bass.ds(hp, 1), slice(c * BANK, (c + 1) * BANK))
                dve.tensor_tensor(a_lo[where], o_sb[c][:].unsqueeze(1), f32(a_hi[where]),
                                  ALU.subtract).then_inc(o_lo, 1)

            def head(hp, par, first=False, last=False):
                for n in range(NBL):
                    if n < 2 and pair_before(hp):
                        invert(hp - 1, par, 2 * n)
                        invert(hp - 1, par, 2 * n + 1)
                        if n == 1:
                            divide(hp - 1, par)
                    if not last:
                        for p in pieces_of(n):
                            piece(*after(hp, par), p)
                    if n == 4 and pair_before(hp):
                        out_lo(hp - 1, par)
                    if last and n >= NBL - 4:
                        invert(hp, 0, n - (NBL - 4))
                        if n == NBL - 1:
                            divide(hp, 0)
                if not last:
                    maxima(*after(hp, par))
                    spread(*after(hp, par))

            for p in range(NPC):
                piece(0, 0, p)
            maxima(0, 0)
            spread(0, 0)

            run(dve, head)
            merge_units.split_lo(dve, 0, 0)
            for quarter in range(4):
                invert(H // 2 - 1, 1, quarter)
            divide(H // 2 - 1, 1)
            out_lo(H // 2 - 1, 0)
            out_lo(H // 2 - 1, 1)

        @block.tensor
        def _(pe):
            pe.sem_inc(merge_units.used, 2)
            pe.sem_inc(st_done, CREDIT)
            pe.sem_inc(pv_done, CREDIT)

            def piece(hp, par, p):
                i, q, a, width = PIECES[p]
                if p == 0:
                    pe.wait_ge(qk_in[par], 64 * hp + 64)
                need(pe, max_done, at(hp, par, p) - 1)
                out, rows = ps[p % 2][:, 0:width], slice(i * P, (i + 1) * P)
                masked = a + width == META + P * (i + 1)
                pe.matmul(out, qa[par][:, rows], ka[par][:, a:a + width], start=True, stop=False)
                last = pe.matmul(out, qb[par][0:CROW + 4, rows], kb_sb[par][0:CROW + 4, a:a + width],
                                 start=False, stop=not masked)
                if masked:
                    last = pe.matmul(ps[p % 2][:, width - P:width], eye[:], mask[:], start=False, stop=True)
                last.then_inc(s_done, 1)

            def scores(hp, par, n):
                c, kb = BLOCKS[n]
                cols, r, a = geometry(c, kb)
                queries = slice(c * BANK + cols.start, (c + 1) * BANK)
                if n == 0:
                    pe.wait_ge(m_done, 2 * hp + (par + 1))
                need(pe, exp_done, at(hp, par, n) - (1 if n < 2 else 2))
                if r < P:
                    pe.sem_inc(pe_passed, 1)
                diagonal = QB * c <= kb < NB
                out = pst[n % 3][0:r, cols]
                pe.matmul(out, ka[par][:, a:a + r], qa[par][:, queries], start=True, stop=False)
                last = pe.matmul(out, kb_sb[par][:, a:a + r], qb[par][:, queries], start=False, stop=not diagonal)
                if diagonal:
                    last = pe.matmul(pst[n % 3][:, cols.start:cols.start + P], eye[:], maskT[:],
                                     start=False, stop=True)
                last.then_inc(st_done, 1)

            def values(hp, par, n):
                c, kb = BLOCKS[n]
                cols, r, _ = geometry(c, kb)
                first = n in (0, HALF0)
                if n == 0:
                    if isinstance(hp, int) and hp == 0:
                        pe.wait_ge(consts, 2)
                    pe.wait_ge(v_in[par], 32 * hp + 32)
                if first:
                    need(pe, o_done, 8 * hp + (4 * par + 2 * c - 2))
                pe.wait_ge(exp_done, at(hp, par, n) + 1)
                if r < P:
                    pe.sem_inc(pe_passed, 1)
                pe.matmul(po[c][:, cols], v_sb[par][0:r, kb, :], pt_sb[(NBL * par + n) % 4][0:r, cols],
                          start=first, stop=(kb == NB)).then_inc(pv_done, 1)

            def turn(hp, par):
                pe.wait_ge(nt_done, 2 * hp + (par + 1))
                pe.sem_inc(pe_passed, 1)
                pe.transpose(pm[0:MROW + MR, 0:P], nt[:], ident[:]).then_inc(m_turned, 1)

            def head(hp, par, first=False, last=False):
                for n in range(NBL):
                    scores(hp, par, n)
                    pieces = () if last else pieces_of(n)
                    if n >= LAG:
                        values(hp, par, n - LAG)
                    for p in pieces:
                        piece(*after(hp, par), p)
                if not last:
                    turn(*after(hp, par))
                for n in range(NBL - LAG, NBL):
                    values(hp, par, n)

            for p in range(NPC):
                piece(0, 0, p)
            turn(0, 0)
            run(pe, head)


def merge(nc, mem, sem, ctx, io, aT, mT, ring, w_o_quarters):
    m_hi, m_lo = mT
    base = 65536 + 2 * 4096
    part = [mem.at(f"mg_part{i}", base + 4096 * i, [P, SEQ]) for i in range(2)]
    sgb = [mem.at(f"mg_sgb{i}", base + 8192 + 4096 * i, [P, SEQ]) for i in range(2)]
    gated = mem.at("mg_gated", base + 16384, [P, SEQ])
    merged = mem.at("mg_merged", base + 20480, [P, SEQ])
    out = [ctx.enter_context(nc.psum_tensor(f"mg_o{i}", [P, SEQ], F32)) for i in range(2)]
    tiles_in = [sem(f"mg_tiles_in{i}") for i in range(2)]
    read, merged_done, hi_done, lo_done = (sem("mg_" + s) for s in ("read", "merged_done", "hi", "lo"))
    halves = [slice(0, BANK), slice(BANK, SEQ)]

    with nc.Block() as block:
        @block.sync
        def _(sp):
            def load_tiles(m, u):
                gate(sp, merged_done, m + 1, ring.passed)
                for dst, src in ((part[u], io["part"]), (sgb[u], io["sgb"])):
                    sp.dma_start(dst[:], src[bass.ds(m, 1)].rearrange("a p t -> p (a t)")).then_inc(tiles_in[u], 16)

            load_tiles(0, 0)
            load_tiles(1, 1)
            with sp.Fori(1, KT // 2) as i:
                for u in range(2):
                    m = 2 * i + u
                    ring.load(sp, io["w_att_out"][0][:, bass.ds(m * P, P)], m, u)
                    load_tiles(m, u)
            raw, raw_in = w_o_quarters
            sp.dma_start(raw[0][:], io["w_merge_out"][0].rearrange("(k p) c -> p k c", p=P)[:, 0:2, :])\
                .then_inc(raw_in[0], 16)

        @block.scalar
        def _(act):
            def merged_hi(m):
                act.wait_ge(merged_done, m + 3)
                act.activation(m_hi[:, bass.ds(m, 1), :], merged[:].unsqueeze(1), ACT.Copy).then_inc(hi_done, 1)

            with act.Fori(0, KT // 2 - 1) as i:
                for u in range(2):
                    ring.split_hi(act, 2 * i + (u + 1), 1 - u, i + u)
                    merged_hi(2 * i + u)
            ring.split_hi(act, KT - 1, 1, KT // 2 - 1)
            merged_hi(KT - 2)
            merged_hi(KT - 1)

        @block.vector
        def _(dve):
            dve.sem_inc(merged_done, 2)

            def merged_lo(m, u, use):
                dve.wait_ge(ring.used, m + 3)
                dve.wait_ge(tiles_in[u], 32 * use + 32)
                dve.tensor_tensor(gated[:], out[u][:], sgb[u][:], ALU.mult).then_inc(read, 1)
                dve.wait_ge(read, m + 1)
                dve.tensor_tensor(merged[:], gated[:], part[u][:], ALU.add).then_inc(merged_done, 1)
                dve.wait_ge(hi_done, m + 1)
                dve.tensor_tensor(m_lo[:, bass.ds(m, 1), :], merged[:].unsqueeze(1),
                                  f32(m_hi[:, bass.ds(m, 1), :]), ALU.subtract).then_inc(lo_done, 1)

            with dve.Fori(0, KT // 2 - 1) as i:
                for u in range(2):
                    ring.split_lo(dve, 2 * i + (u + 1), 1 - u)
                    merged_lo(2 * i + u, u, i)
            ring.split_lo(dve, KT - 1, 1)
            merged_lo(KT - 2, 0, KT // 2 - 1)
            merged_lo(KT - 1, 1, KT // 2 - 1)

        @block.tensor
        def _(pe):
            with pe.Fori(0, KT // 2) as i:
                for u in range(2):
                    m = 2 * i + u
                    pe.wait_ge(merged_done, m + 1)
                    ring.product(pe, m, u, aT, [out[u][:, c] for c in halves], halves)


def residual(nc, mem, sem, ctx, io, mT, x2, logits, retired, first_raw):
    m_hi, m_lo = mT
    NR = NG + NE
    raw, raw_in = first_raw
    w_hi = mem.at("rs_whi", 8192, [P, KT, D], F32R)
    w_lo = mem.at("rs_wlo", 40960, [P, KT, D], F32R)
    base = 106496
    xn = [mem.at(f"rs_xn{i}", base + 4096 * i, [P, D]) for i in range(2)]
    g_b = mem.at("rs_g", 0, [P, D])
    t_hi = mem.at("rs_thi", 4096, [P, KT, P], F32R)
    t_lo = mem.at("rs_tlo", base + 16384, [P, KT, P], F32R)
    sq = mem.at("rs_sq", base + 20480, [P, D])
    base += 24576
    wr = mem.at("rs_wr", base, [P, KT, NR])
    wr_hi = mem.at("rs_wrhi", base + 1152, [P, KT, NR], F32R)
    wr_lo = mem.at("rs_wrlo", base + 2304, [P, KT, NR], F32R)
    br = mem.at("rs_br", base + 3456, [P, NR])
    stat = mem.at("rs_stat", base + 3648, [P, 8])
    ident = io["ident"]
    py = [ctx.enter_context(nc.psum_tensor(f"rs_y{i}", [P, D], F32)) for i in range(2)]
    pT = ctx.enter_context(nc.psum_tensor("rs_T", [P, KT, P], F32))
    pl = ctx.enter_context(nc.psum_tensor("rs_l", [P, BANK], F32))
    names = ("consts_in", "whi", "wlo", "y_done", "x2_done", "squared", "rms", "recip", "xn_done",
             "turned", "t_hi", "t_lo", "logits_mm", "logits_done", "xn_stored", "wr_hi", "wr_lo")
    (consts_in, whi, wlo, y_done, x2_done, squared, rms, recip, xn_done,
     turned, thi_done, tlo_done, logits_mm, logits_done, xn_stored, wrhi_done, wrlo_done) = (
        sem("rs_" + n) for n in names)
    x_in = [sem(f"rs_x_in{i}") for i in range(2)]
    x_blocks = io["x"].rearrange("b (t p) d -> (b t) p d", p=P)
    w_o = io["w_merge_out"][0].rearrange("(k p) c -> p k c", p=P)

    with nc.Block() as block:
        @block.sync
        def _(sp):
            for q in range(1, 4):
                if q >= 2:
                    sp.wait_ge(wlo, 2 * q - 2)
                sp.dma_start(raw[q % 2][:], w_o[:, 2 * q:2 * q + 2, :]).then_inc(raw_in[q % 2], 16)
                if q == 1:
                    sp.dma_start(wr[:, :, 0:NG], io["w_router_group"][0].rearrange("(k p) c -> p k c", p=P)).then_inc(consts_in, 16)
                    sp.dma_start(wr[:, :, NG:NR], io["w_router_expert"][0].rearrange("(k p) c -> p k c", p=P)).then_inc(consts_in, 16)
                    sp.dma_start(br[:, 0:NG], io["b_router_group"].partition_broadcast(P)).then_inc(consts_in, 16)
                    sp.dma_start(br[:, NG:NR], io["b_router_expert"].partition_broadcast(P)).then_inc(consts_in, 16)
                    sp.dma_start(g_b[:], io["norm2_g"].partition_broadcast(P)).then_inc(consts_in, 16)
            for t in range(NB):
                if t >= 2:
                    sp.wait_ge(x2_done, 2 * t - 2)
                sp.dma_start(x2[:, t, :], x_blocks[t]).then_inc(x_in[t % 2], 16)

        @block.gpsimd
        def _(pool):
            for s in retired:
                pool.sem_clear(s)
            for t in range(NB):
                pool.wait_ge(xn_done, t + 1)
                pool.dma_start(io["xn"][t * P:(t + 1) * P, :], xn[t % 2][:]).then_inc(xn_stored, 16)
                pool.wait_ge(xn_stored, 16 * t + 16)

        @block.scalar
        def _(act):
            for k in range(KT):
                q = k // 2
                if k % 2 == 0:
                    act.wait_ge(raw_in[q % 2], 16 * (q // 2) + 16)
                act.activation(w_hi[:, k, :], raw[q % 2][:, k % 2, :], ACT.Copy).then_inc(whi, 1)
            act.wait_ge(consts_in, 80)
            act.activation(wr_hi[:], wr[:], ACT.Copy).then_inc(wrhi_done, 1)

            def front(t):
                act.wait_ge(x2_done, 2 * t + 2)
                act.activation(sq[:], x2[:, t, :], ACT.Square, accum_out=stat[:, 0:1]).then_inc(squared, 1)
                act.wait_ge(squared, t + 1)
                act.activation(stat[:, 2:3], stat[:, 0:1], ACT.Sqrt, scale=1.0 / D,
                               bias=io["eps"][:]).then_inc(rms, 1)

            def back(t):
                act.wait_ge(turned, t + 1)
                if t:
                    act.wait_ge(logits_mm, t)
                act.activation(t_hi[:], pT[:], ACT.Copy).then_inc(thi_done, 1)

            front(0)
            for t in range(1, NB):
                front(t)
                back(t - 1)
            back(NB - 1)

        @block.vector
        def _(dve):
            for k in range(KT):
                dve.wait_ge(whi, k + 1)
                dve.tensor_tensor(w_lo[:, k, :], raw[k // 2 % 2][:, k % 2, :], f32(w_hi[:, k, :]),
                                  ALU.subtract).then_inc(wlo, 1)
            dve.wait_ge(wrhi_done, 1)
            dve.tensor_tensor(wr_lo[:], wr[:], f32(wr_hi[:]), ALU.subtract).then_inc(wrlo_done, 1)

            def front(t):
                dve.wait_ge(y_done, t + 1)
                dve.wait_ge(x_in[t % 2], 16 * (t // 2) + 16)
                for c in range(2):
                    cols = slice(c * BANK, (c + 1) * BANK)
                    dve.tensor_tensor(x2[:, t, cols], py[t % 2][:, cols], x2[:, t, cols],
                                      ALU.add).then_inc(x2_done, 1)
                dve.wait_ge(rms, t + 1)
                dve.reciprocal(stat[:, 4:5], stat[:, 2:3]).then_inc(recip, 1)
                dve.wait_ge(recip, t + 1)
                if t >= 2:
                    dve.wait_ge(turned, t - 1)
                    dve.wait_ge(xn_stored, 16 * (t - 1))
                dve.scalar_tensor_tensor(out=xn[t % 2][:], in0=x2[:, t, :], scalar=stat[:, 4:5], in1=g_b[:],
                                         op0=ALU.mult, op1=ALU.mult).then_inc(xn_done, 1)

            def back(t):
                dve.wait_ge(thi_done, t + 1)
                dve.tensor_tensor(t_lo[:], pT[:], f32(t_hi[:]), ALU.subtract).then_inc(tlo_done, 1)
                dve.wait_ge(logits_mm, t + 1)
                dve.tensor_tensor(logits[:, t, :], pl[:, 0:NR], br[:], ALU.add).then_inc(logits_done, 1)

            front(0)
            for t in range(1, NB):
                front(t)
                back(t - 1)
            back(NB - 1)

        @block.tensor
        def _(pe):
            def product(t):
                for k in range(KT):
                    if t == 0:
                        pe.wait_ge(wlo, k + 1)
                    elif k == 0 and t >= 2:
                        pe.wait_ge(x2_done, 2 * t - 2)
                    for c in range(2):
                        cols = slice(c * BANK, (c + 1) * BANK)
                        rows = slice(t * P, (t + 1) * P)
                        last = split3(pe, py[t % 2][:, cols], m_hi[:, k, rows], m_lo[:, k, rows],
                                      w_hi[:, k, cols], w_lo[:, k, cols], k == 0, k == KT - 1)
                last.then_inc(y_done, 1)

            def route(t):
                pe.wait_ge(xn_done, t + 1)
                if t:
                    pe.wait_ge(tlo_done, t)
                for k in range(KT):
                    last = pe.transpose(pT[:, k, :], xn[t % 2][:, k * P:(k + 1) * P], ident[:])
                last.then_inc(turned, 1)

            def score(t):
                pe.wait_ge(tlo_done, t + 1)
                if t:
                    pe.wait_ge(logits_done, t)
                else:
                    pe.wait_ge(wrlo_done, 1)
                for k in range(KT):
                    last = split3(pe, pl[:, 0:NR], t_hi[:, k, :], t_lo[:, k, :], wr_hi[:, k, :], wr_lo[:, k, :],
                                  k == 0, k == KT - 1)
                last.then_inc(logits_mm, 1)

            product(0)
            for t in range(1, NB):
                product(t)
                if t >= 2:
                    score(t - 2)
                route(t - 1)
            score(NB - 2)
            route(NB - 1)
            score(NB - 1)


def scatter_tokens(pool, io, dest, ids, blocks, scattered):
    for t in blocks:
        for c in range(2):
            pool.indirect_dma_start(io["tokens"], bass.IndirectOffsetOnAxis(ap=dest[:, c, t:t + 1], axis=0),
                                    ids[:, t:t + 1], None).then_inc(scattered, 16)


def route(nc, mem, sem, ctx, io, logits, dest, weights, table, ids, scattered):
    W = 2 ** 100
    offset = [0]

    def tile(name, *shape, dtype=F32):
        t = mem.at("rt_" + name, offset[0], [P, *shape], dtype)
        n = 4
        for d in shape:
            n *= d
        offset[0] += (n + 31) // 32 * 32
        return t

    jrev4, jrev32, j32 = tile("jrev4", NB, NG), tile("jrev32", NB, NE), tile("j32", NE)
    step128 = tile("step128", NB, NE)
    before, pidx, pidx128 = tile("before", P), tile("pidx", 1), tile("pidx128", 1)
    iot = tile("iot", NB, NE, dtype=I32)
    iot4, iotj, iot8, iotp = (tile("iot4", NB, NG, dtype=I32), tile("iotj", NE, dtype=I32),
                              tile("iot8", NB, NE, dtype=I32), tile("iotp", 1, dtype=I32))
    gmax, gsum, gsel = tile("gmax", NB), tile("gsum", NB), tile("gsel", NB)
    d4, e4, oh4, c4 = (tile(n, NB, NG) for n in ("d4", "e4", "oh4", "c4"))
    lem, lem2, d32, c32, oh1, oh2, both = (tile(n, NB, NE) for n in ("lem", "lem2", "d32", "c32", "oh1", "oh2", "both"))
    m1, m2, dm, em, sel, w1 = (tile(n, NB) for n in ("m1", "m2", "dm", "em", "sel", "w1"))
    tot, pos, hit = tile("tot", NB, NE), tile("pos", NB, NE), tile("hit", NB, NE)
    pre = tile("pre", NB + 1, NE)
    inc, start, nblk, bend, bst, lo, ind, rowv = (tile(n, NE) for n in ("inc", "start", "nblk", "bend", "bst", "lo", "ind", "rowv"))
    destf, tabf, tabi = tile("destf", 2, NB), tile("tabf", 4), tile("tabi", 4, dtype=I32)
    zero = tile("zero", 1, dtype=I32)
    ones = io["onesp"]
    p_rank = ctx.enter_context(nc.psum_tensor("rt_rank", [P, BANK], F32))
    p_tot = ctx.enter_context(nc.psum_tensor("rt_tot", [P, BANK], F32))
    names = ("chain", "consts", "iotas", "d4_done", "e4_done", "dm_done", "em_done", "both_done", "ranked", "dest_done", "tab_done",
             "tab_stored", "tab_in", "zeroed")
    (chain, consts, iotas, d4_done, e4_done, dm_done, em_done, both_done, ranked, dest_done, tab_done,
     tab_stored, tab_in, zeroed) = (sem("rt_" + n) for n in names)
    lg, le = logits[:, :, 0:NG], logits[:, :, NG:NG + NE]

    def wide(ap, n):
        return ap.unsqueeze(2).to_broadcast([P, ap.shape[1], n])

    with nc.Block() as block:
        @block.sync
        def _(sp):
            sp.wait_ge(iotas, 7)
            sp.dma_start(io["tokens"][SLOTS:XROWS, :], zero[:]).then_inc(zeroed, 16)
            sp.wait_ge(tab_done, 1)
            sp.dma_start(io["tab"], tabi[:]).then_inc(tab_stored, 16)
            sp.wait_ge(tab_stored, 16)
            sp.dma_start(table[:], io["tab"][0:MAXBLK + 1, :].rearrange("(o p) c -> o (p c)", o=1)).then_inc(tab_in, 16)
            sp.wait_ge(tab_in, 16)
            sp.wait_ge(zeroed, 16)

        @block.gpsimd
        def _(pool):
            pool.iota(iot[:], pattern=[[0, NB], [-1, NE]], base=NE, channel_multiplier=0).then_inc(iotas, 1)
            pool.iota(iot4[:], pattern=[[0, NB], [-1, NG]], base=NG, channel_multiplier=0).then_inc(iotas, 1)
            pool.iota(iotj[:], pattern=[[1, NE]], base=0, channel_multiplier=0).then_inc(iotas, 1)
            pool.iota(iot8[:], pattern=[[P, NB], [0, NE]], base=0, channel_multiplier=0).then_inc(iotas, 1)
            pool.iota(iotp[:], pattern=[[0, 1]], base=0, channel_multiplier=1).then_inc(iotas, 1)
            pool.memset(zero[:], 0).then_inc(iotas, 1)
            pool.iota(ids[:], pattern=[[P, NB]], base=0, channel_multiplier=1)
            pool.memset(before[:], 1.0).then_inc(consts, 1)
            pool.wait_ge(consts, 1)
            pool.affine_select(out=before[:], in_=before[:], compare_op=ALU.is_gt, fill=0.0, base=0,
                               pattern=[[1, P]], channel_multiplier=-1).then_inc(iotas, 1)
            pool.wait_ge(dest_done, 1)
            scatter_tokens(pool, io, dest, ids, range(NB // 2), scattered)

        @block.scalar
        def _(act):
            act.wait_ge(d4_done, 1)
            act.activation(e4[:], d4[:], ACT.Exp).then_inc(e4_done, 1)
            act.wait_ge(dm_done, 1)
            act.activation(em[:], dm[:], ACT.Exp).then_inc(em_done, 1)

        @block.vector
        def _(dve):
            count = [0]

            def link(ins):
                count[0] += 1
                ins.then_inc(chain, 1)
                dve.wait_ge(chain, count[0])

            dve.wait_ge(iotas, 7)
            for dst, src in ((jrev32, iot), (jrev4, iot4), (j32, iotj), (step128, iot8), (pidx, iotp)):
                link(dve.tensor_copy(dst[:], src[:]))
            link(dve.tensor_scalar(pidx128[:], pidx[:], float(P), None, ALU.mult))
            link(dve.tensor_reduce(gmax[:], lg, AX.X, ALU.max))
            dve.tensor_tensor(d4[:], lg, wide(gmax[:], NG), ALU.subtract).then_inc(d4_done, 1)
            dve.wait_ge(d4_done, 1)
            link(dve.scalar_tensor_tensor(out=c4[:], in0=d4[:], scalar=0.0, in1=jrev4[:], op0=ALU.is_ge, op1=ALU.mult))
            link(dve.tensor_reduce(gsel[:], c4[:], AX.X, ALU.max))
            link(dve.tensor_tensor(oh4[:], jrev4[:], wide(gsel[:], NG), ALU.is_equal))
            link(dve.tensor_scalar(oh4[:], oh4[:], -1.0, float(W), ALU.add, ALU.mult))
            link(dve.tensor_copy(lem[:], le))
            link(dve.tensor_tensor(lem[:].rearrange("p b (g e) -> p (b g) e", g=NG),
                                   lem[:].rearrange("p b (g e) -> p (b g) e", g=NG),
                                   wide(oh4[:].rearrange("p b g -> p (b g)"), EPG), ALU.add))

            def pick(logit, top, onehot):
                link(dve.tensor_reduce(top[:], logit[:], AX.X, ALU.max))
                link(dve.tensor_tensor(d32[:], logit[:], wide(top[:], NE), ALU.subtract))
                link(dve.scalar_tensor_tensor(out=c32[:], in0=d32[:], scalar=0.0, in1=jrev32[:],
                                              op0=ALU.is_ge, op1=ALU.mult))
                link(dve.tensor_reduce(sel[:], c32[:], AX.X, ALU.max))
                link(dve.tensor_tensor(onehot[:], jrev32[:], wide(sel[:], NE), ALU.is_equal))

            pick(lem, m1, oh1)
            link(dve.scalar_tensor_tensor(out=lem2[:], in0=oh1[:], scalar=-2.0 * W, in1=lem[:],
                                          op0=ALU.mult, op1=ALU.add))
            pick(lem2, m2, oh2)
            dve.tensor_tensor(dm[:], m2[:], m1[:], ALU.subtract).then_inc(dm_done, 1)
            dve.tensor_tensor(both[:], oh1[:], oh2[:], ALU.add).then_inc(both_done, 1)
            dve.wait_ge(e4_done, 1)
            link(dve.tensor_reduce(gsum[:], e4[:], AX.X, ALU.add))
            dve.wait_ge(em_done, 1)
            link(dve.scalar_tensor_tensor(out=w1[:], in0=em[:], scalar=1.0, in1=gsum[:], op0=ALU.add, op1=ALU.mult))
            link(dve.reciprocal(weights[:, 0, :], w1[:]))
            link(dve.tensor_tensor(weights[:, 1, :], weights[:, 0, :], em[:], ALU.mult))
            dve.wait_ge(ranked, 1)
            link(dve.tensor_copy(tot[:], p_tot[:, 0:NB * NE].rearrange("p (b e) -> p b e", b=NB)))
            link(dve.memset(pre[:, 0, :], 0.0))
            for b in range(NB):
                link(dve.tensor_tensor(pre[:, b + 1, :], pre[:, b, :], tot[:, b, :], ALU.add))
            total = pre[:, NB, :]
            link(dve.tensor_tensor_scan(inc[:], ones[:, 0:NE], total, 0.0, ALU.mult, ALU.add))
            link(dve.tensor_tensor(start[:], inc[:], total, ALU.subtract))
            link(dve.tensor_tensor(pos[:], p_rank[:, 0:NB * NE].rearrange("p (b e) -> p b e", b=NB),
                                   pre[:, 0:NB, :], ALU.add))
            link(dve.tensor_tensor(pos[:], pos[:], start[:].unsqueeze(1).to_broadcast([P, NB, NE]), ALU.add))
            for c, oh in enumerate((oh1, oh2)):
                link(dve.tensor_tensor(hit[:], oh[:], pos[:], ALU.mult))
                link(dve.tensor_reduce(destf[:, c, :], hit[:], AX.X, ALU.add))
            dve.tensor_copy(dest[:], destf[:]).then_inc(dest_done, 1)
            link(dve.tensor_tensor(hit[:], total.unsqueeze(1).to_broadcast([P, NB, NE]), step128[:], ALU.is_gt))
            link(dve.tensor_reduce(nblk[:], hit[:].rearrange("p b e -> p e b"), AX.X, ALU.add))
            link(dve.tensor_tensor_scan(bend[:], ones[:, 0:NE], nblk[:], 0.0, ALU.mult, ALU.add))
            link(dve.tensor_tensor(bst[:], bend[:], nblk[:], ALU.subtract))
            link(dve.tensor_scalar(lo[:], bst[:], pidx[:], None, ALU.is_le))
            link(dve.scalar_tensor_tensor(out=ind[:], in0=bend[:], scalar=pidx[:], in1=lo[:],
                                          op0=ALU.is_gt, op1=ALU.mult))
            link(dve.scalar_tensor_tensor(out=rowv[:], in0=bst[:], scalar=-float(P), in1=start[:],
                                          op0=ALU.mult, op1=ALU.add))
            link(dve.scalar_tensor_tensor(out=rowv[:], in0=rowv[:], scalar=pidx128[:], in1=ind[:],
                                          op0=ALU.add, op1=ALU.mult))
            link(dve.tensor_reduce(tabf[:, 1:2], rowv[:], AX.X, ALU.add))
            link(dve.tensor_tensor(lo[:], ind[:], j32[:], ALU.mult))
            link(dve.tensor_reduce(tabf[:, 0:1], lo[:], AX.X, ALU.add))
            link(dve.tensor_scalar(tabf[:, 2:3], bend[:, NE - 1:NE], -2.0, None, ALU.add))
            link(dve.tensor_tensor(lo[:], ind[:], inc[:], ALU.mult))
            link(dve.tensor_reduce(tabf[:, 3:4], lo[:], AX.X, ALU.add))
            link(dve.tensor_tensor(tabf[:, 3:4], tabf[:, 3:4], tabf[:, 1:2], ALU.subtract))
            link(dve.tensor_scalar(tabf[:, 3:4], tabf[:, 3:4], float(P), None, ALU.min))
            dve.tensor_copy(tabi[:], tabf[:]).then_inc(tab_done, 1)

        @block.tensor
        def _(pe):
            pe.wait_ge(both_done, 1)
            rhs = both[:].rearrange("p b e -> p (b e)")
            pe.matmul(p_rank[:, 0:NB * NE], before[:], rhs, start=True, stop=True)
            pe.matmul(p_tot[:, 0:NB * NE], ones[:, 0:P], rhs, start=True, stop=True).then_inc(ranked, 1)


def experts(nc, mem, sem, ctx, io, dest, table, ids, scattered):
    HALF = KT // 2 * DE
    raw = [mem.at(f"ex_raw{i}", 4 * HALF * i, [P, HALF]) for i in range(6)]
    unit_at = [49152, *(106496 + 16384 * i for i in range(5))]
    w_hi = [mem.at(f"ex_whi{i}", unit_at[i], [P, 2 * HALF], F32R) for i in range(3)]
    w_lo = [mem.at(f"ex_wlo{i}", unit_at[3 + i], [P, 2 * HALF], F32R) for i in range(3)]
    slot_token = mem.at("ex_slot_token", 204800, [P, 1], I32)
    x_hi = mem.at("ex_xhi", 65536, [P, KT, P], F32R)
    x_lo = mem.at("ex_xlo", 69632, [P, KT, P], F32R)
    base = 106496 + 16384 * 5
    x_sb = mem.at("ex_x", base, [P, D])
    y_sb = mem.at("ex_y", base + 4096, [P, D])
    h_hi = mem.at("ex_hhi", base + 8192, [P, KE, P], F32R)
    h_lo = mem.at("ex_hlo", base + 10240, [P, KE, P], F32R)
    act_g = mem.at("ex_silu", base + 12288, [P, DE])
    h_sb = mem.at("ex_h", base + 14336, [P, DE])
    ident = io["ident"]
    p_gate, p_up = (ctx.enter_context(nc.psum_tensor("ex_p" + n, [P, DE], F32)) for n in ("gate", "up"))
    p_y = ctx.enter_context(nc.psum_tensor("ex_py", [P, D], F32))
    p_xT = ctx.enter_context(nc.psum_tensor("ex_pxT", [P, KT, P], F32))
    p_hT = ctx.enter_context(nc.psum_tensor("ex_phT", [P, KE, P], F32))
    raw_in = [sem(f"ex_raw_in{i}") for i in range(6)]
    names = ("x_in", "whi", "wlo", "gate_done", "up_done", "down_done", "x_turned", "x_hi", "x_lo", "silu_done",
             "h_done", "h_turned", "h_hi", "h_lo", "y0_done", "y1_done", "stored", "y_free", "passed", "pool_passed",
             "token_in", "x_clear")
    (x_in, whi, wlo, gate_done, up_done, down_done, x_turned, xhi_done, xlo_done, silu_done,
     h_done, h_turned, hhi_done, hlo_done, y0_done, y1_done, stored, y_free, passed, pool_passed,
     token_in, x_clear) = (
        sem("ex_" + n) for n in names)
    GATE, UP, DOWN = 0, 1, 2
    products = ((GATE, gate_done), (UP, up_done), (DOWN, down_done))

    def order(unit, b, last=False):
        if unit != DOWN and isinstance(b, int) and b == 0:
            return 2 * unit
        return 6 * b + (4 if last else (-2, 0, 8)[unit])

    def entry(eng, b, column, most):
        at = slice(4 * b + column, 4 * b + column + 1) if isinstance(b, int) else bass.ds(4 * b + column, 1)
        return eng.value_load(table[0:1, at], min_val=0, max_val=most)

    def move_rows(eng, b, dma):
        n = entry(eng, b, 3, P)
        with eng.If(n < 65):
            dma(64)
        with eng.Else():
            with eng.If(n < 81):
                dma(80)
            with eng.Else():
                with eng.If(n < 97):
                    dma(96)
                with eng.Else():
                    dma(P)

    def blocks(eng):
        return eng.value_load(table[0:1, 2:3], min_val=SLOTS // P - 2, max_val=MAXBLK - 2) + 2

    with nc.Block() as block:
        @block.sync
        def _(sp):
            earlier = [(4, -2), (5, -2), (0, 0), (1, 0), (2, 1), (3, 1)]

            def load(unit, b, e, throttle=False):
                for s in range(2):
                    if throttle:
                        buffer, distance = earlier[2 * unit + s]
                        gate(sp, raw_in[buffer], 16 * b + (16 * distance + 16), passed)
                    if not (isinstance(b, int) and b == 0):
                        before = order(unit, 0) if isinstance(b, int) and b == 1 else order(unit, b - 1)
                        gate(sp, wlo, before + s + 1, passed)
                    w = io[("w_exp_gate", "w_exp_up", "w_exp_down")[unit]][0][bass.ds(e, 1)]
                    w = w.rearrange("o (s k p) c -> s p (o k) c", s=2, p=P)[s]
                    dst = raw[2 * unit + s][:].rearrange("p (k c) -> p k c", c=D if unit == DOWN else DE)
                    sp.dma_start(dst, w).then_inc(raw_in[2 * unit + s], 16)

            n = blocks(sp)
            e = entry(sp, 0, 0, NE - 1)
            load(GATE, 0, e)
            load(UP, 0, e)
            sp.wait_ge(x_in, 16)
            load(DOWN, 0, e)
            e = entry(sp, 1, 0, NE - 1)
            load(GATE, 1, e)
            load(UP, 1, e)
            with sp.Fori(2, n) as b:
                e = entry(sp, b, 0, NE - 1)
                load(GATE, b, e, throttle=True)
                load(UP, b, e, throttle=True)
                load(DOWN, b - 1, entry(sp, b - 1, 0, NE - 1), throttle=True)
            load(DOWN, n - 1, entry(sp, n - 1, 0, NE - 1))

        @block.gpsimd
        def _(pool):
            scatter_tokens(pool, io, dest, ids, range(NB // 2, NB), scattered)
            pool.sem_inc(y_free, 1)
            pool.wait_ge(scattered, 16 * 2 * NB)
            pool.wait_ge(x_clear, 1)

            def load_x(b):
                first = entry(pool, b, 1, SLOTS)
                if not (isinstance(b, int) and b == 0):
                    gate(pool, x_turned, b, pool_passed)
                pool.dma_start(slot_token[:], io["tokens"][bass.ds(first, P), :]).then_inc(token_in, 16)
                pool.wait_ge(token_in, 16 * b + 16)
                move_rows(pool, b, lambda n: pool.indirect_dma_start(
                    x_sb[0:n, :], None, io["xn"],
                    bass.IndirectOffsetOnAxis(ap=slot_token[0:n, :], axis=0)).then_inc(x_in, 16))

            def store_y(b):
                row = entry(pool, b, 1, SLOTS)
                gate(pool, y0_done, b + 1, pool_passed)
                gate(pool, y1_done, b + 1, pool_passed)
                move_rows(pool, b, lambda n: pool.dma_start(io["ys"][bass.ds(row, n), :], y_sb[0:n, :])
                          .then_inc(stored, 16))
                pool.wait_ge(stored, 16 * b + 16)
                pool.sem_inc(y_free, 1)

            n = blocks(pool)
            for b in range(3):
                load_x(b)
            with pool.Fori(2, n) as b:
                load_x(b + 1)
                store_y(b - 2)
            store_y(n - 2)
            store_y(n - 1)

        @block.scalar
        def _(act):
            def split(unit, b, first=False):
                done = products[unit][1]
                for s in range(2):
                    act.wait_ge(raw_in[2 * unit + s], 16 * b + 16)
                    if s == 0 and not first:
                        act.wait_ge(done, b)
                    act.activation(w_hi[unit][:, s * HALF:(s + 1) * HALF], raw[2 * unit + s][:],
                                   ACT.Copy).then_inc(whi, 1)

            def x_split(b):
                act.wait_ge(x_turned, b + 1)
                act.activation(x_hi[:], p_xT[:], ACT.Copy).then_inc(xhi_done, 1)

            def y_out(b):
                act.wait_ge(down_done, b + 1)
                act.wait_ge(y_free, b + 1)
                act.activation(y_sb[:, 0:BANK], p_y[:, 0:BANK], ACT.Copy).then_inc(y0_done, 1)

            def silu(b, first=False):
                act.wait_ge(gate_done, b + 1)
                if not first:
                    act.wait_ge(h_done, b)
                act.activation(act_g[:], p_gate[:], ACT.Silu).then_inc(silu_done, 1)

            n = blocks(act)
            split(GATE, 0, first=True)
            split(UP, 0, first=True)
            x_split(0)
            silu(0, first=True)
            x_split(1)

            def step(b, first=False):
                split(GATE, b)
                if not first:
                    y_out(b - 2)
                split(UP, b)
                act.wait_ge(h_turned, b)
                act.activation(h_hi[:], p_hT[:], ACT.Copy).then_inc(hhi_done, 1)
                silu(b)
                split(DOWN, b - 1, first)
                x_split(b + 1)

            step(1, first=True)
            with act.Fori(2, n) as b:
                step(b)
            y_out(n - 2)
            act.wait_ge(h_turned, n)
            act.activation(h_hi[:], p_hT[:], ACT.Copy).then_inc(hhi_done, 1)
            split(DOWN, n - 1)
            y_out(n - 1)

        @block.vector
        def _(dve):
            def split(unit, b, last=False):
                for s in range(2):
                    dve.wait_ge(whi, order(unit, b, last) + (s + 1))
                    cols = slice(s * HALF, (s + 1) * HALF)
                    dve.tensor_tensor(w_lo[unit][:, cols], raw[2 * unit + s][:], f32(w_hi[unit][:, cols]),
                                      ALU.subtract).then_inc(wlo, 1)

            def x_split(b):
                dve.wait_ge(xhi_done, b + 1)
                dve.tensor_tensor(x_lo[:], p_xT[:], f32(x_hi[:]), ALU.subtract).then_inc(xlo_done, 1)

            def h_split(b):
                dve.wait_ge(hhi_done, b + 1)
                dve.tensor_tensor(h_lo[:], p_hT[:], f32(h_hi[:]), ALU.subtract).then_inc(hlo_done, 1)

            def hidden(b, first=False):
                dve.wait_ge(silu_done, b + 1)
                dve.wait_ge(up_done, b + 1)
                if not first:
                    dve.wait_ge(h_turned, b)
                dve.tensor_tensor(h_sb[:], p_up[:], act_g[:], ALU.mult).then_inc(h_done, 1)

            def y_out(b):
                dve.wait_ge(down_done, b + 1)
                dve.wait_ge(y_free, b + 1)
                dve.tensor_copy(y_sb[:, BANK:D], p_y[:, BANK:D]).then_inc(y1_done, 1)

            n = blocks(dve)
            dve.memset(x_sb[:], 0.0).then_inc(x_clear, 1)
            split(GATE, 0)
            split(UP, 0)
            x_split(0)
            x_split(1)

            def step(b, first=False):
                hidden(b - 1, first)
                split(GATE, b)
                if not first:
                    y_out(b - 2)
                split(UP, b)
                h_split(b - 1)
                split(DOWN, b - 1)
                x_split(b + 1)

            step(1, first=True)
            with dve.Fori(2, n) as b:
                step(b)
            hidden(n - 1)
            y_out(n - 2)
            h_split(n - 1)
            split(DOWN, n - 1, last=True)
            y_out(n - 1)

        @block.tensor
        def _(pe):
            def product(unit, b, x, outs, final=False):
                kt = KE if unit == DOWN else KT
                for k in range(kt):
                    if k % (kt // 2) == 0:
                        pe.wait_ge(wlo, order(unit, b, final) + (2 * k // kt + 1))
                    for i, out in enumerate(outs):
                        cols = slice((k * len(outs) + i) * BANK, (k * len(outs) + i + 1) * BANK)
                        last = split3(pe, out, x[0][:, k, :], x[1][:, k, :], w_hi[unit][:, cols], w_lo[unit][:, cols],
                                      k == 0, k == kt - 1)
                last.then_inc(products[unit][1], 1)

            def turn_x(b):
                pe.wait_ge(x_in, 16 * b + 16)
                if not (isinstance(b, int) and b == 0):
                    pe.wait_ge(xlo_done, b)
                for k in range(KT):
                    last = pe.transpose(p_xT[:, k, :], x_sb[:, k * P:(k + 1) * P], ident[:])
                last.then_inc(x_turned, 1)

            def turn_h(b):
                pe.wait_ge(h_done, b + 1)
                for k in range(KE):
                    last = pe.transpose(p_hT[:, k, :], h_sb[:, k * P:(k + 1) * P], ident[:])
                last.then_inc(h_turned, 1)

            def gate_product(b):
                pe.wait_ge(xlo_done, b + 1)
                if not (isinstance(b, int) and b == 0):
                    pe.wait_ge(silu_done, b)
                product(GATE, b, (x_hi, x_lo), [p_gate[:]])

            def down_product(b, first=False, final=False):
                pe.wait_ge(hlo_done, b + 1)
                if not first:
                    pe.wait_ge(y0_done, b)
                    pe.wait_ge(y1_done, b)
                product(DOWN, b, (h_hi, h_lo), [p_y[:, 0:BANK], p_y[:, BANK:D]], final)

            n = blocks(pe)
            turn_x(0)
            gate_product(0)
            product(UP, 0, (x_hi, x_lo), [p_up[:]])
            turn_x(1)

            def step(b, first=False):
                gate_product(b)
                turn_h(b - 1)
                product(UP, b, (x_hi, x_lo), [p_up[:]])
                turn_x(b + 1)
                down_product(b - 1, first)

            step(1, first=True)
            with pe.Fori(2, n) as b:
                step(b)
            turn_h(n - 1)
            down_product(n - 1, final=True)


def combine(nc, mem, sem, ctx, io, dest, weights, x2):
    y = [mem.at(f"cb_y{c}", 32768 * c, [P, NB, D]) for c in range(2)]
    half_done, done, out_stored = (sem("cb_" + n) for n in ("half", "done", "out_stored"))
    y_in = [sem(f"cb_y_in{b}") for b in range(NB)]

    with nc.Block() as block:
        @block.sync
        def _(sp):
            for b in range(NB):
                sp.wait_ge(done, b + 1)
                sp.dma_start(io["out"][0][b * P:(b + 1) * P, :], x2[:, b, :]).then_inc(out_stored, 16)
            sp.wait_ge(out_stored, 16 * NB)

        @block.gpsimd
        def _(pool):
            for b in range(NB):
                for c in range(2):
                    pool.indirect_dma_start(y[c][:, b, :], None, io["ys"][0:SLOTS, :],
                                            bass.IndirectOffsetOnAxis(ap=dest[:, c, b:b + 1], axis=0)).then_inc(y_in[b], 16)

        @block.vector
        def _(dve):
            for b in range(NB):
                dve.wait_ge(y_in[b], 32)
                dve.scalar_tensor_tensor(out=x2[:, b, :], in0=y[0][:, b, :], scalar=weights[:, 0, b:b + 1],
                                         in1=x2[:, b, :], op0=ALU.mult, op1=ALU.add).then_inc(half_done, 1)
                dve.wait_ge(half_done, b + 1)
                dve.scalar_tensor_tensor(out=x2[:, b, :], in0=y[1][:, b, :], scalar=weights[:, 1, b:b + 1],
                                         in1=x2[:, b, :], op0=ALU.mult, op1=ALU.add).then_inc(done, 1)


def program(nc, io, upto=99):
    mem = Memory(nc)
    for name, rows, cols in (("qa", P, SEQ), ("qb", HD + 4, SEQ), ("ka", HD, L), ("kb", HD + 4, L)):
        io[name] = nc.dram_tensor(name + "_scratch", [H, rows, cols], F32R).ap()
    scratch = dict(v=[L, D], part=[KT, P, SEQ], sgb=[KT, P, SEQ],
                   xn=[SEQ, D], ys=[XROWS, D])
    io["tokens"] = nc.dram_tensor("tokens_scratch", [XROWS, 1], I32).ap()
    io["tab"] = nc.dram_tensor("tab_scratch", [P, 4], I32).ap()
    for name, shape in scratch.items():
        io[name] = nc.dram_tensor(name + "_scratch", shape, F32).ap()
    with ExitStack() as ctx:
        retired = ExitStack()
        first = []

        def sem(name):
            return ctx.enter_context(nc.semaphore(name))

        def early_sem(name):
            if name.endswith("stored"):
                return sem(name)
            first.append(retired.enter_context(nc.semaphore(name)))
            return first[-1]

        io["ident"] = mem.at("ident", mem.size - 512, [P, P])
        io["eps"] = mem.at("eps", mem.size - 576, [P, 1])
        io["one"] = mem.at("one", mem.size - 544, [P, 1])
        io["onesp"] = mem.at("onesp", mem.size - 576 - 4160, [P, L])
        for i, name in enumerate(("eye", "mask", "maskT")):
            io[name] = mem.at(name, 206336 + 256 * i, [P, P], BF16)
        io["sel"] = mem.at("sel", 206336 + 768, [P, NB])
        h_hi = mem.at("h_hi", 0, [P, KT, L], F32R)
        h_lo = mem.at("h_lo", 33280, [P, KT, L], F32R)
        units = (WeightUnits(mem, early_sem, "cm", 132096, 3),
                 WeightUnits(mem, early_sem, "cf", 132096 + 3 * 12288, 1))
        with ExitStack() as c:
            norm1(nc, mem, early_sem, c, io, (h_hi, h_lo), units)
        if upto < 1:
            return
        c_hi = mem.at("c_hi", 66560, [P, KT, SEQ], F32R)
        c_lo = mem.at("c_lo", 99328, [P, KT, SEQ], F32R)
        w_in_halves = ([mem.at(f"qk_raw{i}", at, [P, KT // 2, BANK]) for i, at in enumerate((185472, 198016))],
                       [sem(f"qk_raw_in{i}") for i in range(2)])
        with ExitStack() as c:
            conv_merge(nc, mem, early_sem, c, io, (h_hi, h_lo), (c_hi, c_lo), units, w_in_halves)
        if upto < 2:
            return
        heads = HeadTiles(mem, sem)
        with ExitStack() as c:
            qkv(nc, mem, sem, c, io, (h_hi, h_lo), heads, w_in_halves)
        if upto < 3:
            return
        a_hi = mem.at("a_hi", 0, [P, KT, SEQ], F32R)
        a_lo = mem.at("a_lo", 32768, [P, KT, SEQ], F32R)
        merge_units = WeightUnits(mem, sem, "mg", 0, 2, places=[98304, 102400, 106496, 65536, 110592, 69632])
        with ExitStack() as c:
            attention(nc, mem, sem, c, io, (a_hi, a_lo), heads, merge_units)
        if upto < 4:
            return
        m_hi = mem.at("m_hi", 142336, [P, KT, SEQ], F32R)
        m_lo = mem.at("m_lo", 175104, [P, KT, SEQ], F32R)
        w_o_quarters = ([mem.at(f"rs_raw{i}", at, [P, KT // 4, D]) for i, at in enumerate((114688, 106496))],
                        [sem(f"rs_raw_in{i}") for i in range(2)])
        with ExitStack() as c:
            merge(nc, mem, sem, c, io, (a_hi, a_lo), (m_hi, m_lo), merge_units, w_o_quarters)
        if upto < 5:
            return
        x2 = mem.at("x2", 73728, [P, NB, D])
        logits = mem.at("logits", 140800, [P, NB, NG + NE])
        with ExitStack() as c:
            residual(nc, mem, sem, c, io, (m_hi, m_lo), x2, logits, first, w_o_quarters)
        retired.close()
        if upto < 6:
            return
        dest = mem.at("dest", 207872, [P, 2, NB], I32)
        weights = mem.at("weights", 207936, [P, 2, NB])
        table = mem.at("table", 205824, [1, 4 * (MAXBLK + 1)], I32)
        scattered = sem("slot_tokens_scattered")
        ids = mem.at("ids", 207872 - 4 * NB, [P, NB], I32)
        with ExitStack() as c:
            route(nc, mem, sem, c, io, logits, dest, weights, table, ids, scattered)
        if upto < 7:
            return
        with ExitStack() as c:
            experts(nc, mem, sem, c, io, dest, table, ids, scattered)
        if upto < 8:
            return
        with ExitStack() as c:
            combine(nc, mem, sem, c, io, dest, weights, x2)


_INS = ['x', 'meta_tokens', 'norm1_g', 'w_in', 'b_forget', 'conv_w', 'w_conv_out', 'q_norm_g', 'k_norm_g',
        'w_att_out', 'w_merge_out', 'norm2_g', 'w_router_group', 'b_router_group', 'w_router_expert',
        'b_router_expert', 'w_exp_gate', 'w_exp_up', 'w_exp_down']


def kernel(**inputs):
    import numpy as _np
    import concourse.bacc as _bacc
    from concourse import mybir as _mybir
    from concourse.bass_utils import run_bass_kernel_spmd as _run

    nc = _bacc.Bacc("TRN2", target_bir_lowering=False, num_devices=1)
    arrays, io = {}, {}
    for name in _INS:
        a = _np.ascontiguousarray(inputs[name])
        arrays[f"in_{name}_dram"] = a
        io[name] = nc.dram_tensor(f"in_{name}_dram", a.shape, _mybir.dt.from_np(a.dtype), kind="ExternalInput").ap()
    io["out"] = nc.dram_tensor("out_0_dram", (1, 1024, 1024), F32, kind="ExternalOutput").ap()
    program(nc, io)
    r = _run(nc, [arrays], core_ids=[0])
    return r.results[0]["out_0_dram"]
```
